# Optimizing a Trainium2 kernel written in Bass

```python
import jax, jax.numpy as jnp
from jax import lax
import numpy as np
import math

D_MODEL = 1024
BATCH = 1
SEQ = 256
DEPTH = 2

D_MIX = D_MODEL
HEAD_DIM = 64
A_HEADS = 6
A_DIM = A_HEADS * HEAD_DIM
IDX_HEADS = 4
IDX_DIM = 64
TOPK_MAX = 256
Q_BLOCK = 128
B_HEADS = 6
B_DK = 64
B_DV = 64
B_DIM = B_HEADS * B_DV
HGRN_CHUNK = 64
C_GROUPS = 4
C_DIM = D_MIX - A_DIM - B_DIM
C_GROUP_DIM = C_DIM // C_GROUPS
C_CHUNK = 128
ROPE_THETA = 10000.0
F_DENSE = 2816
N_EXPERTS = 8
TOP_K = 2
F_EXPERT = 3584
N_DENSE = (DEPTH + 1) // 2
N_MOE = DEPTH // 2
EPS = 1e-6
IN_WIDTHS = (A_DIM, HEAD_DIM, HEAD_DIM, IDX_HEADS * IDX_DIM, IDX_DIM, IDX_HEADS, B_HEADS * B_DK, B_HEADS * B_DK, B_HEADS * B_DV, B_HEADS * B_DV, 2 * C_DIM)
IN_DIM = sum(IN_WIDTHS)


def rms_norm(x, g):
    xf = x.astype(jnp.float32)
    y = xf * lax.rsqrt(jnp.mean(xf * xf, axis=-1, keepdims=True) + EPS)
    return (y * g.astype(jnp.float32)).astype(x.dtype)

def layer_norm(x, g, b):
    xf = x.astype(jnp.float32)
    mu = jnp.mean(xf, axis=-1, keepdims=True)
    var = jnp.mean(jnp.square(xf - mu), axis=-1, keepdims=True)
    y = (xf - mu) * lax.rsqrt(var + EPS)
    return (y * g.astype(jnp.float32) + b.astype(jnp.float32)).astype(x.dtype)

def rope(x, pos):
    d = x.shape[-1]
    inv = ROPE_THETA ** (-jnp.arange(0, d, 2, dtype=jnp.float32) / d)
    ang = pos.astype(jnp.float32)[..., None] * inv
    cos = jnp.cos(ang)[:, :, None, :]
    sin = jnp.sin(ang)[:, :, None, :]
    xf = x.astype(jnp.float32)
    x1, x2 = xf[..., : d // 2], xf[..., d // 2:]
    return jnp.concatenate([x1 * cos - x2 * sin, x2 * cos + x1 * sin], axis=-1).astype(x.dtype)

def dsa_mixer(q, k, v, iq, ik, iw, positions):
    Bn, S = q.shape[0], q.shape[1]
    q = rope(q, positions)
    k = rope(k[:, :, None, :], positions)[:, :, 0, :]
    iq = rope(iq, positions)
    ik = rope(ik[:, :, None, :], positions)[:, :, 0, :]
    n_top = min(TOPK_MAX, S // 4)
    nb = S // Q_BLOCK
    to_blocks = lambda a: jnp.swapaxes(a.reshape((Bn, nb, Q_BLOCK) + a.shape[2:]), 0, 1)
    s_idx = jnp.arange(S)

    def one_block(args):
        qj, iqj, iwj, j = args
        t = j * Q_BLOCK + jnp.arange(Q_BLOCK)
        rel = jax.nn.relu(jnp.einsum('bqhd,bsd->bqhs', iqj, ik).astype(jnp.float32) * IDX_DIM ** -0.5)
        score = jnp.einsum('bqh,bqhs->bqs', iwj.astype(jnp.float32) * IDX_HEADS ** -0.5, rel)
        causal = s_idx[None, :] <= t[:, None]
        score = jnp.where(causal[None], score, -jnp.inf)
        _, idx = lax.top_k(score, n_top)
        flat = idx.reshape(Bn, Q_BLOCK * n_top, 1)
        kg = jnp.take_along_axis(k, flat, axis=1).reshape(Bn, Q_BLOCK, n_top, HEAD_DIM)
        vg = jnp.take_along_axis(v, flat, axis=1).reshape(Bn, Q_BLOCK, n_top, HEAD_DIM)
        logits = jnp.einsum('bqhd,bqkd->bqhk', qj, kg).astype(jnp.float32) * HEAD_DIM ** -0.5
        valid = idx <= t[None, :, None]
        logits = jnp.where(valid[:, :, None, :], logits, -jnp.inf)
        p = jax.nn.softmax(logits, axis=-1).astype(v.dtype)
        return jnp.einsum('bqhk,bqkd->bqhd', p, vg)

    out = lax.map(one_block, (to_blocks(q), to_blocks(iq), to_blocks(iw), jnp.arange(nb)))
    return jnp.swapaxes(out, 0, 1).reshape(Bn, S, A_HEADS * HEAD_DIM)

def hgrn2_mixer(q, f_logit, i, g, lb, onorm_g):
    Bn, S, H, dk = q.shape
    dv = i.shape[-1]
    lb = lb.reshape(H, dk).astype(jnp.float32)
    log_f = jnp.logaddexp(jnp.log(lb), jnp.log1p(-lb) + jax.nn.log_sigmoid(f_logit.astype(jnp.float32)))
    kk = -jnp.expm1(log_f)
    nc = S // HGRN_CHUNK
    chunk = lambda a: a.astype(jnp.float32).reshape(Bn, nc, HGRN_CHUNK, H, a.shape[-1]).transpose(1, 0, 3, 2, 4)
    qc, kc, vc, lfc = chunk(q), chunk(kk), chunk(i), chunk(log_f)
    bc = jnp.cumsum(lfc, axis=3)
    tril = jnp.arange(HGRN_CHUNK)[:, None] >= jnp.arange(HGRN_CHUNK)[None, :]

    def step(state, xs):
        qj, kj, vj, bj = xs
        diff = bj[:, :, :, None, :] - bj[:, :, None, :, :]
        decay = jnp.exp(jnp.where(tril[:, :, None], diff, -jnp.inf))
        attn = jnp.einsum('bhtd,bhsd,bhtsd->bhts', qj, kj, decay)
        o = jnp.einsum('bhts,bhsv->bhtv', attn, vj) + jnp.einsum('bhtd,bhdv->bhtv', qj * jnp.exp(bj), state)
        b_last = bj[:, :, -1:, :]
        new_state = jnp.exp(b_last[:, :, 0, :])[..., None] * state + jnp.einsum('bhsd,bhsv->bhdv', kj * jnp.exp(b_last - bj), vj)
        return new_state, o

    s0 = jnp.zeros((Bn, H, dk, dv), jnp.float32)
    _, o = lax.scan(step, s0, (qc, kc, vc, bc))
    o = o.transpose(1, 0, 3, 2, 4).reshape(Bn, S, H, dv)
    o = rms_norm(o, onorm_g) * jax.nn.silu(g.astype(jnp.float32))
    return o.reshape(Bn, S, H * dv).astype(q.dtype)

def gmlp_mixer(uv, vn_g, vn_b, ws, bs):
    Bn, S = uv.shape[0], uv.shape[1]
    uv = jax.nn.gelu(uv, approximate=False)
    u, v = uv[..., :C_DIM], uv[..., C_DIM:]
    v = layer_norm(v, vn_g, vn_b)
    nc = S // C_CHUNK
    v = v.reshape(Bn, nc, C_CHUNK, C_GROUPS, C_GROUP_DIM)
    mask = jnp.tril(jnp.ones((C_CHUNK, C_CHUNK), ws.dtype))
    w = ws * mask[None]
    mixed = jnp.einsum('gts,bnsgd->bntgd', w, v) + bs.T[None, None, :, :, None]
    return u * mixed.reshape(Bn, S, C_DIM)

def swiglu(h, w_gate, w_up, w_down):
    return (jax.nn.silu(h @ w_gate) * (h @ w_up)) @ w_down

def moe_swiglu(h, w_router, w_gate, w_up, w_down):
    logits = jnp.einsum('bsd,de->bse', h, w_router).astype(jnp.float32)
    top_v, top_i = lax.top_k(logits, TOP_K)
    wts = jax.nn.softmax(top_v, axis=-1)
    gates = jnp.sum(jax.nn.one_hot(top_i, N_EXPERTS, dtype=jnp.float32) * wts[..., None], axis=-2)

    def per_seq(args):
        hb, gb = args
        a = jnp.einsum('sd,edf->sef', hb, w_gate)
        u = jnp.einsum('sd,edf->sef', hb, w_up)
        act = jax.nn.silu(a) * u * gb[:, :, None]
        return jnp.einsum('sef,efd->sd', act, w_down)

    return lax.map(per_seq, (h, gates.astype(h.dtype)))

def first_inputs(seed: int = 0) -> dict:
    key = jax.random.key(seed)
    ks = jax.random.split(key, 24)
    nrm = lambda k, shape, s: jax.random.normal(k, shape, jnp.float32) * s
    x = nrm(ks[0], (BATCH, SEQ, D_MODEL), 1.0)
    c = nrm(ks[1], (BATCH, D_MODEL), 1.0)
    offsets = jax.random.randint(ks[2], (BATCH, 1), 0, 4096, dtype=jnp.int32)
    positions = offsets + jnp.arange(SEQ, dtype=jnp.int32)[None, :]
    return {
        "x": x,
        "c": c,
        "positions": positions,
        "w_ada": nrm(ks[3], (DEPTH, D_MODEL, 6 * D_MODEL), 0.5 * D_MODEL ** -0.5),
        "b_ada": nrm(ks[4], (DEPTH, 6 * D_MODEL), 0.02),
        "g_norm_mix": 1.0 + nrm(ks[5], (DEPTH, D_MODEL), 0.02),
        "g_norm_ffn": 1.0 + nrm(ks[6], (DEPTH, D_MODEL), 0.02),
        "w_in": nrm(ks[7], (DEPTH, D_MODEL, IN_DIM), D_MODEL ** -0.5),
        "w_out": nrm(ks[8], (DEPTH, D_MIX, D_MODEL), D_MIX ** -0.5),
        "hgrn_lb_logits": nrm(ks[9], (DEPTH, B_HEADS * B_DK), 0.5),
        "hgrn_out_norm": 1.0 + nrm(ks[10], (DEPTH, B_DV), 0.02),
        "gmlp_vnorm_g": 1.0 + nrm(ks[11], (DEPTH, C_DIM), 0.02),
        "gmlp_vnorm_b": nrm(ks[12], (DEPTH, C_DIM), 0.02),
        "gmlp_w_s": nrm(ks[13], (DEPTH, C_GROUPS, C_CHUNK, C_CHUNK), C_CHUNK ** -0.5),
        "gmlp_b_s": 1.0 + nrm(ks[14], (DEPTH, C_GROUPS, C_CHUNK), 0.02),
        "ffn_w_gate": nrm(ks[15], (N_DENSE, D_MODEL, F_DENSE), D_MODEL ** -0.5),
        "ffn_w_up": nrm(ks[16], (N_DENSE, D_MODEL, F_DENSE), D_MODEL ** -0.5),
        "ffn_w_down": nrm(ks[17], (N_DENSE, F_DENSE, D_MODEL), F_DENSE ** -0.5),
        "moe_w_router": nrm(ks[18], (N_MOE, D_MODEL, N_EXPERTS), D_MODEL ** -0.5),
        "moe_w_gate": nrm(ks[19], (N_MOE, N_EXPERTS, D_MODEL, F_EXPERT), D_MODEL ** -0.5),
        "moe_w_up": nrm(ks[20], (N_MOE, N_EXPERTS, D_MODEL, F_EXPERT), D_MODEL ** -0.5),
        "moe_w_down": nrm(ks[21], (N_MOE, N_EXPERTS, F_EXPERT, D_MODEL), F_EXPERT ** -0.5),
        "g_final": 1.0 + nrm(ks[22], (D_MODEL,), 0.02),
    }

def first_block(x, c, positions, w_ada, b_ada, g_norm_mix, g_norm_ffn, w_in, w_out, hgrn_lb_logits, hgrn_out_norm, gmlp_vnorm_g, gmlp_vnorm_b, gmlp_w_s, gmlp_b_s, ffn_w_gate, ffn_w_up, ffn_w_down, moe_w_router, moe_w_gate, moe_w_up, moe_w_down, g_final):
    Bn, S = x.shape[0], x.shape[1]
    p_lb = jax.nn.softmax(hgrn_lb_logits.astype(jnp.float32), axis=0)
    cum = jnp.cumsum(p_lb, axis=0)
    lower_bounds = cum - cum[0:1]
    splits = [int(s) for s in np.cumsum(IN_WIDTHS)[:-1]]
    cond = jax.nn.silu(c)
    for l in range(DEPTH):
        mod = cond @ w_ada[l] + b_ada[l]
        sh1, sc1, g1, sh2, sc2, g2 = [m[:, None, :] for m in jnp.split(mod, 6, axis=-1)]
        h = rms_norm(x, g_norm_mix[l]) * (1 + sc1) + sh1
        z = h @ w_in[l]
        aq, ak, av, iq, ik, iw, bq, bf, bi, bg, cuv = jnp.split(z, splits, axis=-1)
        a_out = dsa_mixer(aq.reshape(Bn, S, A_HEADS, HEAD_DIM), ak, av, iq.reshape(Bn, S, IDX_HEADS, IDX_DIM), ik, iw, positions)
        b_out = hgrn2_mixer(bq.reshape(Bn, S, B_HEADS, B_DK), bf.reshape(Bn, S, B_HEADS, B_DK), bi.reshape(Bn, S, B_HEADS, B_DV), bg.reshape(Bn, S, B_HEADS, B_DV), lower_bounds[l], hgrn_out_norm[l])
        c_out = gmlp_mixer(cuv, gmlp_vnorm_g[l], gmlp_vnorm_b[l], gmlp_w_s[l], gmlp_b_s[l])
        mix = jnp.concatenate([a_out, b_out, c_out], axis=-1) @ w_out[l]
        x = x + g1 * mix
        h = rms_norm(x, g_norm_ffn[l]) * (1 + sc2) + sh2
        if l % 2 == 0:
            y = swiglu(h, ffn_w_gate[l // 2], ffn_w_up[l // 2], ffn_w_down[l // 2])
        else:
            y = moe_swiglu(h, moe_w_router[l // 2], moe_w_gate[l // 2], moe_w_up[l // 2], moe_w_down[l // 2])
        x = x + g2 * y
    return rms_norm(x, g_final)


N_HEADS = 16
HEAD_DIM_2 = D_MODEL // N_HEADS
HD = N_HEADS * HEAD_DIM_2
ROT_DIM = HEAD_DIM_2 // 4
ROPE_THETA_2 = 500000.0
N_KV_GROUPS = 2
HEADS_PER_GROUP = N_HEADS // N_KV_GROUPS
CMP_LEN = 32
CMP_STRIDE = 16
CMP_HIDDEN = 256
SLC_LEN = 64
SLC_TOPK = 16
WIN = 512
D_FF = 2816
CONV_W = 3
N_A_LAYERS = (DEPTH + 1) // 2
N_B_LAYERS = DEPTH // 2
RMS_EPS = 1e-6
NEG = -1e30
FORCED_SCORE = 1e6
FORGET_BIAS = 3.0


def rms_norm_2(x, g):
    xf = x.astype(jnp.float32)
    y = xf * lax.rsqrt(jnp.mean(xf * xf, axis=-1, keepdims=True) + RMS_EPS)
    return (y * g.astype(jnp.float32)).astype(x.dtype)

def partial_rope(x, pos):
    half = ROT_DIM // 2
    inv = ROPE_THETA_2 ** (-jnp.arange(half, dtype=jnp.float32) * (2.0 / ROT_DIM))
    ang = pos.astype(jnp.float32)[..., None] * inv
    cos = jnp.cos(ang)[..., None, :]
    sin = jnp.sin(ang)[..., None, :]
    xf = x.astype(jnp.float32)
    x1 = xf[..., :half]
    x2 = xf[..., half:ROT_DIM]
    out = jnp.concatenate([x1 * cos - x2 * sin, x2 * cos + x1 * sin, xf[..., ROT_DIM:]], axis=-1)
    return out.astype(x.dtype)

def forgetting_attention(xn, w_in, b_f, q_gain, k_gain, w_out):
    B, T, _ = xn.shape
    proj = xn @ w_in
    q = rms_norm_2(proj[..., :HD].reshape(B, T, N_HEADS, HEAD_DIM_2), q_gain)
    k = rms_norm_2(proj[..., HD:2 * HD].reshape(B, T, N_HEADS, HEAD_DIM_2), k_gain)
    v = proj[..., 2 * HD:3 * HD].reshape(B, T, N_HEADS, HEAD_DIM_2)
    log_f = jax.nn.log_sigmoid((proj[..., 3 * HD:] + b_f).astype(jnp.float32))
    c = jnp.cumsum(log_f, axis=1).transpose(0, 2, 1)
    q = q.transpose(0, 2, 1, 3)
    k = k.transpose(0, 2, 1, 3)
    v = v.transpose(0, 2, 1, 3)
    scale = HEAD_DIM_2 ** -0.5
    kpos = jnp.arange(T)

    def block(i):
        q0 = i * Q_BLOCK
        qb = lax.dynamic_slice_in_dim(q, q0, Q_BLOCK, axis=2)
        cb = lax.dynamic_slice_in_dim(c, q0, Q_BLOCK, axis=2)
        s = jnp.einsum('bhqd,bhkd->bhqk', qb, k, preferred_element_type=jnp.float32) * scale
        s = s + cb[..., :, None] - c[..., None, :]
        qpos = q0 + jnp.arange(Q_BLOCK)
        s = jnp.where(kpos[None, :] <= qpos[:, None], s, -jnp.inf)
        p = jax.nn.softmax(s, axis=-1)
        return jnp.einsum('bhqk,bhkd->bqhd', p.astype(v.dtype), v)

    o = lax.map(block, jnp.arange(T // Q_BLOCK))
    o = jnp.moveaxis(o, 0, 1).reshape(B, T, HD)
    return o @ w_out

def conv_ffn(xn, w_up, conv_w, conv_b, w_down):
    T = xn.shape[1]
    u = xn @ w_up
    u_pad = jnp.pad(u, ((0, 0), (CONV_W - 1, 0), (0, 0)))
    c = sum((conv_w[j] * u_pad[:, j:j + T] for j in range(CONV_W)), conv_b)
    gate, val = jnp.split(c, 2, axis=-1)
    return (jax.nn.silu(gate) * val) @ w_down

def shared_kv(h, positions, kv_norm, kv_w, kc_pe, vc_pe, kc_w1, kc_w2, vc_w1, vc_w2, kc_gain, ks_gain, kw_gain):
    B, T, _ = h.shape
    hn = rms_norm_2(h, kv_norm)
    parts = (hn @ kv_w).reshape(B, T, 6, N_KV_GROUPS, HEAD_DIM_2)
    kc_raw, vc_raw = parts[:, :, 0], parts[:, :, 1]
    ks, vs = parts[:, :, 2], parts[:, :, 3]
    kw, vw = parts[:, :, 4], parts[:, :, 5]
    n_cmp = (T - CMP_LEN) // CMP_STRIDE + 1
    starts = jnp.arange(n_cmp) * CMP_STRIDE
    idx = starts[:, None] + jnp.arange(CMP_LEN)[None, :]

    def compress(raw, pe, w1, w2):
        blk = raw[:, idx] + pe[None, None, :, None, :]
        blk = jnp.moveaxis(blk, 3, 2).reshape(B, n_cmp, N_KV_GROUPS, CMP_LEN * HEAD_DIM_2)
        return jax.nn.gelu(blk @ w1) @ w2

    kc = compress(kc_raw, kc_pe, kc_w1, kc_w2)
    vc = compress(vc_raw, vc_pe, vc_w1, vc_w2)
    ends = starts + CMP_LEN - 1
    kc = partial_rope(rms_norm_2(kc, kc_gain), positions[:, ends])
    ks = partial_rope(rms_norm_2(ks, ks_gain), positions)
    kw = partial_rope(rms_norm_2(kw, kw_gain), positions)
    return kc, vc, ks, vs, kw, vw

def native_sparse_attention(xn, positions, kc, vc, ks, vs, kw, vw, w_in, b_gate, q_gain, w_out):
    B, T, _ = xn.shape
    G, HG, dh = N_KV_GROUPS, HEADS_PER_GROUP, HEAD_DIM_2
    proj = xn @ w_in
    q = partial_rope(rms_norm_2(proj[..., :HD].reshape(B, T, N_HEADS, dh), q_gain), positions)
    q = q.reshape(B, T, G, HG, dh).transpose(0, 2, 3, 1, 4)
    gates = jax.nn.sigmoid((proj[..., HD:] + b_gate).astype(jnp.float32)).reshape(B, T, 3, G, HG)
    n_cmp = kc.shape[1]
    n_slc = T // SLC_LEN
    top_k = min(SLC_TOPK, n_slc)
    kc_g = kc.transpose(0, 2, 1, 3)
    vc_g = vc.transpose(0, 2, 1, 3)
    ks_blk = ks.transpose(0, 2, 1, 3).reshape(B, G, n_slc, SLC_LEN * dh)
    vs_blk = vs.transpose(0, 2, 1, 3).reshape(B, G, n_slc, SLC_LEN * dh)
    pad = ((0, 0), (0, 0), (WIN, 0), (0, 0))
    kw_pad = jnp.pad(kw.transpose(0, 2, 1, 3), pad)
    vw_pad = jnp.pad(vw.transpose(0, 2, 1, 3), pad)
    cmp_start = jnp.arange(n_cmp) * CMP_STRIDE
    cmp_end = cmp_start + CMP_LEN - 1
    slc_start = jnp.arange(n_slc) * SLC_LEN
    overlap = jnp.maximum(jnp.minimum(cmp_start[:, None] + CMP_LEN, slc_start[None, :] + SLC_LEN)
                          - jnp.maximum(cmp_start[:, None], slc_start[None, :]), 0).astype(jnp.float32) / CMP_LEN
    scale = dh ** -0.5
    bidx = jnp.arange(B)[:, None, None]
    gidx = jnp.arange(G)[None, :, None]
    jb = jnp.arange(n_slc)

    def block(i):
        q0 = i * Q_BLOCK
        qpos = q0 + jnp.arange(Q_BLOCK)
        qb = lax.dynamic_slice_in_dim(q, q0, Q_BLOCK, axis=3)
        s_c = jnp.einsum('bghqd,bgkd->bghqk', qb, kc_g, preferred_element_type=jnp.float32) * scale
        m_c = cmp_end[None, :] <= qpos[:, None]
        s_c = jnp.where(m_c, s_c, NEG)
        e_c = jnp.exp(s_c - jnp.max(s_c, axis=-1, keepdims=True)) * m_c
        p_c = e_c / jnp.maximum(jnp.sum(e_c, axis=-1, keepdims=True), 1.0)
        o_c = jnp.einsum('bghqk,bgkd->bqghd', p_c.astype(vc_g.dtype), vc_g)
        imp = jnp.einsum('bghqk,kn->bgqn', p_c, overlap)
        cur = qpos // SLC_LEN
        forced = (jb[None, :] == 0) | (jb[None, :] == cur[:, None]) | (jb[None, :] == cur[:, None] - 1)
        eligible = slc_start[None, :] <= qpos[:, None]
        score = jnp.where(eligible, jnp.where(forced, FORCED_SCORE, imp), NEG)
        _, sel = lax.top_k(score, top_k)
        flat = sel.reshape(B, G, Q_BLOCK * top_k)
        k_sel = ks_blk[bidx, gidx, flat].reshape(B, G, Q_BLOCK, top_k * SLC_LEN, dh)
        v_sel = vs_blk[bidx, gidx, flat].reshape(B, G, Q_BLOCK, top_k * SLC_LEN, dh)
        tok = (sel[..., None] * SLC_LEN + jnp.arange(SLC_LEN)).reshape(B, G, Q_BLOCK, top_k * SLC_LEN)
        m_s = tok <= qpos[None, None, :, None]
        s_s = jnp.einsum('bghqd,bgqkd->bghqk', qb, k_sel, preferred_element_type=jnp.float32) * scale
        p_s = jax.nn.softmax(jnp.where(m_s[:, :, None], s_s, -jnp.inf), axis=-1)
        o_s = jnp.einsum('bghqk,bgqkd->bqghd', p_s.astype(v_sel.dtype), v_sel)
        k_win = lax.dynamic_slice_in_dim(kw_pad, q0, WIN + Q_BLOCK, axis=2)
        v_win = lax.dynamic_slice_in_dim(vw_pad, q0, WIN + Q_BLOCK, axis=2)
        kpos = q0 - WIN + jnp.arange(WIN + Q_BLOCK)
        dist = qpos[:, None] - kpos[None, :]
        m_w = (dist >= 0) & (dist < WIN) & (kpos[None, :] >= 0)
        s_w = jnp.einsum('bghqd,bgkd->bghqk', qb, k_win, preferred_element_type=jnp.float32) * scale
        p_w = jax.nn.softmax(jnp.where(m_w, s_w, -jnp.inf), axis=-1)
        o_w = jnp.einsum('bghqk,bgkd->bqghd', p_w.astype(v_win.dtype), v_win)
        g = lax.dynamic_slice_in_dim(gates, q0, Q_BLOCK, axis=1)[..., None]
        o = g[:, :, 0] * o_c + g[:, :, 1] * o_s + g[:, :, 2] * o_w
        return o.astype(xn.dtype)

    o = lax.map(block, jnp.arange(T // Q_BLOCK))
    o = jnp.moveaxis(o, 0, 1).reshape(B, T, HD)
    return o @ w_out

def second_inputs(seed: int = 0) -> dict:
    key = jax.random.key(seed)
    ks = jax.random.split(key, 32)
    f32 = jnp.float32
    nrm = lambda k, shape, s: jax.random.normal(k, shape, f32) * s
    gain = lambda k, shape: 1.0 + 0.02 * jax.random.normal(k, shape, f32)
    D, F, G = D_MODEL, D_FF, N_KV_GROUPS
    return {
        "x": jax.random.normal(ks[0], (BATCH, SEQ, D), f32),
        "positions": jnp.broadcast_to(jnp.arange(SEQ, dtype=jnp.int32), (BATCH, SEQ)),
        "a_norm": gain(ks[1], (N_A_LAYERS, D)),
        "a_w_in": nrm(ks[2], (N_A_LAYERS, D, 3 * HD + N_HEADS), D ** -0.5),
        "a_b_f": FORGET_BIAS + 0.1 * jax.random.normal(ks[3], (N_A_LAYERS, N_HEADS), f32),
        "a_q_gain": gain(ks[4], (N_A_LAYERS, HEAD_DIM_2)),
        "a_k_gain": gain(ks[5], (N_A_LAYERS, HEAD_DIM_2)),
        "a_w_out": nrm(ks[6], (N_A_LAYERS, HD, D), HD ** -0.5),
        "kv_norm": gain(ks[7], (D,)),
        "kv_w": nrm(ks[8], (D, 6 * G * HEAD_DIM_2), D ** -0.5),
        "kc_pe": nrm(ks[9], (CMP_LEN, HEAD_DIM_2), 0.02),
        "vc_pe": nrm(ks[10], (CMP_LEN, HEAD_DIM_2), 0.02),
        "kc_w1": nrm(ks[11], (CMP_LEN * HEAD_DIM_2, CMP_HIDDEN), (CMP_LEN * HEAD_DIM_2) ** -0.5),
        "kc_w2": nrm(ks[12], (CMP_HIDDEN, HEAD_DIM_2), CMP_HIDDEN ** -0.5),
        "vc_w1": nrm(ks[13], (CMP_LEN * HEAD_DIM_2, CMP_HIDDEN), (CMP_LEN * HEAD_DIM_2) ** -0.5),
        "vc_w2": nrm(ks[14], (CMP_HIDDEN, HEAD_DIM_2), CMP_HIDDEN ** -0.5),
        "kc_gain": gain(ks[15], (HEAD_DIM_2,)),
        "ks_gain": gain(ks[16], (HEAD_DIM_2,)),
        "kw_gain": gain(ks[17], (HEAD_DIM_2,)),
        "b_norm": gain(ks[18], (N_B_LAYERS, D)),
        "b_w_in": nrm(ks[19], (N_B_LAYERS, D, HD + 3 * N_HEADS), D ** -0.5),
        "b_b_gate": nrm(ks[20], (N_B_LAYERS, 3 * N_HEADS), 0.01),
        "b_q_gain": gain(ks[21], (N_B_LAYERS, HEAD_DIM_2)),
        "b_w_out": nrm(ks[22], (N_B_LAYERS, HD, D), HD ** -0.5),
        "f_norm": gain(ks[23], (DEPTH, D)),
        "f_w_up": nrm(ks[24], (DEPTH, D, 2 * F), D ** -0.5),
        "f_conv_w": nrm(ks[25], (DEPTH, CONV_W, 2 * F), CONV_W ** -0.5),
        "f_conv_b": nrm(ks[26], (DEPTH, 2 * F), 0.01),
        "f_w_down": nrm(ks[27], (DEPTH, F, D), F ** -0.5),
    }

def second_block(x, positions, a_norm, a_w_in, a_b_f, a_q_gain, a_k_gain, a_w_out, kv_norm, kv_w, kc_pe, vc_pe, kc_w1, kc_w2, vc_w1, vc_w2, kc_gain, ks_gain, kw_gain, b_norm, b_w_in, b_b_gate, b_q_gain, b_w_out, f_norm, f_w_up, f_conv_w, f_conv_b, f_w_down):
    h = x
    kv = None
    for layer in range(DEPTH):
        if layer < N_A_LAYERS:
            i = layer
            h = h + forgetting_attention(rms_norm_2(h, a_norm[i]), a_w_in[i], a_b_f[i], a_q_gain[i], a_k_gain[i], a_w_out[i])
        else:
            i = layer - N_A_LAYERS
            kc, vc, ks, vs, kw, vw = kv
            h = h + native_sparse_attention(rms_norm_2(h, b_norm[i]), positions, kc, vc, ks, vs, kw, vw,
                                            b_w_in[i], b_b_gate[i], b_q_gain[i], b_w_out[i])
        h = h + conv_ffn(rms_norm_2(h, f_norm[layer]), f_w_up[layer], f_conv_w[layer], f_conv_b[layer], f_w_down[layer])
        if layer == N_A_LAYERS - 1:
            kv = shared_kv(h, positions, kv_norm, kv_w, kc_pe, vc_pe, kc_w1, kc_w2, vc_w1, vc_w2, kc_gain, ks_gain, kw_gain)
    return h


def setup_inputs(seed=0):
    out = dict(first_inputs(seed))
    for name, value in second_inputs(seed + 1).items():
        if name != "x":
            out[name + "_2"] = value
    return out


def reference(
    x, c, positions, w_ada, b_ada, g_norm_mix, g_norm_ffn, w_in, w_out, hgrn_lb_logits,
    hgrn_out_norm, gmlp_vnorm_g, gmlp_vnorm_b, gmlp_w_s, gmlp_b_s, ffn_w_gate, ffn_w_up,
    ffn_w_down, moe_w_router, moe_w_gate, moe_w_up, moe_w_down, g_final, positions_2, a_norm_2,
    a_w_in_2, a_b_f_2, a_q_gain_2, a_k_gain_2, a_w_out_2, kv_norm_2, kv_w_2, kc_pe_2, vc_pe_2,
    kc_w1_2, kc_w2_2, vc_w1_2, vc_w2_2, kc_gain_2, ks_gain_2, kw_gain_2, b_norm_2, b_w_in_2,
    b_b_gate_2, b_q_gain_2, b_w_out_2, f_norm_2, f_w_up_2, f_conv_w_2, f_conv_b_2, f_w_down_2,
):
    x = first_block(
        x, c, positions, w_ada, b_ada, g_norm_mix, g_norm_ffn, w_in, w_out, hgrn_lb_logits,
        hgrn_out_norm, gmlp_vnorm_g, gmlp_vnorm_b, gmlp_w_s, gmlp_b_s, ffn_w_gate, ffn_w_up,
        ffn_w_down, moe_w_router, moe_w_gate, moe_w_up, moe_w_down, g_final,
    )
    return second_block(
        x, positions_2, a_norm_2, a_w_in_2, a_b_f_2, a_q_gain_2, a_k_gain_2, a_w_out_2,
        kv_norm_2, kv_w_2, kc_pe_2, vc_pe_2, kc_w1_2, kc_w2_2, vc_w1_2, vc_w2_2, kc_gain_2,
        ks_gain_2, kw_gain_2, b_norm_2, b_w_in_2, b_b_gate_2, b_q_gain_2, b_w_out_2, f_norm_2,
        f_w_up_2, f_conv_w_2, f_conv_b_2, f_w_down_2,
    )


_drawn_inputs = setup_inputs


def setup_inputs(seed=0):
    import zlib

    import numpy as np

    out = dict(_drawn_inputs(seed))
    spreads = {}
    factors = {'hgrn_out_norm': 5.776,
     'gmlp_vnorm_g': 6.969,
     'gmlp_vnorm_b': 5.397,
     'gmlp_b_s': 8.0,
     'a_norm_2': 4.771,
     'a_b_f_2': 2.905,
     'a_q_gain_2': 8.0,
     'a_k_gain_2': 7.431,
     'kv_norm_2': 8.0,
     'kc_pe_2': 8.0,
     'vc_pe_2': 62.87,
     'kc_gain_2': 22.422,
     'ks_gain_2': 8.0,
     'kw_gain_2': 8.0,
     'b_norm_2': 8.0,
     'b_b_gate_2': 47.689,
     'b_q_gain_2': 8.0,
     'f_norm_2': 2.732,
     'f_conv_b_2': 5.722}
    for name, (base, spread) in spreads.items():
        noise = np.random.default_rng([zlib.crc32(name.encode()), seed]).standard_normal(out[name].shape)
        drawn = base * np.exp(spread * noise) if base else spread * noise
        out[name] = __import__('jax').numpy.asarray(drawn.astype(out[name].dtype))
    for name, factor in factors.items():
        out[name] = (out[name] * factor).astype(out[name].dtype)
    return out
```

```python
from contextlib import ExitStack, contextmanager

import numpy as np

import concourse.bass as bass
from concourse import mybir

F32 = mybir.dt.float32
F32R = mybir.dt.float32r
I32 = mybir.dt.int32
U32 = mybir.dt.uint32
ALU = mybir.AluOpType
ACT = mybir.ActivationFunctionType
AX = mybir.AxisListType

P = 128
D = 1024
KC = D // P
T = 256
TB = T // P
HD = 64
EPS = 1e-6
NEG = -1e30
GONE = -3e38
TOPK = 64
A_HEADS, IDX_HEADS = 6, 4
B_HEADS = 6
BD = B_HEADS * HD
C_DIM, C_GROUPS = 256, 4
IN_DIM = 2884
F_DENSE = 2816
N_EXPERTS, F_EXPERT = 8, 3584
HEADS2 = 16
FA_DIM = 3 * D + HEADS2
N_CMP = 15
KV_DIM = 768
NSA_DIM = D + 3 * HEADS2
FG = 512
NT = FG // P
RAW = 6
SLOT = 2048
LEVELS = 7

AQ, AK, AV, IQ, IK, IW, BQ, BF, BI, BG, CU = 0, 384, 448, 512, 768, 832, 836, 1220, 1604, 1988, 2372

C_ID = 0
C_M01 = C_ID + 128
C_NEG = C_M01 + 384
C_CM01 = C_NEG + 384
C_CNEG = C_CM01 + 32
C_INV1 = C_CNEG + 32
C_INV2 = C_INV1 + 32
C_IOTA = C_INV2 + 8
C_E = C_IOTA + 8
C_LM = C_E + (LEVELS + 2) * P
C_END = C_LM + LEVELS * P
AT = [0, P]


def constants():
    c = np.zeros((P, C_END), np.float32)
    p = np.arange(P)[:, None]
    f = np.arange(P)[None, :]
    c[:, C_ID:C_ID + P] = p == f
    for b in range(TB):
        w = (b + 1) * P
        m = (np.arange(w)[None, :] <= p + b * P).astype(np.float32)
        c[:, C_M01 + AT[b]:C_M01 + AT[b] + w] = m
        c[:, C_NEG + AT[b]:C_NEG + AT[b] + w] = (1 - m) * NEG
        m = (np.arange(N_CMP)[None, :] * 16 + 31 <= p + b * P).astype(np.float32)
        c[:, C_CM01 + 16 * b:C_CM01 + 16 * b + N_CMP] = m
        c[:, C_CNEG + 16 * b:C_CNEG + 16 * b + N_CMP] = (1 - m) * NEG
    c[:, C_INV1:C_INV1 + 32] = np.float32(10000.0) ** (-np.arange(0, 64, 2, dtype=np.float32) / 64)
    c[:, C_INV2:C_INV2 + 8] = np.float32(500000.0) ** (-np.arange(8, dtype=np.float32) * np.float32(2.0 / 16))
    c[:, C_IOTA:C_IOTA + 8] = np.arange(8)
    for level in range(LEVELS):
        m = 1 << level
        start = f // (2 * m) * (2 * m)
        ref = start + m - 1
        right = f - start >= m
        e = np.where(right, (p > ref) & (p <= f), (p > f) & (p <= ref))
        c[:, C_E + level * P:C_E + (level + 1) * P] = e
        same = p // (2 * m) == f // (2 * m)
        c[:, C_LM + level * P:C_LM + (level + 1) * P] = same & right & (p % (2 * m) < m)
    c[:, C_E + LEVELS * P:C_E + (LEVELS + 1) * P] = p > f
    c[:, C_E + (LEVELS + 1) * P:C_E + (LEVELS + 2) * P] = p <= f
    return c


class Counts:

    def __init__(self, eng):
        self.eng, self.waited, self.signalled, self.turns = eng, {}, {}, []

    def _value(self, count, sem):
        for i, rates in self.turns:
            if sem in rates:
                count = i * rates[sem] + count
        return count

    def got(self, sem, k=1):
        self.waited[sem] = self.waited.get(sem, 0) + k
        return self._value(self.waited[sem], sem)

    def sent(self, sem, k=1):
        self.signalled[sem] = self.signalled.get(sem, 0) + k
        return self._value(self.signalled[sem], sem)

    @contextmanager
    def loop(self, n, rates):
        before = (dict(self.waited), dict(self.signalled))
        with self.eng.Fori(0, n) as i:
            self.turns.append((i, rates))
            yield i
            self.turns.pop()
        for now, was in zip((self.waited, self.signalled), before):
            for sem, count in list(now.items()):
                one = count - was.get(sem, 0)
                assert one in (0, rates.get(sem, 0)), (sem.name, one, rates.get(sem, 0))
                now[sem] += one * (n - 1)


def build(nc, a, consts, out):
    with ExitStack() as ctx:
        def semaphore(name):
            return ctx.enter_context(nc.semaphore(name))

        raw_full = [semaphore(f"raw_full{r}") for r in range(RAW)]
        w_lo_ready = semaphore("w_lo_ready")
        result = semaphore("result")
        gain_free = semaphore("gain_free")
        mod_free = semaphore("mod_free")
        lp_free = semaphore("lp_free")
        lb_free = semaphore("lb_free")
        ws_free = semaphore("ws_free")
        conv_free = semaphore("conv_free")
        cmp_free = semaphore("cmp_free")
        w_used = semaphore("w_used")
        w_hi_ready = semaphore("w_hi_ready")
        tr_psum = semaphore("tr_psum")
        xT_hi_ready = semaphore("xT_hi_ready")
        sumsq_ready = semaphore("sumsq_ready")
        root_in = semaphore("root_in")
        root_out = semaphore("root_out")
        x_ready = semaphore("x_ready")
        att_centred = semaphore("att_centred")
        att_exp = semaphore("att_exp")
        att_tr = semaphore("att_tr")
        att_trcopied = semaphore("att_trcopied")
        heads_tr = semaphore("heads_tr")
        heads_sb = semaphore("heads_sb")
        conv_done = semaphore("conv_done")
        up_done = semaphore("up_done")
        silu_done = semaphore("silu_done")
        act_prod = semaphore("act_prod")
        act_hi = semaphore("act_hi")
        angles_ready = semaphore("angles_ready")
        sines = semaphore("sines")
        cond_silu = semaphore("cond_silu")
        cond_ready = semaphore("cond_ready")
        cond_hi = semaphore("cond_hi")
        lb_diff = semaphore("lb_diff")
        lb_exp = semaphore("lb_exp")
        lb_sum = semaphore("lb_sum")
        lb_ln = semaphore("lb_ln")
        lf_abs = semaphore("lf_abs")
        lf_exp = semaphore("lf_exp")
        lf_one = semaphore("lf_one")
        lf_ln = semaphore("lf_ln")
        lb_comp = semaphore("lb_comp")
        kk_sig = semaphore("kk_sig")
        decay_sum = semaphore("decay_sum")
        decay = semaphore("decay")
        o_out = semaphore("o_out")
        gate_silu = semaphore("gate_silu")
        gelu_uv = semaphore("gelu_uv")
        ws_tr = semaphore("ws_tr")
        ws_sb = semaphore("ws_sb")
        gate_diff = semaphore("gate_diff")
        gate_exp = semaphore("gate_exp")
        conv_tr = semaphore("conv_tr")
        conv_sb = semaphore("conv_sb")
        raw_tr = semaphore("raw_tr")
        raw_sb = semaphore("raw_sb")
        blk_ready = semaphore("blk_ready")
        blk_hi = semaphore("blk_hi")
        hid_done = semaphore("hid_done")
        hid_sb = semaphore("hid_sb")
        kc_tr = semaphore("kc_tr")
        kc_sb = semaphore("kc_sb")
        bgate_added = semaphore("bgate_added")
        gates_sig = semaphore("gates_sig")
        lin_evac = semaphore("lin_evac")
        rows_ready = semaphore("rows_ready")
        xT_ready = semaphore("xT_ready")
        att_scores = semaphore("att_scores")
        att_probs = semaphore("att_probs")
        att_out = semaphore("att_out")
        att_taken = semaphore("att_taken")
        y_free = semaphore("y_free")
        act_ready = semaphore("act_ready")
        cond_tr = semaphore("cond_tr")
        cond_cols = semaphore("cond_cols")
        heads_ready = semaphore("heads_ready")
        idx_scores = semaphore("idx_scores")
        rec_rows = semaphore("rec_rows")
        level_prod = semaphore("level_prod")
        weighted = semaphore("weighted")
        rec_att = semaphore("rec_att")
        ws_masked = semaphore("ws_masked")
        v_normed = semaphore("v_normed")
        spatial = semaphore("spatial")
        router_logits = semaphore("router_logits")
        fa_logf_ready = semaphore("fa_logf_ready")
        fa_cumsum = semaphore("fa_cumsum")
        dup_ready = semaphore("dup_ready")
        blk_lo = semaphore("blk_lo")
        cmp_out = semaphore("cmp_out")
        kc_normed = semaphore("kc_normed")
        dve_step = semaphore("dve_step")
        stored = semaphore("stored")
        ld_first = semaphore("ld_first")
        ld_const = semaphore("ld_const")
        ld_conv = semaphore("ld_conv")
        ld_cmp = semaphore("ld_cmp")
        ld_gain = semaphore("ld_gain")
        ld_mod = semaphore("ld_mod")
        ld_x = semaphore("ld_x")
        ld_lb = semaphore("ld_lb")
        ld_lp = semaphore("ld_lp")
        ld_ws = semaphore("ld_ws")

        def sb(name, shape, dt=F32):
            return ctx.enter_context(nc.sbuf_tensor(name, shape, dt))

        raw = sb("raw", [P, RAW, SLOT])
        w_hi = sb("w_hi", [P, 2, SLOT], F32R)
        w_lo = sb("w_lo", [P, 2, SLOT], F32R)
        xT_hi = sb("xT_hi", [P, KC, T], F32R)
        xT_lo = sb("xT_lo", [P, KC, T], F32R)
        aT_hi = sb("aT_hi", [P, NT, T], F32R)
        aT_lo = sb("aT_lo", [P, NT, T], F32R)
        X = sb("X", [P, TB, D])
        Zf = sb("Z", [P, TB * FA_DIM])
        mix = sb("mix", [P, TB, D])
        const = sb("const", [P, C_END])
        small = sb("small", [P, 512])
        lp = sb("lp", [P, 576])
        arena = sb("arena", [P, 11520])
        ps = ctx.enter_context(nc.psum_tensor("ps", [P, 8, 512], F32))

        ident = const[:, C_ID:C_ID + P]
        ones = const[:, C_M01 + P:C_M01 + 2 * P]

        def zrows(width):
            return Zf[:, 0:TB * width].rearrange("p (b n) -> p b n", b=TB)

        acc = Zf[:, 0:2048].rearrange("p (b n) -> p b n", b=TB)
        H = Zf[:, 2048:4096].rearrange("p (b n) -> p b n", b=TB)
        gain = Zf[:, 4096:5120]

        class Cut:

            def __init__(self, t, at=0):
                self.t, self.at = t, at

            def __call__(self, size_, rows=P, **dims):
                s = self.t[0:rows, self.at:self.at + size_]
                self.at += size_
                assert self.at <= self.t.shape[1], self.at
                if dims:
                    keys = list(dims)
                    s = s.rearrange(f"p ({' '.join(keys)} rest_) -> p {' '.join(keys)} rest_", **dims)
                return s

        sm = Cut(small)
        sumsq = sm(2)
        rstd = sm(2)
        stat_a = sm(32)
        stat_b = sm(32)
        negmax = sm(4)
        rowsum = sm(4)
        rinv = sm(4)
        cos1, sin1 = sm(64, b=2), sm(64, b=2)
        cos2, sin2 = sm(16, b=2), sm(16, b=2)
        cosc, sinc = sm(8), sm(8)
        posf = sm(3)
        tick = sm(2)
        posi = small[:, sm.at:sm.at + 3].bitcast(I32)
        sm.at += 3
        top8 = sm(8)
        top_i = small[:, sm.at:sm.at + 8].bitcast(U32)
        sm.at += 8
        top_f = sm(8)
        ew = sm(8)
        router = sm(64, c=8)
        logits = sm(16, b=2)
        gates = sm(16, b=2)
        iw_half = sm(8, b=2)
        fa_logf = sm(32, b=2)
        fa_c = sm(32, b=2)
        bsT = sm(4)
        condT = sm(8)

        ar = Cut(arena)
        mod = ar(3 * D, m=3)
        a1 = ar.at
        attP = ar(1024)
        attT = ar(1024)
        rope_t = [ar(224) for _ in range(4)]
        headsT = ar(12 * T, n=12)
        idx_rel = ar(1024)
        idx_acc = ar(256)
        topw = ar(256)
        dsa_mask = ar(512, b=2)
        ar.at = a1
        h_qT, h_kT = ar(BD // HD * T), ar(BD // HD * T)
        h_W, h_QW = ar(1536), ar(1536)
        h_A = ar(1536)
        h_AX = ar(768)
        h_LF = Cut(arena)(768, b=2)
        h_t1 = Cut(arena, a1 + 3072)(768, b=2)
        h_t2 = Cut(arena, a1 + 3840)(768, b=2)
        h_kk = Cut(arena, a1 + 4608)(768, b=2)
        h_lb = Cut(arena, a1 + 6144)(768, b=2)
        h_t3 = Cut(arena, a1 + 5376)(768, b=2)
        h_O = Cut(arena, a1)(768, b=2)
        h_sq = Cut(arena, a1 + 768)(768, b=2)
        h_sg = Cut(arena, a1 + 1536)(768, b=2)
        ar.at = a1 + 3072
        ws = ar(512, g=4)
        wsT = ar(512, g=4)
        g_t = ar(512, b=2)
        bs_rows = ar(128, rows=4)
        ar.at = 0
        kvT = ar(4 * T, n=4, rows=HD)
        kv_v = ar(512, b=2)
        kcT = ar(32, rows=HD, g=2)
        vcr = ar(128, rows=N_CMP, g=2)
        b2 = ar.at
        attP2 = ar(1024)
        attT2 = ar(1024)
        qa, ka = ar(TB * HEADS2 * 66, b=2), ar(TB * HEADS2 * 66, b=2)
        qTb, kTb = ar(1024), ar(1024)
        fa_sq = ar(1024)
        ar.at = b2 + 2048
        nsa_tmp = ar(256)
        nq_sq = ar(1024)
        nrope = [ar(256) for _ in range(4)]
        nqT = ar(1024)
        ar.at = b2
        convT = ar(44 * 4)
        conv_rows = ar(512, j=4)
        cgate = ar(1024)
        cval = ar(1024)
        ar.at = b2
        rawdup = ar(512, b=2)
        rawT = ar(512)
        pe_rows = ar(128, rows=16)
        peT = ar(16)
        blk32 = ar(480, l=16)
        hidT = ar(60, c=2)
        w2c = ar(256)
        kc_n = ar(128, rows=N_CMP, g=2)
        kc_t = ar(128, rows=N_CMP, g=2)
        kv_sq = ar(512)
        crope = [ar(16, rows=N_CMP) for _ in range(4)]
        krope = [ar(32) for _ in range(4)]
        ar.at = a1
        act_g = ar(1024)
        act_f = ar(1024)
        conv_end = b2 + 176 + 512 + 2048
        if conv_end > a1:
            act_g = Cut(arena, conv_end)(1024)
            act_f = Cut(arena, conv_end + 1024)(1024)
        cond_rows = Cut(arena, 8192)(128, rows=KC)
        lb_rows = Cut(arena, a1 + 6912)(768, b=2)

        onorm, vn_g, vn_b = lp[:, 0:64], lp[:, 64:320], lp[:, 320:576]
        qg, kg = lp[:, 0:64], lp[:, 64:128]
        bf_b = lp[:, 128:144]
        ksg, kwg, kcg = lp[:, 144:208], lp[:, 208:272], lp[:, 272:336]
        bgate = lp[:, 336:384]
        nqg = lp[:, 384:448]

        plan = []

        def rows(w, c0, nk, f0, nf):
            return w[c0 * P:(c0 + nk) * P, f0:f0 + nf].rearrange("(k p) f -> p k f", p=P)

        def linear_slots(w, n):
            got = []
            for f0 in range(0, n, FG):
                nf = min(FG, n - f0)
                nk = KC if nf <= FG // 2 else KC // 2
                got += [(nk, nf, rows(w, c, nk, f0, nf)) for c in range(0, KC, nk)]
            return got

        block = ctx.enter_context(nc.Block())

        def linears():
            s = {}
            for l in range(2):
                for half in range(2):
                    s[f"ada{l}{half}"] = linear_slots(a["w_ada"][l, :, half * 3 * D:(half + 1) * 3 * D], 3 * D)
                s[f"in{l}"] = linear_slots(a["w_in"][l], IN_DIM)
                s[f"out{l}"] = linear_slots(a["w_out"][l], D)
            s["fa_in"] = linear_slots(a["a_w_in_2"][0], FA_DIM)
            s["fa_out"] = linear_slots(a["a_w_out_2"][0], D)
            s["kv"] = linear_slots(a["kv_w_2"], KV_DIM)
            for n in "kv":
                w = a[f"{n}c_w1_2"]
                s[f"{n}c"] = [(8, 256, rows(w, 0, 8, 0, 256)), (8, 256, rows(w, 8, 8, 0, 256))]
            s["nsa_in"] = linear_slots(a["b_w_in_2"][0], NSA_DIM)
            s["nsa_out"] = linear_slots(a["b_w_out_2"][0], D)
            return s

        SL = linears()
        N_GROUPS = F_DENSE // FG

        ORDER = ["ada00", "in0", "out0", "ada01", "ffn0", "ada10", "in1", "out1", "ada11", "moe",
                 "fa_in", "fa_out", "conv0", "kv", "kc", "vc", "nsa_in", "nsa_out", "conv1"]

        def slot_lengths():
            for name in ORDER:
                if name in SL:
                    yield from [nk * nf for nk, nf, _ in SL[name]]
                elif name == "moe":
                    yield from [SLOT] * (6 * N_EXPERTS * F_EXPERT // FG)
                else:
                    yield from [SLOT] * (6 * N_GROUPS + 3)

        LEN = list(slot_lengths())

        @block.sync
        def _(sp):
            counts = Counts(sp)
            got, sent = counts.got, counts.sent
            n = 0

            def load(src, nk, nf, loop=None):
                nonlocal n
                r = n % RAW
                if n >= RAW:
                    sp.wait_ge(w_lo_ready, got(w_lo_ready))
                dst = raw[:, r, 0:nk * nf].rearrange("p (k f) -> p k f", k=nk)
                sp.dma_start(dst, src).then_inc(raw_full[r], 16)
                n += 1

            def ffn_group(wg, wu, wd, f0, nf, r0):
                if nf == FG:
                    for w in (wg, wu):
                        for c in (0, 4):
                            load(w[c * P:(c + 4) * P, bass.ds(f0, nf)].rearrange("(k p) f -> p k f", p=P), 4, nf)
                    for c in (0, 2):
                        load(wd[bass.ds(r0 + c * P, 2 * P), :].rearrange("(k p) f -> p k f", p=P), 2, D)
                else:
                    for w in (wg, wu):
                        load(rows(w, 0, KC, f0, nf), KC, nf)
                    load(wd[r0:r0 + 2 * P, :].rearrange("(k p) f -> p k f", p=P), 2, D)

            def dense(wg, wu, wd):
                nonlocal n
                with counts.loop(N_GROUPS, {w_lo_ready: 6}) as g:
                    ffn_group(wg, wu, wd, g * FG, FG, g * FG)
                n += 6 * (N_GROUPS - 1)
                ffn_group(wg, wu, wd, N_GROUPS * FG, FG // 2, N_GROUPS * FG)

            for name in ORDER:
                if name in SL:
                    for nk, nf, src in SL[name]:
                        load(src, nk, nf)
                elif name == "ffn0":
                    dense(a["ffn_w_gate"][0], a["ffn_w_up"][0], a["ffn_w_down"][0])
                elif name == "moe":
                    groups = F_EXPERT // FG
                    wg = a["moe_w_gate"][0].rearrange("e d f -> (e d) f")
                    wu = a["moe_w_up"][0].rearrange("e d f -> (e d) f")
                    wd = a["moe_w_down"][0].rearrange("e f d -> (e f) d")
                    with counts.loop(N_EXPERTS, {w_lo_ready: 6 * groups}) as e:
                        with counts.loop(groups, {w_lo_ready: 6}) as g:
                            for w in (wg, wu):
                                for c in (0, 4):
                                    src = w[bass.ds(e * D + c * P, 4 * P), bass.ds(g * FG, FG)]
                                    load(src.rearrange("(k p) f -> p k f", p=P), 4, FG)
                            for c in (0, 2):
                                src = wd[bass.ds(e * F_EXPERT + g * FG + c * P, 2 * P), :]
                                load(src.rearrange("(k p) f -> p k f", p=P), 2, D)
                    n += 6 * (groups * N_EXPERTS - 1)
                else:
                    l = int(name[-1])
                    w = a["f_w_up_2"][l]
                    dense(w[:, 0:F_DENSE], w[:, F_DENSE:2 * F_DENSE], a["f_w_down_2"][l])
            assert n == len(LEN)
            sp.wait_ge(result, got(result))
            sp.dma_start(out[0].rearrange("(b p) n -> p b n", p=P), X[:, :, :]).then_inc(stored, 16)
            sp.wait_ge(stored, 16)

        @block.gpsimd
        def _(pool):
            counts = Counts(pool)
            got, sent = counts.got, counts.sent

            def load(dst, src, sem, **how):
                pool.dma_start(dst, src, **how).then_inc(sem, 16)

            load(const[:, :], consts, ld_const)
            load(X[:, :, :], a["x"][0].rearrange("(b p) n -> p b n", p=P), ld_x)
            load(cond_rows, a["c"][0].rearrange("(k p) -> k p", p=P), ld_first)
            load(posi[:, 0:2], a["positions"][0].rearrange("(b p) -> p b", p=P), ld_first,
                 allow_slow_non_contiguous=True)
            load(router, a["moe_w_router"][0].rearrange("(c p) e -> p c e", p=P), ld_first)

            def gain_row(src):
                pool.wait_ge(gain_free, got(gain_free))
                load(gain, src.partition_broadcast(P), ld_gain)

            def ada_bias(l, half):
                if (l, half) != (0, 0):
                    pool.wait_ge(mod_free, got(mod_free))
                load(arena[:, 0:3 * D], a["b_ada"][l, half * 3 * D:(half + 1) * 3 * D].partition_broadcast(P),
                     ld_mod)

            for l in range(2):
                ada_bias(l, 0)
                if l == 0:
                    load(gain, a["g_norm_mix"][l].partition_broadcast(P), ld_gain)
                else:
                    gain_row(a["g_norm_mix"][l])
                if l:
                    pool.wait_ge(lp_free, got(lp_free))
                load(onorm, a["hgrn_out_norm"][l].partition_broadcast(P), ld_lp)
                load(vn_g, a["gmlp_vnorm_g"][l].partition_broadcast(P), ld_lp)
                load(vn_b, a["gmlp_vnorm_b"][l].partition_broadcast(P), ld_lp)
                if l:
                    pool.wait_ge(lb_free, got(lb_free))
                    load(lb_rows, a["hgrn_lb_logits"].partition_broadcast(P), ld_lb)
                pool.wait_ge(ws_free, got(ws_free))
                load(ws, a["gmlp_w_s"][l].rearrange("g t s -> t g s"), ld_ws)
                load(bs_rows, a["gmlp_b_s"][l], ld_ws)
                ada_bias(l, 1)
                gain_row(a["g_norm_ffn"][l])
            gain_row(a["g_final"])
            pool.wait_ge(lp_free, got(lp_free))
            for dst, name in ((qg, "a_q_gain_2"), (kg, "a_k_gain_2"), (bf_b, "a_b_f_2")):
                load(dst, a[name][0].partition_broadcast(P), ld_lp)
            for dst, name in ((ksg, "ks_gain_2"), (kwg, "kw_gain_2"), (kcg, "kc_gain_2")):
                load(dst, a[name].partition_broadcast(P), ld_lp)
            load(bgate, a["b_b_gate_2"][0].partition_broadcast(P), ld_lp)
            load(nqg, a["b_q_gain_2"][0].partition_broadcast(P), ld_lp)
            load(posi[:, 0:2], a["positions_2"][0].rearrange("(b p) -> p b", p=P), ld_lp,
                 allow_slow_non_contiguous=True)
            ends = a["positions_2"][0].rearrange("(n s) -> n s", s=16)[1:1 + N_CMP, 15:16]
            load(posi[0:N_CMP, 2:3], ends, ld_lp, allow_slow_non_contiguous=True)
            gain_row(a["a_norm_2"][0])

            def conv_params(l):
                pool.wait_ge(conv_free, got(conv_free))
                load(conv_rows[0:44, 0:3, :], a["f_conv_w_2"][l].rearrange("j (t p) -> t j p", p=P), ld_conv)
                load(conv_rows[0:44, 3, :], a["f_conv_b_2"][l].rearrange("(t p) -> t p", p=P), ld_conv)
                gain_row(a["f_norm_2"][l])

            conv_params(0)
            gain_row(a["kv_norm_2"])
            for n in "kv":
                pool.wait_ge(cmp_free, got(cmp_free))
                load(pe_rows, a[f"{n}c_pe_2"].rearrange("(l s) d -> l (s d)", s=2), ld_cmp)
                load(w2c[:, 0:128].rearrange("p (c n) -> p c n", c=2),
                     a[f"{n}c_w2_2"].rearrange("(c p) n -> p c n", p=P), ld_cmp)
            gain_row(a["b_norm_2"][0])
            conv_params(1)

        @block.scalar
        def _(act):
            counts = Counts(act)
            got, sent = counts.got, counts.sent
            n = [0]

            def split():
                k = n[0]
                if k < len(LEN):
                    r = k % RAW
                    act.wait_ge(raw_full[r], got(raw_full[r], 16))
                    if k >= 2:
                        act.wait_ge(w_used, got(w_used))
                    act.activation(w_hi[:, k % 2, 0:LEN[k]], raw[:, r, 0:LEN[k]], ACT.Copy).then_inc(w_hi_ready, 1)
                n[0] += 1

            landed = {sem: 16 for sem in raw_full}

            def more(turns, per):
                n[0] += per * (turns - 1)

            def linear(name):
                for _ in SL[name]:
                    split()

            def to_columns():
                for k in range(4):
                    act.wait_ge(tr_psum, got(tr_psum))
                    act.activation(xT_hi[:, 2 * k:2 * k + 2, :],
                                             ps[:, k, :].rearrange("p (k t) -> p k t", k=2), ACT.Copy).then_inc(xT_hi_ready, 1)

            def square_sums(src):
                for b in range(TB):
                    act.activation(H[:, b, :], src[:, b, :], ACT.Square, accum_out=sumsq[:, b:b + 1]).then_inc(sumsq_ready, 1)

            def root(x, times=1):
                for _ in range(times):
                    act.wait_ge(root_in, got(root_in))
                    act.activation(x, x, ACT.Sqrt).then_inc(root_out, 1)

            def norm():
                act.wait_ge(x_ready, got(x_ready))
                square_sums(X)
                root(rstd)
                to_columns()

            def attend(P_, T_, nh, W, rows_=P):
                nch = (W + P - 1) // P
                kw = min(W, P)
                s = P_[:, 0:nh * 256].rearrange("p (h w) -> p h w", h=nh)[:, :, 0:W]
                act.wait_ge(att_centred, got(att_centred))
                act.activation(s, s, ACT.Exp).then_inc(att_exp, 1)
                act.wait_ge(att_tr, got(att_tr))
                for k in range((nh * nch * P + 511) // 512):
                    w = min(512, nh * nch * P - 512 * k)
                    ins = act.activation(T_[0:kw, 512 * k:512 * k + w], ps[0:kw, 6 + k, 0:w], ACT.Copy)
                ins.then_inc(att_trcopied, 1)

            def copy_heads(dst, banks, rows_):
                act.wait_ge(heads_tr, got(heads_tr))
                for k, (bank, w) in enumerate(banks):
                    act.activation(dst[0:rows_, 512 * k:512 * k + w], ps[0:rows_, bank, 0:w], ACT.Copy).then_inc(heads_sb, 1)

            def dense(conv):
                with counts.loop(N_GROUPS, {**landed, w_hi_ready: 6, w_used: 6, up_done: 4, silu_done: 4,
                                          act_prod: 4, act_hi: 4, conv_done: 4}):
                    group(NT, conv)
                more(N_GROUPS, 6)
                group(NT // 2, conv)

            def group(nt, conv=False):
                nsl = 2 if nt == NT else 1
                for _ in range(2 * nsl):
                    split()
                for j in range(nt):
                    if conv:
                        act.wait_ge(conv_done, got(conv_done))
                        g = cgate[:, j * T:(j + 1) * T]
                    else:
                        act.wait_ge(up_done, got(up_done))
                        g = ps[:, j, 0:T]
                    act.activation(act_g[:, j * T:(j + 1) * T], g, ACT.Silu).then_inc(silu_done, 1)
                    act.wait_ge(act_prod, got(act_prod))
                    act.activation(aT_hi[:, j, :], act_f[:, j * T:(j + 1) * T], ACT.Copy).then_inc(act_hi, 1)
                for _ in range(nsl):
                    split()

            split()
            def rotary_sines():
                act.wait_ge(angles_ready, got(angles_ready))
                act.activation(sin1[:, :, :], sin1[:, :, :], ACT.Sin).then_inc(sines, 1)
                act.activation(cos1[:, :, :], cos1[:, :, :], ACT.Sin).then_inc(sines, 1)

            act.wait_ge(ld_first, 48)
            act.activation(cond_rows, cond_rows, ACT.Silu).then_inc(cond_silu, 1)
            rotary_sines()

            def cond_columns():
                act.wait_ge(cond_ready, got(cond_ready))
                act.activation(xT_hi[:, 0:4, :].rearrange("p a (b m) -> p (a b) m", b=2),
                                         condT.unsqueeze(2).to_broadcast([P, KC, P]), ACT.Copy).then_inc(cond_hi, 1)

            for l in range(2):
                cond_columns()
                linear(f"ada{l}0")
                norm()
                linear(f"in{l}")
                copy_heads(headsT.rearrange("p n t -> p (n t)"), [(k, 512) for k in range(6)], HD)
                for b in range(TB):
                    for _ in range(2):
                        attend(attP, attT, 3, (b + 1) * P)
                if l:
                    act.wait_ge(lb_diff, got(lb_diff))
                    act.activation(h_t2[:, :, :], lb_rows, ACT.Exp).then_inc(lb_exp, 1)
                    act.wait_ge(lb_sum, got(lb_sum))
                    act.activation(h_t1[:, 0, :], h_t1[:, 0, :], ACT.Ln).then_inc(lb_ln, 1)
                act.wait_ge(lf_abs, got(lf_abs))
                act.activation(h_t1, h_t1, ACT.Exp, scale=-1.0).then_inc(lf_exp, 1)
                act.wait_ge(lf_exp, sent(lf_exp))
                act.wait_ge(lf_one, got(lf_one))
                act.activation(h_t1, h_t1, ACT.Ln).then_inc(lf_ln, 1)
                if l:
                    act.wait_ge(lf_abs, got(lf_abs))
                    act.activation(h_t1, h_t1, ACT.Exp, scale=-1.0).then_inc(lf_exp, 1)
                    act.wait_ge(lf_exp, sent(lf_exp))
                    act.wait_ge(lf_one, got(lf_one))
                    act.activation(h_t1, h_t1, ACT.Ln).then_inc(lf_ln, 1)
                    act.activation(h_t3[:, 0, :], h_lb[:, 1, :], ACT.Exp).then_inc(lb_comp, 1)
                    act.wait_ge(lb_comp, sent(lb_comp))
                z = zrows(IN_DIM)
                act.activation(h_kk, z[:, :, BF:BF + BD], ACT.Sigmoid, scale=-1.0).then_inc(kk_sig, 1)
                act.wait_ge(heads_tr, got(heads_tr))
                for k in range(6):
                    dst = (h_qT if k < 3 else h_kT)[0:HD, 512 * (k % 3):512 * (k % 3) + 512]
                    act.activation(dst, ps[0:HD, k, :], ACT.Copy).then_inc(heads_sb, 1)
                for level in range(LEVELS + 1):
                    act.wait_ge(decay_sum, got(decay_sum))
                    act.activation(h_W[0:HD, :].rearrange("p (a n) -> p a n", a=3), ps[0:HD, 0:3, :],
                                             ACT.Exp).then_inc(decay, 1)
                act.wait_ge(o_out, got(o_out))
                act.activation(h_sg, z[:, :, BG:BG + BD], ACT.Silu).then_inc(gate_silu, 1)
                act.activation(z[:, :, CU:CU + 2 * C_DIM], z[:, :, CU:CU + 2 * C_DIM], ACT.Gelu).then_inc(gelu_uv, 1)
                act.wait_ge(gelu_uv, sent(gelu_uv))
                root(stat_a[:, 0:12])
                act.wait_ge(ws_tr, got(ws_tr))
                act.activation(wsT.rearrange("p g n -> p (g n)"), ps[:, 0, :], ACT.Copy).then_inc(ws_sb, 1)
                act.activation(bsT, ps[:, 1, 0:4], ACT.Copy).then_inc(ws_sb, 1)
                root(stat_b[:, 0:2])
                to_columns()
                linear(f"out{l}")
                cond_columns()
                linear(f"ada{l}1")
                norm()
                if l == 0:
                    dense(False)
                else:
                    for b in range(TB):
                        act.wait_ge(gate_diff, got(gate_diff))
                        act.activation(ew[:, 1:2], ew[:, 0:1], ACT.Exp).then_inc(gate_exp, 1)
                    groups = F_EXPERT // FG
                    names = {**landed, w_hi_ready: 6, w_used: 6, up_done: 4, silu_done: 4, act_prod: 4, act_hi: 4}
                    with counts.loop(N_EXPERTS, {k: v * groups for k, v in names.items()}):
                        with counts.loop(groups, names):
                            group(NT)
                    more(N_EXPERTS * groups, 6)
            act.wait_ge(x_ready, got(x_ready))
            square_sums(X)
            root(rstd)
            act.wait_ge(angles_ready, got(angles_ready))
            for s in (sin2, cos2):
                act.activation(s, s, ACT.Sin).then_inc(sines, 1)
            for s in (sinc, cosc):
                act.activation(s[0:N_CMP, :], s[0:N_CMP, :], ACT.Sin).then_inc(sines, 1)
            norm()
            linear("fa_in")
            act.wait_ge(lf_abs, got(lf_abs))
            act.activation(stat_b, stat_b, ACT.Exp, scale=-1.0).then_inc(lf_exp, 1)
            act.wait_ge(lf_exp, sent(lf_exp))
            act.wait_ge(lf_one, got(lf_one))
            act.activation(stat_b, stat_b, ACT.Ln).then_inc(lf_ln, 1)
            root(stat_a[:, 0:16], 4)
            for hb in range(4):
                act.wait_ge(heads_tr, got(heads_tr))
                for dst, bank in ((qTb, 0), (kTb, 4)):
                    for k in range(2):
                        act.activation(dst[0:66, 512 * k:512 * k + 512], ps[0:66, bank + k, :], ACT.Copy).then_inc(heads_sb, 1)
                for b in range(TB):
                    attend(attP2, attT2, 4, (b + 1) * P)
            to_columns()
            linear("fa_out")

            def conv_layer():
                act.wait_ge(conv_tr, got(conv_tr))
                act.activation(convT, ps[:, 7, 0:176], ACT.Copy).then_inc(conv_sb, 1)
                norm()
                dense(True)

            conv_layer()
            norm()
            linear("kv")
            root(stat_a[:, 0:2], 4)
            copy_heads(kvT.rearrange("p n t -> p (n t)"), [(0, 512), (1, 512)], HD)
            for n_ in "kv":
                act.wait_ge(raw_tr, got(raw_tr))
                act.activation(rawT, ps[:, 2, :], ACT.Copy).then_inc(raw_sb, 1)
                act.activation(peT, ps[:, 3, 0:16], ACT.Copy).then_inc(raw_sb, 1)
                act.wait_ge(blk_ready, got(blk_ready))
                act.activation(xT_hi[:, 0:2, :].rearrange("p a t -> p (a t)")[:, 0:480],
                                         blk32.rearrange("p l n -> p (l n)"), ACT.Copy).then_inc(blk_hi, 1)
                linear(f"{n_}c")
                act.wait_ge(hid_done, got(hid_done))
                for c in range(2):
                    ins = act.activation(hidT[:, c, :], ps[:, 4 + c, 0:2 * N_CMP], ACT.Gelu_apprx_tanh)
                ins.then_inc(hid_sb, 1)
                if n_ == "k":
                    root(stat_a[0:N_CMP, 0:2])
                    act.wait_ge(kc_tr, got(kc_tr))
                    act.activation(kcT[:, :, 0:N_CMP],
                                             ps[0:HD, 7, 0:32].rearrange("p (g n) -> p g n", g=2)[:, :, 0:N_CMP],
                                             ACT.Copy).then_inc(kc_sb, 1)
            norm()
            linear("nsa_in")
            act.wait_ge(bgate_added, got(bgate_added))
            z = zrows(NSA_DIM)
            act.activation(z[:, :, D:NSA_DIM], z[:, :, D:NSA_DIM], ACT.Sigmoid).then_inc(gates_sig, 1)
            root(stat_a[:, 0:16], 2)
            for hb in range(4):
                copy_heads(nqT, [(0, 512), (1, 512)], HD)
                for b in range(TB):
                    attend(attP2, attT2, 4, N_CMP)
                    attend(attP2, attT2, 4, (b + 1) * P)
                    attend(attP2, attT2, 4, (b + 1) * P)
            to_columns()
            linear("nsa_out")
            conv_layer()

        @block.tensor
        def _(pe):
            counts = Counts(pe)
            got, sent = counts.got, counts.sent
            n = [0]

            def slot(nk):
                k = n[0]
                pe.wait_ge(w_lo_ready, got(w_lo_ready))
                n[0] += 1
                return [w[:, k % 2, 0:LEN[k]].rearrange("p (k f) -> p k f", k=nk) for w in (w_hi, w_lo)]

            def three(out_, lh, ll, rh, rl, start, stop):
                pe.matmul(out_, lh, rh, start=start, stop=False)
                pe.matmul(out_, lh, rl, start=False, stop=False)
                return pe.matmul(out_, ll, rh, start=False, stop=stop)

            def linear(name, blocks=TB, cond=False):
                f = gi = 0
                slots = SL[name]
                i = 0
                while i < len(slots):
                    nk, nf, _ = slots[i]
                    per = KC // nk
                    if gi >= 2:
                        pe.wait_ge(lin_evac, got(lin_evac))
                    for part in range(per):
                        hi, lo = slot(nk)
                        for k in range(nk):
                            c = part * nk + k
                            for b in range(blocks):
                                if cond:
                                    xh, xl = (x[:, c // 2, c % 2 * P:c % 2 * P + P] for x in (xT_hi, xT_lo))
                                else:
                                    xh, xl = (x[:, c, b * P:(b + 1) * P] for x in (xT_hi, xT_lo))
                                last = three(ps[:, 2 * (gi % 2) + b, 0:nf], xh, xl, hi[:, k, :], lo[:, k, :],
                                             c == 0, c == KC - 1)
                        last.then_inc(w_used, 1)
                    i += per
                    gi += 1
                got(lin_evac, min(2, gi))

            def to_columns(src):
                pe.wait_ge(rows_ready, got(rows_ready))
                for k in range(4):
                    for c in (2 * k, 2 * k + 1):
                        for b in range(TB):
                            last = pe.transpose(ps[:, k, (c % 2) * T + b * P:(c % 2) * T + (b + 1) * P],
                                                src[:, b, c * P:(c + 1) * P], ident)
                    last.then_inc(tr_psum, 1)
                pe.wait_ge(xT_ready, got(xT_ready, 4))

            def attend(P_, T_, q, k, v, nh, W):
                nch = (W + P - 1) // P
                kw = min(W, P)
                for h in range(nh):
                    last = pe.matmul(ps[:, 4 + h // 2, (h % 2) * 256:(h % 2) * 256 + W], q(h), k(h),
                                     start=True, stop=True)
                last.then_inc(att_scores, 1)
                pe.wait_ge(att_probs, got(att_probs))
                s = P_[:, 0:nh * 256].rearrange("p (h w) -> p h w", h=nh)
                for h in range(nh):
                    for c in range(nch):
                        u = h * nch + c
                        last = pe.transpose(ps[0:kw, 6 + u // 4, (u % 4) * P:(u % 4 + 1) * P],
                                            s[:, h, c * P:c * P + kw], ident)
                last.then_inc(att_tr, 1)
                pe.wait_ge(att_trcopied, got(att_trcopied))
                for h in range(nh):
                    for c in range(nch):
                        u = h * nch + c
                        last = pe.matmul(ps[:, 3, h * HD:(h + 1) * HD], T_[0:kw, u * P:(u + 1) * P], v(h, c),
                                         start=c == 0, stop=c == nch - 1)
                last.then_inc(att_out, 1)
                pe.wait_ge(att_taken, got(att_taken))

            def group(nt, first):
                nf = nt * P
                nk = 4 if nt == NT else KC
                for m in range(2):
                    for part in range(KC // nk):
                        hi, lo = slot(nk)
                        for j in range(nt):
                            for k in range(nk):
                                c = part * nk + k
                                last = three(ps[:, j, m * T:(m + 1) * T], hi[:, k, j * P:(j + 1) * P],
                                             lo[:, k, j * P:(j + 1) * P], xT_hi[:, c, :], xT_lo[:, c, :],
                                             c == 0, c == KC - 1)
                            if m == 1 and part == KC // nk - 1:
                                last.then_inc(up_done, 1)
                        if m == 0 or part < KC // nk - 1:
                            last.then_inc(w_used, 1)
                up_open = True
                pe.wait_ge(y_free, got(y_free))
                for part in range(nt // 2):
                    hi, lo = slot(2)
                    for k in range(2):
                        j = 2 * part + k
                        pe.wait_ge(act_ready, got(act_ready))
                        for b in range(TB):
                            for half in range(2):
                                last = three(ps[:, 4 + 2 * b + half, :], aT_hi[:, j, b * P:(b + 1) * P],
                                             aT_lo[:, j, b * P:(b + 1) * P], hi[:, k, half * 512:(half + 1) * 512],
                                             lo[:, k, half * 512:(half + 1) * 512], j == 0, j == nt - 1)
                                if up_open:
                                    last.then_inc(w_used, 1)
                                    up_open = False
                    last.then_inc(w_used, 1)

            FFN_RATES = {w_lo_ready: 6, w_used: 6, up_done: 4, y_free: 1, act_ready: 4}

            def dense():
                with counts.loop(N_GROUPS, FFN_RATES):
                    group(NT, False)
                n[0] += 6 * (N_GROUPS - 1)
                group(NT // 2, False)
                got(y_free)

            pe.wait_ge(ld_const, 16)
            pe.wait_ge(cond_silu, got(cond_silu))
            pe.transpose(ps[:, 7, 0:KC], cond_rows, ident[0:KC, 0:KC]).then_inc(cond_tr, 1)
            for l in range(2):
                pe.wait_ge(cond_cols, got(cond_cols))
                linear(f"ada{l}0", 1, True)
                to_columns(H)
                linear(f"in{l}")
                z = zrows(IN_DIM)
                pe.wait_ge(heads_ready, got(heads_ready))
                u = 0
                for col in [AQ + HD * h for h in range(A_HEADS)] + [AK] + [IQ + HD * h for h in range(IDX_HEADS)] + [IK]:
                    for b in range(TB):
                        last = pe.transpose(ps[0:HD, u // 4, (u % 4) * P:(u % 4 + 1) * P], z[:, b, col:col + HD], ident)
                        u += 1
                last.then_inc(heads_tr, 1)
                pe.wait_ge(heads_sb, got(heads_sb, 6))
                for b in range(TB):
                    W = (b + 1) * P
                    for h in range(IDX_HEADS):
                        last = pe.matmul(ps[:, 2 * b + h // 2, (h % 2) * 256:(h % 2) * 256 + W],
                                         headsT[0:HD, 7 + h, b * P:(b + 1) * P], headsT[0:HD, 11, 0:W],
                                         start=True, stop=True)
                    last.then_inc(idx_scores, 1)
                for b in range(TB):
                    for hb in range(2):
                        attend(attP, attT, lambda h: headsT[0:HD, 3 * hb + h, b * P:(b + 1) * P],
                               lambda h: headsT[0:HD, 6, 0:(b + 1) * P],
                               lambda h, c: z[:, c, AV:AV + HD], 3, (b + 1) * P)
                pe.wait_ge(rec_rows, got(rec_rows))
                u = 0
                for src, c0 in ((z, BQ), (h_kk, 0)):
                    for h in range(B_HEADS):
                        for b in range(TB):
                            last = pe.transpose(ps[0:HD, u // 4, (u % 4) * P:(u % 4 + 1) * P],
                                                src[:, b, c0 + h * HD:c0 + (h + 1) * HD], ident)
                            u += 1
                last.then_inc(heads_tr, 1)
                pe.wait_ge(heads_sb, got(heads_sb, 6))

                def cut3(t, h, b):
                    return t[0:HD, (h * TB + b) * P:(h * TB + b + 1) * P]

                def products(kt, qt):
                    for h in range(B_HEADS):
                        for b in range(TB):
                            u = h * TB + b
                            last = pe.matmul(ps[:, 3 + u // 4, (u % 4) * P:(u % 4 + 1) * P], cut3(kt, h, b),
                                             cut3(qt, h, b), start=True, stop=True)
                    last.then_inc(level_prod, 1)

                products(h_kT, h_qT)
                for level in range(LEVELS + 1):
                    for h in range(B_HEADS):
                        for b in range(TB):
                            u = h * TB + b
                            e = C_E + (level + (b if level == LEVELS else 0)) * P
                            last = pe.matmul(ps[0:HD, u // 4, (u % 4) * P:(u % 4 + 1) * P],
                                             h_LF[:, b, h * HD:(h + 1) * HD], const[:, e:e + P], start=True, stop=True)
                    last.then_inc(decay_sum, 1)
                    pe.wait_ge(weighted, got(weighted))
                    if level < LEVELS:
                        products(h_W, h_QW)
                    else:
                        for h in range(B_HEADS):
                            last = pe.matmul(ps[:, 3 + h // 4, (h % 4) * P:(h % 4 + 1) * P], cut3(h_W, h, 0),
                                             cut3(h_QW, h, 1), start=True, stop=True)
                        last.then_inc(level_prod, 1)
                pe.wait_ge(rec_att, got(rec_att))
                for h in range(B_HEADS):
                    v = [z[:, b, BI + h * HD:BI + (h + 1) * HD] for b in range(TB)]
                    A = [h_A[:, (h * TB + b) * P:(h * TB + b + 1) * P] for b in range(TB)]
                    pe.matmul(ps[:, 6, h * HD:(h + 1) * HD], A[0], v[0], start=True, stop=True)
                    pe.matmul(ps[:, 7, h * HD:(h + 1) * HD], h_AX[:, h * P:(h + 1) * P], v[0], start=True, stop=False)
                    last = pe.matmul(ps[:, 7, h * HD:(h + 1) * HD], A[1], v[1], start=False, stop=True)
                last.then_inc(o_out, 1)
                pe.wait_ge(ws_masked, got(ws_masked))
                for g in range(C_GROUPS):
                    pe.transpose(ps[:, 0, g * P:(g + 1) * P], ws[:, g, :], ident)
                pe.transpose(ps[:, 1, 0:4], bs_rows, ident[0:4, 0:4]).then_inc(ws_tr, 1)
                pe.wait_ge(ws_sb, got(ws_sb, 2))
                pe.wait_ge(v_normed, got(v_normed))
                for b in range(TB):
                    for g in range(C_GROUPS):
                        c = CU + C_DIM + g * HD
                        last = pe.matmul(ps[:, 2 + b, g * HD:(g + 1) * HD], wsT[:, g, :], z[:, b, c:c + HD],
                                         start=True, stop=True)
                last.then_inc(spatial, 1)
                to_columns(mix)
                linear(f"out{l}")
                pe.wait_ge(cond_cols, got(cond_cols))
                linear(f"ada{l}1", 1, True)
                to_columns(H)
                if l == 0:
                    dense()
                else:
                    for b in range(TB):
                        for c in range(KC):
                            for x in (xT_hi, xT_lo):
                                last = pe.matmul(ps[:, 4, b * 8:b * 8 + 8], x[:, c, b * P:(b + 1) * P].bitcast(F32),
                                                 router[:, c, :], start=c == 0 and x is xT_hi,
                                                 stop=c == KC - 1 and x is xT_lo)
                    last.then_inc(router_logits, 1)
                    groups = F_EXPERT // FG
                    with counts.loop(N_EXPERTS, {k: v * groups for k, v in FFN_RATES.items()}):
                        with counts.loop(groups, FFN_RATES):
                            group(NT, False)
                    n[0] += 6 * (N_EXPERTS * groups - 1)
                    got(y_free)
            to_columns(H)
            linear("fa_in")
            z = zrows(FA_DIM)
            pe.wait_ge(fa_logf_ready, got(fa_logf_ready))
            tri = const[:, C_E + (LEVELS + 1) * P:C_E + (LEVELS + 2) * P]
            pe.matmul(ps[:, 0, 0:16], tri, fa_logf[:, 0, :], start=True, stop=True)
            pe.matmul(ps[:, 0, 16:32], ones, fa_logf[:, 0, :], start=True, stop=False)
            pe.matmul(ps[:, 0, 16:32], tri, fa_logf[:, 1, :], start=False, stop=True).then_inc(fa_cumsum, 1)
            pe.wait_ge(heads_ready, got(heads_ready))
            for hb in range(4):
                for src, bank in ((qa, 0), (ka, 4)):
                    for h in range(4):
                        for b in range(TB):
                            c = (4 * hb + h) * 66
                            last = pe.transpose(ps[0:66, bank + h // 2, (h % 2) * T + b * P:(h % 2) * T + (b + 1) * P],
                                                src[:, b, c:c + 66], ident)
                last.then_inc(heads_tr, 1)
                pe.wait_ge(heads_sb, got(heads_sb, 4))
                for b in range(TB):
                    attend(attP2, attT2, lambda h: qTb[0:66, h * T + b * P:h * T + (b + 1) * P],
                           lambda h: kTb[0:66, h * T:h * T + (b + 1) * P],
                           lambda h, c: z[:, c, 2 * D + (4 * hb + h) * HD:2 * D + (4 * hb + h + 1) * HD],
                           4, (b + 1) * P)
            to_columns(mix)
            linear("fa_out")

            def conv_layer(l):
                pe.wait_ge(ld_conv, 32 * (l + 1))
                for j in range(4):
                    last = pe.transpose(ps[:, 7, j * 44:(j + 1) * 44], conv_rows[0:44, j, :], ident[0:44, 0:44])
                last.then_inc(conv_tr, 1)
                pe.wait_ge(conv_sb, got(conv_sb))
                to_columns(H)
                dense()

            conv_layer(0)
            to_columns(H)
            linear("kv")
            z = zrows(KV_DIM)
            pe.wait_ge(heads_ready, got(heads_ready))
            for i, c0 in enumerate((256, 320, 512, 576)):
                for b in range(TB):
                    last = pe.transpose(ps[0:HD, i // 2, (i % 2) * T + b * P:(i % 2) * T + (b + 1) * P],
                                        z[:, b, c0:c0 + HD], ident)
            last.then_inc(heads_tr, 1)
            pe.wait_ge(heads_sb, got(heads_sb, 2))
            for i, name in enumerate("kv"):
                pe.wait_ge(dup_ready, got(dup_ready))
                for g in range(2):
                    for b in range(TB):
                        pe.transpose(ps[:, 2, g * T + b * P:g * T + (b + 1) * P], rawdup[:, b, g * P:(g + 1) * P], ident)
                pe.wait_ge(ld_cmp, 32 * (i + 1))
                pe.transpose(ps[:, 3, 0:16], pe_rows, ident[0:16, 0:16]).then_inc(raw_tr, 1)
                pe.wait_ge(blk_lo, got(blk_lo))
                bh, bl = (x[:, 0:2, :].rearrange("p a t -> p (a t)")[:, 0:480].rearrange("p (l n) -> p l n", l=16)
                          for x in (xT_hi, xT_lo))
                for part in range(2):
                    hi, lo = slot(8)
                    for c in range(2):
                        for k in range(8):
                            lpair = 8 * part + k
                            last = three(ps[:, 4 + c, 0:2 * N_CMP], hi[:, k, c * P:(c + 1) * P],
                                         lo[:, k, c * P:(c + 1) * P], bh[:, lpair, :], bl[:, lpair, :],
                                         lpair == 0, lpair == 15)
                    if part == 0:
                        last.then_inc(w_used, 1)
                last.then_inc(hid_done, 1)
                pe.wait_ge(hid_sb, got(hid_sb))
                for g in range(2):
                    for c in range(2):
                        last = pe.matmul(ps[0:N_CMP, 6, g * HD:(g + 1) * HD], hidT[:, c, g * N_CMP:(g + 1) * N_CMP],
                                         w2c[:, c * HD:(c + 1) * HD], start=c == 0, stop=c == 1)
                        if g == c == 0:
                            last.then_inc(w_used, 1)
                last.then_inc(cmp_out, 1)
                if name == "k":
                    pe.wait_ge(kc_normed, got(kc_normed))
                    for g in range(2):
                        last = pe.transpose(ps[0:HD, 7, g * 16:g * 16 + N_CMP], kc_n[:, g, :],
                                            ident[0:N_CMP, 0:N_CMP])
                    last.then_inc(kc_tr, 1)
                    pe.wait_ge(kc_sb, got(kc_sb))
            to_columns(H)
            linear("nsa_in")
            z = zrows(NSA_DIM)
            pe.wait_ge(heads_ready, got(heads_ready))
            for hb in range(4):
                for h in range(4):
                    for b in range(TB):
                        c = (4 * hb + h) * HD
                        last = pe.transpose(ps[0:HD, h // 2, (h % 2) * T + b * P:(h % 2) * T + (b + 1) * P],
                                            z[:, b, c:c + HD], ident)
                last.then_inc(heads_tr, 1)
                pe.wait_ge(heads_sb, got(heads_sb, 2))
                g = hb // 2
                for b in range(TB):
                    def q(h):
                        return nqT[0:HD, h * T + b * P:h * T + (b + 1) * P]
                    attend(attP2, attT2, q, lambda h: kcT[:, g, 0:N_CMP], lambda h, c: vcr[:, g, :], 4, N_CMP)
                    for kind in range(2):
                        attend(attP2, attT2, q, lambda h: kvT[:, 2 * kind + g, 0:(b + 1) * P],
                               lambda h, c: kv_v[:, c, kind * P + g * HD:kind * P + (g + 1) * HD], 4, (b + 1) * P)
            to_columns(mix)
            linear("nsa_out")
            conv_layer(1)

        @block.vector
        def _(dve):
            counts = Counts(dve)
            got, sent = counts.got, counts.sent
            n = [0]

            def split():
                k = n[0]
                if k < len(LEN):
                    dve.wait_ge(w_hi_ready, got(w_hi_ready))
                    dve.tensor_tensor(w_lo[:, k % 2, 0:LEN[k]], raw[:, k % RAW, 0:LEN[k]],
                                                w_hi[:, k % 2, 0:LEN[k]].bitcast(F32), ALU.subtract).then_inc(w_lo_ready, 1)
                n[0] += 1

            def step(ins):
                ins.then_inc(dve_step, 1)
                dve.wait_ge(dve_step, sent(dve_step))

            def tt(o, x, y, op):
                step(dve.tensor_tensor(o, x, y, op))

            def ts(o, x, s1, op0, s2=None, op1=None):
                if op1 is None:
                    step(dve.tensor_scalar(o, x, s1, None, op0))
                else:
                    step(dve.tensor_scalar(o, x, s1, s2, op0, op1))

            def stt(o, x, s, y, op0, op1):
                step(dve.scalar_tensor_tensor(o, x, s, y, op0, op1))

            def linear(name, evac):
                f = gi = done_slots = 0
                slots = SL[name]
                i = 0
                while i < len(slots):
                    nk, nf, _ = slots[i]
                    per = KC // nk
                    for _ in range(per):
                        split()
                    used(per)
                    evac(gi, 2 * (gi % 2), f, nf)
                    f += nf
                    i += per
                    gi += 1

            def used(k):
                dve.wait_ge(w_used, got(w_used, k))

            def to_columns():
                for k in range(4):
                    dve.wait_ge(xT_hi_ready, got(xT_hi_ready))
                    dve.tensor_tensor(xT_lo[:, 2 * k:2 * k + 2, :],
                                                ps[:, k, :].rearrange("p (k t) -> p k t", k=2),
                                                xT_hi[:, 2 * k:2 * k + 2, :].bitcast(F32), ALU.subtract).then_inc(xT_ready, 1)

            def inv_root(o, x, width):
                ts(o, x, 1.0 / width, ALU.mult, EPS, ALU.add)
                dve.reciprocal(o, o).then_inc(root_in, 1)
                dve.wait_ge(root_in, sent(root_in))
                dve.wait_ge(root_out, got(root_out))

            gains = [0]

            def norm(adaptive):
                dve.wait_ge(sumsq_ready, got(sumsq_ready, 2))
                gains[0] += 16
                dve.wait_ge(ld_gain, gains[0])
                inv_root(rstd, sumsq, D)
                scale = gain
                if adaptive:
                    stt(mod[:, 1, :], mod[:, 1, :], 1.0, gain, ALU.add, ALU.mult)
                    scale = mod[:, 1, :]
                for b in range(TB):
                    stt(H[:, b, :], X[:, b, :], rstd[:, b:b + 1], scale, ALU.mult, ALU.mult)
                    if adaptive:
                        tt(H[:, b, :], H[:, b, :], mod[:, 0, :], ALU.add)
                beat().then_inc(rows_ready, 1)
                dve.wait_ge(rows_ready, sent(rows_ready))
                to_columns()

            def into_rows(width):
                z = zrows(width)

                def evac(gi, bank, f, nf):
                    step(dve.tensor_copy(z[:, 0, f:f + nf], ps[:, bank, 0:nf]))
                    dve.tensor_copy(z[:, 1, f:f + nf], ps[:, bank + 1, 0:nf]).then_inc(lin_evac, 1)
                    dve.wait_ge(lin_evac, sent(lin_evac))
                return evac

            def into_residual(gate):
                def evac(gi, bank, f, nf):
                    for b in range(TB):
                        if gate:
                            tt(mix[:, b, f:f + nf], ps[:, bank + b, 0:nf], mod[:, 2, f:f + nf], ALU.mult)
                            tt(X[:, b, f:f + nf], X[:, b, f:f + nf], mix[:, b, f:f + nf], ALU.add)
                        else:
                            tt(X[:, b, f:f + nf], X[:, b, f:f + nf], ps[:, bank + b, 0:nf], ALU.add)
                    beat().then_inc(lin_evac, 1)
                    dve.wait_ge(lin_evac, sent(lin_evac))
                return evac

            mods = [0]

            def ada(name):
                beat().then_inc(cond_ready, 1)
                dve.wait_ge(cond_ready, sent(cond_ready))
                dve.wait_ge(cond_hi, got(cond_hi))
                cb = condT.unsqueeze(2).to_broadcast([P, KC, P])
                dve.tensor_tensor(xT_lo[:, 0:4, :].rearrange("p a (b m) -> p (a b) m", b=2), cb, xT_hi[:, 0:4, :].rearrange("p a (b m) -> p (a b) m", b=2).bitcast(F32), ALU.subtract).then_inc(cond_cols, 1)
                dve.wait_ge(cond_cols, sent(cond_cols))
                mods[0] += 16
                dve.wait_ge(ld_mod, mods[0])
                flat = arena[:, 0:3 * D]

                def evac(gi, bank, f, nf):
                    dve.tensor_tensor(flat[:, f:f + nf], flat[:, f:f + nf], ps[:, bank, 0:nf], ALU.add).then_inc(lin_evac, 1)
                    dve.wait_ge(lin_evac, sent(lin_evac))
                linear(name, evac)

            def beat():
                return dve.tensor_copy(tick[:, 1:2], tick[:, 0:1])

            def angles(pos, inv, width, s, c, rows_=P):
                c1 = 6.28125
                c2 = float(np.float32(np.round((2 * np.pi - c1) * 2 ** 20) / 2 ** 20))
                c3 = float(2 * np.pi - c1 - c2)
                magic = 1.5 * 2 ** 23
                ts(s, inv, pos, ALU.mult)
                ts(c, s, float(1 / (2 * np.pi)), ALU.mult, magic, ALU.add)
                ts(c, c, magic, ALU.subtract)
                for k in (c1, c2, c3):
                    stt(s, c, -k, s, ALU.mult, ALU.add)
                ts(s, s, 3.1415925, ALU.min, -3.1415925, ALU.max)
                stt(c, s, -1.0, s, ALU.mult, ALU.max)
                ts(c, c, -1.0, ALU.mult, float(np.pi / 2), ALU.add)

            def rope(x, nh, half, cos, sin, tmp, rows_=P):
                x1, x2 = x[:, :, 0:half], x[:, :, half:2 * half]
                cb = cos.unsqueeze(1).to_broadcast([rows_, nh, half])
                sb_ = sin.unsqueeze(1).to_broadcast([rows_, nh, half])
                t = [m[:, 0:nh * half].rearrange("p (h d) -> p h d", h=nh) for m in tmp]
                for o, x_, y in ((t[0], x1, cb), (t[1], x2, sb_), (t[2], x2, cb), (t[3], x1, sb_)):
                    dve.tensor_tensor(o, x_, y, ALU.mult).then_inc(dve_step, 1)
                dve.wait_ge(dve_step, sent(dve_step, 4))
                tt(x1, t[0], t[1], ALU.subtract)
                tt(x2, t[2], t[3], ALU.add)

            def attend(P_, nh, W, scale, mask, take, m01=None):
                nb = [P, nh, W]
                s = P_[:, 0:nh * 256].rearrange("p (h w) -> p h w", h=nh)[:, :, 0:W]
                dve.wait_ge(att_scores, got(att_scores))
                for h in range(nh):
                    ins = dve.scalar_tensor_tensor(s[:, h, :], ps[:, 4 + h // 2, (h % 2) * 256:(h % 2) * 256 + W],
                                                   scale, mask, ALU.mult, ALU.add)
                    ins.then_inc(dve_step, 1)
                dve.wait_ge(dve_step, sent(dve_step, nh))
                step(dve.tensor_reduce(negmax[:, 0:nh], s, AX.X, ALU.max))
                dve.tensor_tensor(s, s, negmax[:, 0:nh].unsqueeze(2).to_broadcast(nb), ALU.subtract).then_inc(att_centred, 1)
                dve.wait_ge(att_centred, sent(att_centred))
                dve.wait_ge(att_exp, got(att_exp))
                if m01 is not None:
                    tt(s, s, m01.unsqueeze(1).to_broadcast(nb), ALU.mult)
                dve.tensor_reduce(rowsum[:, 0:nh], s, AX.X, ALU.add).then_inc(att_probs, 1)
                dve.wait_ge(att_probs, sent(att_probs))
                ts(rowsum[:, 0:nh], rowsum[:, 0:nh], 1.0, ALU.max)
                step(dve.reciprocal(rinv[:, 0:nh], rowsum[:, 0:nh]))
                dve.wait_ge(att_out, got(att_out))
                take(ps[:, 3, 0:nh * HD].rearrange("p (h d) -> p h d", h=nh), rinv[:, 0:nh])

            def take_into(dst):
                def take(o, r):
                    nh = r.shape[1]
                    dve.tensor_tensor(dst.rearrange("p (h d) -> p h d", h=nh), o, r.unsqueeze(2).to_broadcast([P, nh, HD]), ALU.mult).then_inc(att_taken, 1)
                    dve.wait_ge(att_taken, sent(att_taken))
                return take

            def log_sigmoid(o, x, t, second=None):
                dve.scalar_tensor_tensor(t, x, -1.0, x, ALU.mult, ALU.max).then_inc(lf_abs, 1)
                dve.wait_ge(lf_abs, sent(lf_abs))
                dve.wait_ge(lf_exp, got(lf_exp))
                dve.tensor_scalar(t, t, 1.0, None, ALU.add).then_inc(lf_one, 1)
                dve.wait_ge(lf_one, sent(lf_one))
                dve.wait_ge(lf_ln, got(lf_ln))
                stt(o, x, 0.0, t, ALU.min, ALU.subtract)

            def group(nt, weight, conv=None):
                nsl = 2 if nt == NT else 1
                for _ in range(2 * nsl - 1):
                    split()
                split()
                for j in range(nt):
                    cols = slice(j * T, (j + 1) * T)
                    dve.wait_ge(up_done, got(up_done))
                    up = ps[:, j, T:2 * T]
                    if conv is not None:
                        for m, dst in ((0, cgate), (1, cval)):
                            w = [conv(m, k, j) for k in range(4)]
                            u = ps[:, j, m * T:(m + 1) * T]
                            d = dst[:, cols]
                            ts(d, u, w[2], ALU.mult, w[3], ALU.add)
                            stt(d[:, 1:T], u[:, 0:T - 1], w[1], d[:, 1:T], ALU.mult, ALU.add)
                            stt(d[:, 2:T], u[:, 0:T - 2], w[0], d[:, 2:T], ALU.mult, ALU.add)
                        beat().then_inc(conv_done, 1)
                        dve.wait_ge(conv_done, sent(conv_done))
                        up = cval[:, cols]
                    dve.wait_ge(silu_done, got(silu_done))
                    dve.tensor_tensor(act_f[:, cols], act_g[:, cols], up, ALU.mult).then_inc(act_prod, 1)
                    dve.wait_ge(act_hi, got(act_hi))
                    dve.tensor_tensor(aT_lo[:, j, :], act_f[:, cols], aT_hi[:, j, :].bitcast(F32),
                                                ALU.subtract).then_inc(act_ready, 1)
                for _ in range(nsl - 1):
                    split()
                split()
                used(3 * nsl)
                for b in range(TB):
                    for half in range(2):
                        y = ps[:, 4 + 2 * b + half, :]
                        o = acc[:, b, half * 512:(half + 1) * 512]
                        if weight is None:
                            tt(o, o, y, ALU.add)
                        else:
                            stt(o, y, weight(b), o, ALU.mult, ALU.add)
                beat().then_inc(y_free, 1)
                dve.wait_ge(y_free, sent(y_free))

            def dve_rates(conv):
                r = {w_hi_ready: 6, w_lo_ready: 6, w_used: 6, up_done: 4, silu_done: 4, act_prod: 4,
                     act_hi: 4, act_ready: 4, y_free: 1, dve_step: 4}
                if conv:
                    r[conv_done] = 4
                    r[dve_step] += 4 * 6
                return r

            def clear_acc():
                dve.memset(acc, 0.0).then_inc(y_free, 1)
                dve.wait_ge(y_free, sent(y_free))

            def dense(conv):
                clear_acc()
                with counts.loop(N_GROUPS, dve_rates(conv)) as g:
                    if conv:
                        def w(m, k, j):
                            return convT[:, bass.ds(g * NT + (k * 44 + m * 22 + j), 1)]
                        group(NT, None, w)
                    else:
                        group(NT, None)
                n[0] += 6 * (N_GROUPS - 1)
                if conv:
                    def w(m, k, j):
                        c = k * 44 + m * 22 + N_GROUPS * NT + j
                        return convT[:, c:c + 1]
                    group(NT // 2, None, w)
                else:
                    group(NT // 2, None)

            def add_gated():
                for b in range(TB):
                    tt(acc[:, b, :], acc[:, b, :], mod[:, 2, :], ALU.mult)
                for b in range(TB):
                    tt(X[:, b, :], X[:, b, :], acc[:, b, :], ALU.add)

            def head_norm(dst, src, nh, g, rows_=P, sq=None):
                x = src
                t = sq[0:rows_, 0:nh * HD].rearrange("p (h d) -> p h d", h=nh)
                tt(t, x, x, ALU.mult)
                step(dve.tensor_reduce(stat_a[0:rows_, 0:nh], t, AX.X, ALU.add))
                inv_root(stat_a[0:rows_, 0:nh], stat_a[0:rows_, 0:nh], HD)
                tt(dst, x, stat_a[0:rows_, 0:nh].unsqueeze(2).to_broadcast([rows_, nh, HD]), ALU.mult)
                tt(dst, dst, g[0:rows_, :].unsqueeze(1).to_broadcast([rows_, nh, HD]), ALU.mult)

            split()
            step(dve.memset(tick, 0.0))
            dve.wait_ge(ld_const, 16)
            dve.wait_ge(ld_first, 48)
            step(dve.tensor_copy(posf[:, 0:2], posi[:, 0:2]))
            for b in range(TB):
                angles(posf[:, b:b + 1], const[:, C_INV1:C_INV1 + 32], 32, sin1[:, b, :], cos1[:, b, :])
            beat().then_inc(angles_ready, 1)
            dve.wait_ge(angles_ready, sent(angles_ready))
            dve.wait_ge(sines, got(sines, 2))
            dve.wait_ge(cond_tr, got(cond_tr))
            step(dve.tensor_copy(condT, ps[:, 7, 0:KC]))
            dve.wait_ge(ld_x, 16)
            lp_loads = 0
            for l in range(2):
                ada(f"ada{l}0")
                beat().then_inc(x_ready, 1)
                dve.wait_ge(x_ready, sent(x_ready))
                norm(True)
                z = zrows(IN_DIM)
                linear(f"in{l}", into_rows(IN_DIM))
                for b in range(TB):
                    for c0, nh in ((AQ, 7), (IQ, 5)):
                        rope(z[:, b, c0:c0 + nh * HD].rearrange("p (h d) -> p h d", h=nh), nh, 32,
                             cos1[:, b, :], sin1[:, b, :], rope_t)
                dve.tensor_scalar(iw_half, z[:, :, IW:IW + IDX_HEADS], IDX_HEADS ** -0.5, None, ALU.mult).then_inc(heads_ready, 1)
                dve.wait_ge(heads_ready, sent(heads_ready))
                for b in range(TB):
                    W = (b + 1) * P
                    dve.wait_ge(idx_scores, got(idx_scores))
                    rel = idx_rel.rearrange("p (h w) -> p h w", h=4)
                    for k in range(2):
                        ts(rel[:, 2 * k:2 * k + 2, 0:W],
                           ps[:, 2 * b + k, :].rearrange("p (h w) -> p h w", h=2)[:, :, 0:W],
                           HD ** -0.5, ALU.mult, 0.0, ALU.max)
                    s = idx_acc[:, 0:W]
                    ts(s, rel[:, 0, 0:W], iw_half[:, b, 0:1], ALU.mult)
                    for h in range(1, IDX_HEADS):
                        stt(s, rel[:, h, 0:W], iw_half[:, b, h:h + 1], s, ALU.mult, ALU.add)
                    tt(s, s, const[:, C_M01 + AT[b]:C_M01 + AT[b] + W], ALU.mult)
                    tt(s, s, const[:, C_NEG + AT[b]:C_NEG + AT[b] + W], ALU.add)
                    for _ in range(TOPK // 8):
                        step(dve.max(top8, s))
                        step(dve.match_replace(s, top8, s, GONE))
                    ts(topw[:, 0:W], s, GONE / 2, ALU.is_gt, NEG, ALU.mult)
                    tt(dsa_mask[:, b, 0:W], topw[:, 0:W], const[:, C_NEG + AT[b]:C_NEG + AT[b] + W], ALU.add)
                for b in range(TB):
                    for hb in range(2):
                        attend(attP, 3, (b + 1) * P, HD ** -0.5, dsa_mask[:, b, 0:(b + 1) * P],
                               take_into(mix[:, b, 192 * hb:192 * hb + 192]))
                F = z[:, :, BF:BF + BD]
                if l:
                    beat().then_inc(lb_free, 1)
                    dve.wait_ge(lb_free, sent(lb_free))
                    dve.wait_ge(ld_lb, 16)
                    tt(h_t3[:, 0, :], lb_rows[:, 0, :], lb_rows[:, 1, :], ALU.max)
                    for k in range(2):
                        tt(lb_rows[:, k, :], lb_rows[:, k, :], h_t3[:, 0, :], ALU.subtract)
                    beat().then_inc(lb_diff, 1)
                    dve.wait_ge(lb_diff, sent(lb_diff))
                    dve.wait_ge(lb_exp, got(lb_exp))
                    dve.tensor_tensor(h_t1[:, 0, :], h_t2[:, 0, :], h_t2[:, 1, :], ALU.add).then_inc(lb_sum, 1)
                    dve.wait_ge(lb_sum, sent(lb_sum))
                    dve.wait_ge(lb_ln, got(lb_ln))
                    tt(h_lb[:, 0, :], lb_rows[:, 1, :], h_t1[:, 0, :], ALU.subtract)
                    tt(h_lb[:, 1, :], lb_rows[:, 0, :], h_t1[:, 0, :], ALU.subtract)
                log_sigmoid(h_LF, F, h_t1)
                if l:
                    lb = h_lb[:, 0:1, :].to_broadcast([P, TB, BD])
                    lcomp = h_lb[:, 1:2, :].to_broadcast([P, TB, BD])
                    tt(h_LF, h_LF, lcomp, ALU.add)
                    tt(h_t2, h_LF, lb, ALU.subtract)
                    tt(h_LF, h_LF, lb, ALU.max)
                    dve.scalar_tensor_tensor(h_t1, h_t2, -1.0, h_t2, ALU.mult, ALU.max).then_inc(lf_abs, 1)
                    dve.wait_ge(lf_abs, sent(lf_abs))
                    dve.wait_ge(lf_exp, got(lf_exp))
                    dve.tensor_scalar(h_t1, h_t1, 1.0, None, ALU.add).then_inc(lf_one, 1)
                    dve.wait_ge(lf_one, sent(lf_one))
                    dve.wait_ge(lf_ln, got(lf_ln))
                    tt(h_LF, h_LF, h_t1, ALU.add)
                    dve.wait_ge(lb_comp, got(lb_comp))
                dve.wait_ge(kk_sig, got(kk_sig))
                if l:
                    tt(h_kk, h_kk, h_t3[:, 0:1, :].to_broadcast([P, TB, BD]), ALU.mult)
                beat().then_inc(rec_rows, 1)
                dve.wait_ge(rec_rows, sent(rec_rows))
                got(heads_sb, 6)
                dve.wait_ge(heads_sb, got(heads_sb, 6))

                hs = mix[:, 0, BD:BD + 512]
                dve.wait_ge(level_prod, got(level_prod))
                for k in range(3):
                    tt(h_A[:, 512 * k:512 * k + 512].rearrange("p (n t) -> p n t", n=4),
                       ps[:, 3 + k, :].rearrange("p (n t) -> p n t", n=4),
                       ident.unsqueeze(1).to_broadcast([P, 4, P]), ALU.mult)
                for level in range(LEVELS + 1):
                    dve.wait_ge(decay, got(decay))
                    w = h_W[0:HD, :]
                    tt(h_QW[0:HD, :], h_qT[0:HD, :], w, ALU.mult)
                    dve.tensor_tensor(w, h_kT[0:HD, :], w, ALU.mult).then_inc(weighted, 1)
                    dve.wait_ge(weighted, sent(weighted))
                    dve.wait_ge(level_prod, got(level_prod))
                    if level < LEVELS:
                        m = const[:, C_LM + level * P:C_LM + (level + 1) * P]
                        for k in range(3):
                            t = hs.rearrange("p (n t) -> p n t", n=4)
                            tt(t, ps[:, 3 + k, :].rearrange("p (n t) -> p n t", n=4),
                               m.unsqueeze(1).to_broadcast([P, 4, P]), ALU.mult)
                            tt(h_A[:, 512 * k:512 * k + 512], h_A[:, 512 * k:512 * k + 512], hs, ALU.add)
                    else:
                        step(dve.tensor_copy(h_AX[:, 0:512], ps[:, 3, :]))
                        dve.tensor_copy(h_AX[:, 512:768], ps[:, 4, 0:256]).then_inc(rec_att, 1)
                        dve.wait_ge(rec_att, sent(rec_att))
                dve.wait_ge(o_out, got(o_out))
                for b in range(TB):
                    step(dve.tensor_copy(h_O[:, b, :], ps[:, 6 + b, 0:BD]))
                beat().then_inc(ws_free, 1)
                dve.wait_ge(ws_free, sent(ws_free))
                tt(h_sq, h_O, h_O, ALU.mult)
                step(dve.tensor_reduce(stat_a[:, 0:12], h_sq.rearrange("p b (h d) -> p (b h) d", d=HD), AX.X, ALU.add))
                inv_root(stat_a[:, 0:12], stat_a[:, 0:12], HD)
                o4 = h_O.rearrange("p b (h d) -> p (b h) d", d=HD)
                tt(o4, o4, stat_a[:, 0:12].unsqueeze(2).to_broadcast([P, 12, HD]), ALU.mult)
                lp_loads += 48
                dve.wait_ge(ld_lp, lp_loads)
                tt(o4, o4, onorm.unsqueeze(1).to_broadcast([P, 12, HD]), ALU.mult)
                dve.wait_ge(gate_silu, got(gate_silu))
                tt(mix[:, :, BD:2 * BD], h_O, h_sg, ALU.mult)
                dve.wait_ge(ld_ws, 32 * (l + 1))
                dve.tensor_tensor(ws, ws, const[:, C_M01:C_M01 + P].unsqueeze(1).to_broadcast([P, 4, P]), ALU.mult).then_inc(ws_masked, 1)
                dve.wait_ge(ws_masked, sent(ws_masked))
                dve.wait_ge(gelu_uv, got(gelu_uv))
                V = z[:, :, CU + C_DIM:CU + 2 * C_DIM]
                step(dve.tensor_reduce(stat_a[:, 0:2], V, AX.X, ALU.add))
                ts(stat_a[:, 0:2], stat_a[:, 0:2], 1.0 / C_DIM, ALU.mult)
                for b in range(TB):
                    ts(V[:, b, :], V[:, b, :], stat_a[:, b:b + 1], ALU.subtract)
                tt(g_t, V, V, ALU.mult)
                step(dve.tensor_reduce(stat_b[:, 0:2], g_t, AX.X, ALU.add))
                inv_root(stat_b[:, 0:2], stat_b[:, 0:2], C_DIM)
                for b in range(TB):
                    stt(V[:, b, :], V[:, b, :], stat_b[:, b:b + 1], vn_g, ALU.mult, ALU.mult)
                dve.tensor_tensor(V, V, vn_b.unsqueeze(1).to_broadcast([P, TB, C_DIM]), ALU.add).then_inc(v_normed, 1)
                dve.wait_ge(v_normed, sent(v_normed))
                dve.wait_ge(spatial, got(spatial))
                for b in range(TB):
                    tt(g_t[:, b, :].rearrange("p (g d) -> p g d", g=4),
                       ps[:, 2 + b, 0:C_DIM].rearrange("p (g d) -> p g d", g=4),
                       bsT.unsqueeze(2).to_broadcast([P, 4, HD]), ALU.add)
                dve.tensor_tensor(mix[:, :, 2 * BD:D], g_t, z[:, :, CU:CU + C_DIM], ALU.mult).then_inc(rows_ready, 1)
                dve.wait_ge(rows_ready, sent(rows_ready))
                beat().then_inc(lp_free, 1)
                dve.wait_ge(lp_free, sent(lp_free))
                beat().then_inc(gain_free, 1)
                dve.wait_ge(gain_free, sent(gain_free))
                to_columns()
                linear(f"out{l}", into_residual(True))
                beat().then_inc(mod_free, 1)
                dve.wait_ge(mod_free, sent(mod_free))
                ada(f"ada{l}1")
                beat().then_inc(x_ready, 1)
                dve.wait_ge(x_ready, sent(x_ready))
                norm(True)
                if l == 0:
                    dense(False)
                else:
                    dve.wait_ge(router_logits, got(router_logits))
                    step(dve.tensor_copy(logits.rearrange("p b e -> p (b e)"), ps[:, 4, 0:16]))
                    iota = const[:, C_IOTA:C_IOTA + 8]
                    for b in range(TB):
                        step(dve.max(top8, logits[:, b, :]))
                        step(dve.max_index(top_i, top8, logits[:, b, :]))
                        step(dve.tensor_copy(top_f, top_i))
                        dve.tensor_tensor(ew[:, 0:1], top8[:, 1:2], top8[:, 0:1], ALU.subtract).then_inc(gate_diff, 1)
                        dve.wait_ge(gate_diff, sent(gate_diff))
                        dve.wait_ge(gate_exp, got(gate_exp))
                        ts(ew[:, 2:3], ew[:, 1:2], 1.0, ALU.add)
                        step(dve.reciprocal(ew[:, 2:3], ew[:, 2:3]))
                        tt(ew[:, 3:4], ew[:, 1:2], ew[:, 2:3], ALU.mult)
                        ts(top8, iota, top_f[:, 0:1], ALU.is_equal, ew[:, 2:3], ALU.mult)
                        ts(gates[:, b, :], iota, top_f[:, 1:2], ALU.is_equal, ew[:, 3:4], ALU.mult)
                        tt(gates[:, b, :], gates[:, b, :], top8, ALU.add)
                    clear_acc()
                    groups = F_EXPERT // FG
                    rates = dve_rates(False)
                    with counts.loop(N_EXPERTS, {k: v * groups for k, v in rates.items()}) as e:
                        with counts.loop(groups, rates):
                            group(NT, lambda b: gates[:, b, bass.ds(e, 1)])
                    n[0] += 6 * (N_EXPERTS * groups - 1)
                add_gated()
                if l == 0:
                    beat().then_inc(mod_free, 1)
                    dve.wait_ge(mod_free, sent(mod_free))
                beat().then_inc(gain_free, 1)
                dve.wait_ge(gain_free, sent(gain_free))
            beat().then_inc(x_ready, 1)
            dve.wait_ge(x_ready, sent(x_ready))
            dve.wait_ge(sumsq_ready, got(sumsq_ready, 2))
            gains[0] += 16
            dve.wait_ge(ld_gain, gains[0])
            inv_root(rstd, sumsq, D)
            for b in range(TB):
                stt(X[:, b, :], X[:, b, :], rstd[:, b:b + 1], gain, ALU.mult, ALU.mult)
            beat().then_inc(gain_free, 1)
            dve.wait_ge(gain_free, sent(gain_free))
            lp_loads += 160
            dve.wait_ge(ld_lp, lp_loads)
            step(dve.tensor_copy(posf[:, 0:2], posi[:, 0:2]))
            step(dve.tensor_copy(posf[0:N_CMP, 2:3], posi[0:N_CMP, 2:3]))
            inv2 = const[:, C_INV2:C_INV2 + 8]
            for b in range(TB):
                angles(posf[:, b:b + 1], inv2, 8, sin2[:, b, :], cos2[:, b, :])
            angles(posf[0:N_CMP, 2:3], inv2[0:N_CMP, :], 8, sinc[0:N_CMP, :], cosc[0:N_CMP, :])
            beat().then_inc(angles_ready, 1)
            dve.wait_ge(angles_ready, sent(angles_ready))
            beat().then_inc(x_ready, 1)
            dve.wait_ge(x_ready, sent(x_ready))
            dve.wait_ge(sines, got(sines, 4))
            norm(False)
            linear("fa_in", into_rows(FA_DIM))
            z = zrows(FA_DIM)
            tt(fa_logf, z[:, :, 3 * D:FA_DIM], bf_b.unsqueeze(1).to_broadcast([P, TB, HEADS2]), ALU.add)
            lf_t = stat_b.rearrange("p (b h) -> p b h", b=2)
            log_sigmoid(fa_logf, fa_logf, lf_t)
            beat().then_inc(fa_logf_ready, 1)
            dve.wait_ge(fa_logf_ready, sent(fa_logf_ready))
            for src0, dst, g in ((0, qa, qg), (D, ka, kg)):
                for b in range(TB):
                    x = z[:, b, src0:src0 + D].rearrange("p (h d) -> p h d", h=HEADS2)
                    o = dst[:, b, :].rearrange("p (h d) -> p h d", h=HEADS2)[:, :, 0:HD]
                    head_norm(o, x, HEADS2, g, sq=fa_sq)
            dve.wait_ge(fa_cumsum, got(fa_cumsum))
            step(dve.tensor_copy(fa_c.rearrange("p b h -> p (b h)"), ps[:, 0, 0:32]))
            up8 = float(HD) ** 0.5
            for b in range(TB):
                q4 = qa[:, b, :].rearrange("p (h d) -> p h d", h=HEADS2)
                k4 = ka[:, b, :].rearrange("p (h d) -> p h d", h=HEADS2)
                c = fa_c[:, b, :].unsqueeze(2)
                step(dve.memset(q4[:, :, 64:65], up8))
                ts(q4[:, :, 65:66], c, up8, ALU.mult)
                ts(k4[:, :, 64:65], c, -1.0, ALU.mult)
                step(dve.memset(k4[:, :, 65:66], 1.0))
            beat().then_inc(heads_ready, 1)
            dve.wait_ge(heads_ready, sent(heads_ready))
            for hb in range(4):
                for b in range(TB):
                    attend(attP2, 4, (b + 1) * P, HD ** -0.5, const[:, C_NEG + AT[b]:C_NEG + AT[b] + (b + 1) * P],
                           take_into(mix[:, b, 256 * hb:256 * hb + 256]))
            beat().then_inc(rows_ready, 1)
            dve.wait_ge(rows_ready, sent(rows_ready))
            beat().then_inc(conv_free, 1)
            dve.wait_ge(conv_free, sent(conv_free))
            beat().then_inc(gain_free, 1)
            dve.wait_ge(gain_free, sent(gain_free))
            to_columns()
            linear("fa_out", into_residual(False))

            def conv_layer():
                beat().then_inc(x_ready, 1)
                dve.wait_ge(x_ready, sent(x_ready))
                norm(False)
                dense(True)
                for b in range(TB):
                    tt(X[:, b, :], X[:, b, :], acc[:, b, :], ALU.add)
                beat().then_inc(gain_free, 1)
                dve.wait_ge(gain_free, sent(gain_free))

            conv_layer()
            beat().then_inc(cmp_free, 1)
            dve.wait_ge(cmp_free, sent(cmp_free))
            beat().then_inc(x_ready, 1)
            dve.wait_ge(x_ready, sent(x_ready))
            norm(False)
            linear("kv", into_rows(KV_DIM))
            z = zrows(KV_DIM)
            for c0, g in ((256, ksg), (512, kwg)):
                for b in range(TB):
                    x = z[:, b, c0:c0 + P].rearrange("p (h d) -> p h d", h=2)
                    head_norm(x, x, 2, g, sq=kv_sq)
                    rope(x, 2, 8, cos2[:, b, :], sin2[:, b, :], krope)
            beat().then_inc(heads_ready, 1)
            dve.wait_ge(heads_ready, sent(heads_ready))
            for kind, c0 in enumerate((384, 640)):
                step(dve.tensor_copy(kv_v[:, :, kind * P:(kind + 1) * P], z[:, :, c0:c0 + P]))
            for i, name in enumerate("kv"):
                for g in range(2):
                    for s in range(2):
                        step(dve.tensor_copy(rawdup[:, :, g * P + s * HD:g * P + (s + 1) * HD],
                                           z[:, :, i * P + g * HD:i * P + (g + 1) * HD]))
                beat().then_inc(dup_ready, 1)
                dve.wait_ge(dup_ready, sent(dup_ready))
                dve.wait_ge(raw_sb, got(raw_sb, 2))
                for s in range(2):
                    part = slice(s * HD, (s + 1) * HD)
                    for g in range(2):
                        src = rawT[part, g * T:(g + 1) * T].rearrange("p (n l s) -> p s l n", l=8, s=2)[:, s, :, :]
                        for half in range(2):
                            o = blk32[part, 8 * half:8 * half + 8, g * N_CMP:(g + 1) * N_CMP]
                            tt(o, src[:, :, half:half + N_CMP],
                               peT[part, 8 * half:8 * half + 8].unsqueeze(2).to_broadcast([HD, 8, N_CMP]), ALU.add)
                beat().then_inc(blk_ready, 1)
                dve.wait_ge(blk_ready, sent(blk_ready))
                dve.wait_ge(blk_hi, got(blk_hi))
                bh, bl = (x[:, 0:2, :].rearrange("p a t -> p (a t)")[:, 0:480] for x in (xT_hi, xT_lo))
                dve.tensor_tensor(bl, blk32.rearrange("p l n -> p (l n)"), bh.bitcast(F32), ALU.subtract).then_inc(blk_lo, 1)
                dve.wait_ge(blk_lo, sent(blk_lo))
                split()
                split()
                used(2)
                dve.wait_ge(cmp_out, got(cmp_out))
                o6 = ps[0:N_CMP, 6, 0:P].rearrange("p (g d) -> p g d", g=2)
                if name == "k":
                    step(dve.tensor_copy(kc_n, o6))
                    head_norm(kc_n, kc_n, 2, kcg, N_CMP, kc_t.rearrange("p g d -> p (g d)"))
                    rope(kc_n, 2, 8, cosc[0:N_CMP, :], sinc[0:N_CMP, :], crope, N_CMP)
                    beat().then_inc(kc_normed, 1)
                    dve.wait_ge(kc_normed, sent(kc_normed))
                    dve.wait_ge(kc_sb, got(kc_sb))
                    beat().then_inc(cmp_free, 1)
                    dve.wait_ge(cmp_free, sent(cmp_free))
                else:
                    step(dve.tensor_copy(vcr, o6))
            beat().then_inc(gain_free, 1)
            dve.wait_ge(gain_free, sent(gain_free))
            beat().then_inc(x_ready, 1)
            dve.wait_ge(x_ready, sent(x_ready))
            norm(False)
            linear("nsa_in", into_rows(NSA_DIM))
            z = zrows(NSA_DIM)
            dve.tensor_tensor(z[:, :, D:NSA_DIM], z[:, :, D:NSA_DIM], bgate.unsqueeze(1).to_broadcast([P, TB, 3 * HEADS2]), ALU.add).then_inc(bgate_added, 1)
            dve.wait_ge(bgate_added, sent(bgate_added))
            for b in range(TB):
                x = z[:, b, 0:D].rearrange("p (h d) -> p h d", h=HEADS2)
                head_norm(x, x, HEADS2, nqg, sq=nq_sq)
                rope(x, HEADS2, 8, cos2[:, b, :], sin2[:, b, :], nrope)
            beat().then_inc(heads_ready, 1)
            dve.wait_ge(heads_ready, sent(heads_ready))
            dve.wait_ge(gates_sig, got(gates_sig))

            def take_gated(b, hb, kind):
                def take(o, r):
                    g0 = D + kind * HEADS2 + 4 * hb
                    tt(r, r, z[:, b, g0:g0 + 4], ALU.mult)
                    dst = mix[:, b, 256 * hb:256 * hb + 256].rearrange("p (h d) -> p h d", h=4)
                    rb = r.unsqueeze(2).to_broadcast([P, 4, HD])
                    if kind == 0:
                        dve.tensor_tensor(dst, o, rb, ALU.mult).then_inc(att_taken, 1)
                        dve.wait_ge(att_taken, sent(att_taken))
                    else:
                        t = nsa_tmp.rearrange("p (h d) -> p h d", h=4)
                        dve.tensor_tensor(t, o, rb, ALU.mult).then_inc(att_taken, 1)
                        dve.wait_ge(att_taken, sent(att_taken))
                        tt(dst, dst, t, ALU.add)
                return take

            for hb in range(4):
                for b in range(TB):
                    attend(attP2, 4, N_CMP, HD ** -0.5, const[:, C_CNEG + 16 * b:C_CNEG + 16 * b + N_CMP],
                           take_gated(b, hb, 0), const[:, C_CM01 + 16 * b:C_CM01 + 16 * b + N_CMP])
                    for kind in (1, 2):
                        attend(attP2, 4, (b + 1) * P, HD ** -0.5,
                               const[:, C_NEG + AT[b]:C_NEG + AT[b] + (b + 1) * P], take_gated(b, hb, kind))
            beat().then_inc(rows_ready, 1)
            dve.wait_ge(rows_ready, sent(rows_ready))
            beat().then_inc(conv_free, 1)
            dve.wait_ge(conv_free, sent(conv_free))
            beat().then_inc(gain_free, 1)
            dve.wait_ge(gain_free, sent(gain_free))
            to_columns()
            linear("nsa_out", into_residual(False))
            conv_layer()
            beat().then_inc(result, 1)
            dve.wait_ge(result, sent(result))


_INS = ["x", "c", "positions", "w_ada", "b_ada", "g_norm_mix", "g_norm_ffn", "w_in", "w_out", "hgrn_lb_logits",
        "hgrn_out_norm", "gmlp_vnorm_g", "gmlp_vnorm_b", "gmlp_w_s", "gmlp_b_s", "ffn_w_gate", "ffn_w_up",
        "ffn_w_down", "moe_w_router", "moe_w_gate", "moe_w_up", "moe_w_down", "g_final", "positions_2", "a_norm_2",
        "a_w_in_2", "a_b_f_2", "a_q_gain_2", "a_k_gain_2", "a_w_out_2", "kv_norm_2", "kv_w_2", "kc_pe_2", "vc_pe_2",
        "kc_w1_2", "kc_w2_2", "vc_w1_2", "vc_w2_2", "kc_gain_2", "ks_gain_2", "kw_gain_2", "b_norm_2", "b_w_in_2",
        "b_b_gate_2", "b_q_gain_2", "b_w_out_2", "f_norm_2", "f_w_up_2", "f_conv_w_2", "f_conv_b_2", "f_w_down_2"]


def kernel(**inputs):
    import concourse.bacc as _bacc
    from concourse.bass_utils import run_bass_kernel_spmd as _run

    nc = _bacc.Bacc("TRN2", target_bir_lowering=False, num_devices=1)
    arrays, args = {}, {}
    for name in _INS:
        v = np.ascontiguousarray(inputs[name])
        arrays[f"in_{name}"] = v
        args[name] = nc.dram_tensor(f"in_{name}", v.shape, mybir.dt.from_np(v.dtype), kind="ExternalInput").ap()
    arrays["shape_constants"] = constants()
    consts = nc.dram_tensor("shape_constants", (P, C_END), F32, kind="ExternalInput").ap()
    out = nc.dram_tensor("out", (1, T, D), F32, kind="ExternalOutput").ap()
    build(nc, args, consts, out)
    r = _run(nc, [arrays], core_ids=[0])
    return r.results[0]["out"]
```

```python
from contextlib import ExitStack, contextmanager

import numpy as np

import concourse.bass as bass
from concourse import mybir

F32 = mybir.dt.float32
F32R = mybir.dt.float32r
I32 = mybir.dt.int32
U32 = mybir.dt.uint32
ALU = mybir.AluOpType
ACT = mybir.ActivationFunctionType
AX = mybir.AxisListType

P = 128
D = 1024
KC = D // P
T = 256
TB = T // P
HD = 64
EPS = 1e-6
NEG = -1e30
GONE = -3e38
TOPK = 64
A_HEADS, IDX_HEADS = 6, 4
B_HEADS = 6
BD = B_HEADS * HD
C_DIM, C_GROUPS = 256, 4
IN_DIM = 2884
F_DENSE = 2816
N_EXPERTS, F_EXPERT = 8, 3584
HEADS2 = 16
FA_DIM = 3 * D + HEADS2
N_CMP = 15
KV_DIM = 768
NSA_DIM = D + 3 * HEADS2
MOE_SLOTS = 6 * N_EXPERTS * F_EXPERT // 512
FG = 512
NT = FG // P
RAW = 6
SLOT = 2048
LEVELS = 7

AQ, AK, AV, IQ, IK, IW, BQ, BF, BI, BG, CU = 0, 384, 448, 512, 768, 832, 836, 1220, 1604, 1988, 2372

C_ID = 0
C_M01 = C_ID + 128
C_NEG = C_M01 + 384
C_CM01 = C_NEG + 384
C_CNEG = C_CM01 + 32
C_INV1 = C_CNEG + 32
C_INV2 = C_INV1 + 32
C_IOTA = C_INV2 + 8
C_E = C_IOTA + P
C_LM = C_E + (LEVELS + 2) * P
C_END = C_LM + LEVELS * P
AT = [0, P]


def constants():
    c = np.zeros((P, C_END), np.float32)
    p = np.arange(P)[:, None]
    f = np.arange(P)[None, :]
    c[:, C_ID:C_ID + P] = p == f
    for b in range(TB):
        w = (b + 1) * P
        m = (np.arange(w)[None, :] <= p + b * P).astype(np.float32)
        c[:, C_M01 + AT[b]:C_M01 + AT[b] + w] = m
        c[:, C_NEG + AT[b]:C_NEG + AT[b] + w] = (1 - m) * NEG
        m = (np.arange(N_CMP)[None, :] * 16 + 31 <= p + b * P).astype(np.float32)
        c[:, C_CM01 + 16 * b:C_CM01 + 16 * b + N_CMP] = m
        c[:, C_CNEG + 16 * b:C_CNEG + 16 * b + N_CMP] = (1 - m) * NEG
    c[:, C_INV1:C_INV1 + 32] = np.float32(10000.0) ** (-np.arange(0, 64, 2, dtype=np.float32) / 64)
    c[:, C_INV2:C_INV2 + 8] = np.float32(500000.0) ** (-np.arange(8, dtype=np.float32) * np.float32(2.0 / 16))
    c[:, C_IOTA:C_IOTA + P] = np.arange(P)
    for level in range(LEVELS):
        m = 1 << level
        start = f // (2 * m) * (2 * m)
        ref = start + m - 1
        right = f - start >= m
        e = np.where(right, (p > ref) & (p <= f), (p > f) & (p <= ref))
        c[:, C_E + level * P:C_E + (level + 1) * P] = e
        same = p // (2 * m) == f // (2 * m)
        c[:, C_LM + level * P:C_LM + (level + 1) * P] = same & right & (p % (2 * m) < m)
    c[:, C_E + LEVELS * P:C_E + (LEVELS + 1) * P] = p > f
    c[:, C_E + (LEVELS + 1) * P:C_E + (LEVELS + 2) * P] = p <= f
    return c


class Counts:

    def __init__(self, eng):
        self.eng, self.waited, self.signalled, self.turns = eng, {}, {}, []

    def _value(self, count, sem):
        for i, rates in self.turns:
            if sem in rates:
                count = i * rates[sem] + count
        return count

    def got(self, sem, k=1):
        self.waited[sem] = self.waited.get(sem, 0) + k
        return self._value(self.waited[sem], sem)

    def sent(self, sem, k=1):
        self.signalled[sem] = self.signalled.get(sem, 0) + k
        return self._value(self.signalled[sem], sem)

    @contextmanager
    def loop(self, n, rates):
        before = (dict(self.waited), dict(self.signalled))
        with self.eng.Fori(0, n) as i:
            self.turns.append((i, rates))
            yield i
            self.turns.pop()
        for now, was in zip((self.waited, self.signalled), before):
            for sem, count in list(now.items()):
                one = count - was.get(sem, 0)
                assert one in (0, rates.get(sem, 0)), (sem.name, one, rates.get(sem, 0))
                now[sem] += one * (n - 1)


def build(nc, a, consts, out):
    with ExitStack() as ctx:
        def semaphore(name):
            return ctx.enter_context(nc.semaphore(name))

        chosen_places = semaphore("chosen_places")
        places = semaphore("places")
        overflow_known = semaphore("overflow_known")
        picked = semaphore("picked")
        gathered = semaphore("gathered")
        xg_hi_ready = semaphore("xg_hi_ready")
        xg_ready = semaphore("xg_ready")
        back_tr = semaphore("back_tr")
        back_sb = semaphore("back_sb")
        e_silu_done = semaphore("e_silu_done")
        e_act_rows = semaphore("e_act_rows")
        e_act_tr = semaphore("e_act_tr")
        e_act_hi = semaphore("e_act_hi")
        e_act_cols = semaphore("e_act_cols")
        e_out_sb = semaphore("e_out_sb")
        e_scattered = semaphore("e_scattered")
        e_taken = semaphore("e_taken")
        raw_full = [semaphore(f"raw_full{r}") for r in range(RAW)]
        w_lo_ready = semaphore("w_lo_ready")
        result = semaphore("result")
        gain_free = semaphore("gain_free")
        mod_free = semaphore("mod_free")
        lp_free = semaphore("lp_free")
        lb_free = semaphore("lb_free")
        ws_free = semaphore("ws_free")
        conv_free = semaphore("conv_free")
        cmp_free = semaphore("cmp_free")
        w_used = semaphore("w_used")
        w_hi_ready = semaphore("w_hi_ready")
        tr_psum = semaphore("tr_psum")
        xT_hi_ready = semaphore("xT_hi_ready")
        sumsq_ready = semaphore("sumsq_ready")
        root_in = semaphore("root_in")
        root_out = semaphore("root_out")
        x_ready = semaphore("x_ready")
        idx_taken = semaphore("idx_taken")
        att_centred = semaphore("att_centred")
        att_exp = semaphore("att_exp")
        att_tr = semaphore("att_tr")
        att_trcopied = semaphore("att_trcopied")
        heads_tr = semaphore("heads_tr")
        heads_sb = semaphore("heads_sb")
        conv_done = semaphore("conv_done")
        up_done = semaphore("up_done")
        silu_done = semaphore("silu_done")
        act_prod = semaphore("act_prod")
        act_hi = semaphore("act_hi")
        angles_ready = semaphore("angles_ready")
        sines = semaphore("sines")
        cond_silu = semaphore("cond_silu")
        cond_ready = semaphore("cond_ready")
        cond_hi = semaphore("cond_hi")
        lb_diff = semaphore("lb_diff")
        lb_exp = semaphore("lb_exp")
        lb_sum = semaphore("lb_sum")
        lb_ln = semaphore("lb_ln")
        lf_abs = semaphore("lf_abs")
        lf_exp = semaphore("lf_exp")
        lf_one = semaphore("lf_one")
        lf_ln = semaphore("lf_ln")
        lb_comp = semaphore("lb_comp")
        kk_sig = semaphore("kk_sig")
        decay_sum = semaphore("decay_sum")
        decay = semaphore("decay")
        o_out = semaphore("o_out")
        gate_silu = semaphore("gate_silu")
        gelu_uv = semaphore("gelu_uv")
        ws_tr = semaphore("ws_tr")
        ws_sb = semaphore("ws_sb")
        gate_diff = semaphore("gate_diff")
        gate_exp = semaphore("gate_exp")
        conv_tr = semaphore("conv_tr")
        conv_sb = semaphore("conv_sb")
        raw_tr = semaphore("raw_tr")
        raw_sb = semaphore("raw_sb")
        blk_ready = semaphore("blk_ready")
        blk_hi = semaphore("blk_hi")
        hid_done = semaphore("hid_done")
        hid_sb = semaphore("hid_sb")
        kc_tr = semaphore("kc_tr")
        kc_sb = semaphore("kc_sb")
        bgate_added = semaphore("bgate_added")
        gates_sig = semaphore("gates_sig")
        lin_evac = semaphore("lin_evac")
        rows_ready = semaphore("rows_ready")
        xT_ready = semaphore("xT_ready")
        att_scores = semaphore("att_scores")
        att_probs = semaphore("att_probs")
        att_out = semaphore("att_out")
        att_taken = semaphore("att_taken")
        y_free = semaphore("y_free")
        act_ready = semaphore("act_ready")
        cond_tr = semaphore("cond_tr")
        cond_cols = semaphore("cond_cols")
        heads_ready = semaphore("heads_ready")
        idx_scores = semaphore("idx_scores")
        rec_rows = semaphore("rec_rows")
        level_prod = semaphore("level_prod")
        weighted = semaphore("weighted")
        rec_att = semaphore("rec_att")
        ws_masked = semaphore("ws_masked")
        v_normed = semaphore("v_normed")
        spatial = semaphore("spatial")
        router_logits = semaphore("router_logits")
        fa_logf_ready = semaphore("fa_logf_ready")
        fa_cumsum = semaphore("fa_cumsum")
        dup_ready = semaphore("dup_ready")
        blk_lo = semaphore("blk_lo")
        cmp_out = semaphore("cmp_out")
        kc_normed = semaphore("kc_normed")
        dve_step = semaphore("dve_step")
        stored = semaphore("stored")
        ld_first = semaphore("ld_first")
        ld_const = semaphore("ld_const")
        ld_conv = semaphore("ld_conv")
        ld_cmp = semaphore("ld_cmp")
        ld_gain = semaphore("ld_gain")
        ld_mod = semaphore("ld_mod")
        ld_x = semaphore("ld_x")
        ld_lb = semaphore("ld_lb")
        ld_lp = semaphore("ld_lp")
        ld_ws = semaphore("ld_ws")

        def sb(name, shape, dt=F32):
            return ctx.enter_context(nc.sbuf_tensor(name, shape, dt))

        raw = sb("raw", [P, RAW, SLOT])
        w_hi = sb("w_hi", [P, 2, SLOT], F32R)
        w_lo = sb("w_lo", [P, 2, SLOT], F32R)
        xT_hi = sb("xT_hi", [P, KC, T], F32R)
        xT_lo = sb("xT_lo", [P, KC, T], F32R)
        aT_hi = sb("aT_hi", [P, NT, T], F32R)
        aT_lo = sb("aT_lo", [P, NT, T], F32R)
        X = sb("X", [P, TB, D])
        Zf = sb("Z", [P, TB * FA_DIM])
        mix = sb("mix", [P, TB, D])
        const = sb("const", [P, C_END])
        small = sb("small", [P, 592])
        lp = sb("lp", [P, 576])
        arena = sb("arena", [P, 11520])
        ps = ctx.enter_context(nc.psum_tensor("ps", [P, 8, 512], F32))

        ident = const[:, C_ID:C_ID + P]
        ones = const[:, C_M01 + P:C_M01 + 2 * P]

        def zrows(width):
            return Zf[:, 0:TB * width].rearrange("p (b n) -> p b n", b=TB)

        acc = Zf[:, 0:2048].rearrange("p (b n) -> p b n", b=TB)
        H = Zf[:, 2048:4096].rearrange("p (b n) -> p b n", b=TB)
        gain = Zf[:, 4096:5120]

        class Cut:

            def __init__(self, t, at=0):
                self.t, self.at = t, at

            def __call__(self, size_, rows=P, **dims):
                s = self.t[0:rows, self.at:self.at + size_]
                self.at += size_
                assert self.at <= self.t.shape[1], self.at
                if dims:
                    keys = list(dims)
                    s = s.rearrange(f"p ({' '.join(keys)} rest_) -> p {' '.join(keys)} rest_", **dims)
                return s

        sm = Cut(small)
        sumsq = sm(2)
        rstd = sm(2)
        stat_a = sm(32)
        stat_b = sm(32)
        rowmax, negmax, rowsum, rinv = (sm(8, i=2) for _ in range(4))
        cos1, sin1 = sm(64, b=2), sm(64, b=2)
        cos2, sin2 = sm(16, b=2), sm(16, b=2)
        cosc, sinc = sm(8), sm(8)
        posf = sm(3)
        tick = sm(2)
        posi = small[:, sm.at:sm.at + 3].bitcast(I32)
        sm.at += 3
        top8 = sm(8)
        top_i = small[:, sm.at:sm.at + 8].bitcast(U32)
        sm.at += 8
        top_f = sm(8)
        ew = sm(8)
        router = sm(64, c=8)
        logits = sm(16, b=2)
        gates = sm(16, b=2)
        chosen = sm(16, b=2)
        place = sm(16, b=2)
        overflow = small[:, sm.at:sm.at + 1].bitcast(I32)
        sm.at += 1
        most = sm(1)
        iw_half = sm(8, b=2)
        fa_logf = sm(32, b=2)
        fa_c = sm(32, b=2)
        bsT = sm(4)
        condT = sm(8)

        ar = Cut(arena)
        mod = ar(3 * D, m=3)
        a1 = ar.at
        attP = ar(1024)
        attT = ar(1024)
        rope_t = [ar(224) for _ in range(4)]
        headsT = ar(12 * T, n=12)
        idx_rel = ar(1024)
        idx_acc = ar(256)
        topw = ar(256)
        dsa_mask = ar(512, b=2)
        ar.at = a1
        h_qT, h_kT = ar(BD // HD * T), ar(BD // HD * T)
        h_W, h_QW = ar(1536), ar(1536)
        h_A = ar(1536)
        h_AX = ar(768)
        h_LF = Cut(arena)(768, b=2)
        h_t1 = Cut(arena, a1 + 3072)(768, b=2)
        h_t2 = Cut(arena, a1 + 3840)(768, b=2)
        h_kk = Cut(arena, a1 + 4608)(768, b=2)
        h_lb = Cut(arena, a1 + 6144)(768, b=2)
        h_t3 = Cut(arena, a1 + 5376)(768, b=2)
        h_O = Cut(arena, a1)(768, b=2)
        h_sq = Cut(arena, a1 + 768)(768, b=2)
        h_sg = Cut(arena, a1 + 1536)(768, b=2)
        ar.at = a1 + 3072
        ws = ar(512, g=4)
        wsT = ar(512, g=4)
        g_t = ar(512, b=2)
        bs_rows = ar(128, rows=4)
        ar.at = 0
        kvT = ar(4 * T, n=4, rows=HD)
        kv_v = ar(512, b=2)
        kcT = ar(32, rows=HD, g=2)
        vcr = ar(128, rows=N_CMP, g=2)
        b2 = ar.at
        attP2 = ar(1024)
        attT2 = ar(1024)
        qa, ka = ar(TB * HEADS2 * 66, b=2), ar(TB * HEADS2 * 66, b=2)
        qTb, kTb = ar(1024), ar(1024)
        fa_sq = ar(1024)
        ar.at = b2 + 2048
        nsa_tmp = ar(256)
        nq_sq = ar(1024)
        nrope = [ar(256) for _ in range(4)]
        nqT = ar(1024)
        ar.at = b2
        convT = ar(44 * 4)
        conv_rows = ar(512, j=4)
        cgate = ar(1024)
        cval = ar(1024)
        ar.at = b2
        rawdup = ar(512, b=2)
        rawT = ar(512)
        pe_rows = ar(128, rows=16)
        peT = ar(16)
        blk32 = ar(480, l=16)
        hidT = ar(60, c=2)
        w2c = ar(256)
        kc_n = ar(128, rows=N_CMP, g=2)
        kc_t = ar(128, rows=N_CMP, g=2)
        kv_sq = ar(512)
        crope = [ar(16, rows=N_CMP) for _ in range(4)]
        krope = [ar(32) for _ in range(4)]
        att_bufs, fa_bufs, nsa_bufs = (attP, idx_rel), (attP2, fa_sq), (attP2, nq_sq)
        ar.at = a1
        act_g = ar(1024)
        act_f = ar(1024)
        conv_end = b2 + 176 + 512 + 2048
        if conv_end > a1:
            act_g = Cut(arena, conv_end)(1024)
            act_f = Cut(arena, conv_end + 1024)(1024)
        em = Cut(arena, conv_end)
        e_gate, e_act = em(512), em(512)
        e_out = em(D)
        pick = em(256, b=2)
        back = em(256, b=2)
        backT = em(256)
        cond_rows = Cut(arena, 8192)(128, rows=KC)
        lb_rows = Cut(arena, a1 + 6912)(768, b=2)

        onorm, vn_g, vn_b = lp[:, 0:64], lp[:, 64:320], lp[:, 320:576]
        qg, kg = lp[:, 0:64], lp[:, 64:128]
        bf_b = lp[:, 128:144]
        ksg, kwg, kcg = lp[:, 144:208], lp[:, 208:272], lp[:, 272:336]
        bgate = lp[:, 336:384]
        nqg = lp[:, 384:448]

        plan = []

        def rows(w, c0, nk, f0, nf):
            return w[c0 * P:(c0 + nk) * P, f0:f0 + nf].rearrange("(k p) f -> p k f", p=P)

        def linear_slots(w, n):
            got = []
            for f0 in range(0, n, FG):
                nf = min(FG, n - f0)
                nk = KC if nf <= FG // 2 else KC // 2
                got += [(nk, nf, rows(w, c, nk, f0, nf)) for c in range(0, KC, nk)]
            return got

        block = ctx.enter_context(nc.Block())

        def linears():
            s = {}
            for l in range(2):
                for half in range(2):
                    s[f"ada{l}{half}"] = linear_slots(a["w_ada"][l, :, half * 3 * D:(half + 1) * 3 * D], 3 * D)
                s[f"in{l}"] = linear_slots(a["w_in"][l], IN_DIM)
                s[f"out{l}"] = linear_slots(a["w_out"][l], D)
            s["fa_in"] = linear_slots(a["a_w_in_2"][0], FA_DIM)
            s["fa_out"] = linear_slots(a["a_w_out_2"][0], D)
            s["kv"] = linear_slots(a["kv_w_2"], KV_DIM)
            for n in "kv":
                w = a[f"{n}c_w1_2"]
                s[f"{n}c"] = [(8, 256, rows(w, 0, 8, 0, 256)), (8, 256, rows(w, 8, 8, 0, 256))]
            s["nsa_in"] = linear_slots(a["b_w_in_2"][0], NSA_DIM)
            s["nsa_out"] = linear_slots(a["b_w_out_2"][0], D)
            return s

        SL = linears()
        N_GROUPS = F_DENSE // FG

        ORDER = ["ada00", "in0", "out0", "ada01", "ffn0", "ada10", "in1", "out1", "ada11", "moe",
                 "fa_in", "fa_out", "conv0", "kv", "kc", "vc", "nsa_in", "nsa_out", "conv1"]

        def slot_lengths():
            for name in ORDER:
                if name in SL:
                    yield from [nk * nf for nk, nf, _ in SL[name]]
                elif name == "moe":
                    yield from [SLOT] * (2 * MOE_SLOTS)
                else:
                    yield from [SLOT] * (6 * N_GROUPS + 3)

        LEN = list(slot_lengths())
        E_GROUPS = F_EXPERT // FG
        MOE_END = sum(len(SL[name]) for name in ORDER[:9] if name in SL) + 6 * N_GROUPS + 3 + MOE_SLOTS

        @block.sync
        def _(sp):
            counts = Counts(sp)
            got, sent = counts.got, counts.sent
            n = 0

            def load(src, nk, nf, loop=None):
                nonlocal n
                r = n % RAW
                if n >= RAW:
                    sp.wait_ge(w_lo_ready, got(w_lo_ready))
                dst = raw[:, r, 0:nk * nf].rearrange("p (k f) -> p k f", k=nk)
                sp.dma_start(dst, src).then_inc(raw_full[r], 16)
                n += 1

            def ffn_group(wg, wu, wd, f0, nf, r0):
                if nf == FG:
                    for w in (wg, wu):
                        for c in (0, 4):
                            load(w[c * P:(c + 4) * P, bass.ds(f0, nf)].rearrange("(k p) f -> p k f", p=P), 4, nf)
                    for c in (0, 2):
                        load(wd[bass.ds(r0 + c * P, 2 * P), :].rearrange("(k p) f -> p k f", p=P), 2, D)
                else:
                    for w in (wg, wu):
                        load(rows(w, 0, KC, f0, nf), KC, nf)
                    load(wd[r0:r0 + 2 * P, :].rearrange("(k p) f -> p k f", p=P), 2, D)

            def dense(wg, wu, wd):
                nonlocal n
                with counts.loop(N_GROUPS, {w_lo_ready: 6}) as g:
                    ffn_group(wg, wu, wd, g * FG, FG, g * FG)
                n += 6 * (N_GROUPS - 1)
                ffn_group(wg, wu, wd, N_GROUPS * FG, FG // 2, N_GROUPS * FG)

            def experts():
                nonlocal n
                wg = a["moe_w_gate"][0].rearrange("e d f -> (e d) f")
                wu = a["moe_w_up"][0].rearrange("e d f -> (e d) f")
                wd = a["moe_w_down"][0].rearrange("e f d -> (e f) d")

                def into(w, e, g):
                    for c in (0, 4):
                        src = w[bass.ds(e * D + c * P, 4 * P), bass.ds(g * FG, FG)]
                        load(src.rearrange("(k p) f -> p k f", p=P), 4, FG)

                def down(e, g):
                    for c in (0, 2):
                        src = wd[bass.ds(e * F_EXPERT + g * FG + c * P, 2 * P), :]
                        load(src.rearrange("(k p) f -> p k f", p=P), 2, D)

                with counts.loop(N_EXPERTS, {w_lo_ready: 6 * E_GROUPS}) as e:
                    into(wg, e, 0)
                    into(wu, e, 0)
                    with counts.loop(E_GROUPS - 1, {w_lo_ready: 6}) as g:
                        into(wg, e, g + 1)
                        down(e, g)
                        into(wu, e, g + 1)
                    n += 6 * (E_GROUPS - 2)
                    down(e, E_GROUPS - 1)
                n += 6 * E_GROUPS * (N_EXPERTS - 1)

            for name in ORDER:
                if name in SL:
                    for nk, nf, src in SL[name]:
                        load(src, nk, nf)
                elif name == "ffn0":
                    dense(a["ffn_w_gate"][0], a["ffn_w_up"][0], a["ffn_w_down"][0])
                elif name == "moe":
                    experts()
                    sp.wait_ge(overflow_known, 1)
                    more_than_128 = sp.value_load(overflow[0:1, 0:1], min_val=0, max_val=1)
                    with sp.If(more_than_128 > 0):
                        experts()
                    with sp.Else():
                        for sem in raw_full:
                            total = 16 * ((MOE_END - 1 - raw_full.index(sem)) // RAW + 1)
                            sp.wait_ge(sem, total)
                            sp.sem_inc(sem, 16 * MOE_SLOTS // RAW)
                            sp.wait_ge(sem, total + 16 * MOE_SLOTS // RAW)
                else:
                    l = int(name[-1])
                    w = a["f_w_up_2"][l]
                    dense(w[:, 0:F_DENSE], w[:, F_DENSE:2 * F_DENSE], a["f_w_down_2"][l])
            assert n == len(LEN)
            sp.wait_ge(result, got(result))
            sp.dma_start(out[0].rearrange("(b p) n -> p b n", p=P), X[:, :, :]).then_inc(stored, 16)
            sp.wait_ge(stored, 16)

        @block.gpsimd
        def _(pool):
            counts = Counts(pool)
            got, sent = counts.got, counts.sent

            def load(dst, src, sem, **how):
                pool.dma_start(dst, src, **how).then_inc(sem, 16)

            load(const[:, :], consts, ld_const)
            load(X[:, :, :], a["x"][0].rearrange("(b p) n -> p b n", p=P), ld_x)
            load(cond_rows, a["c"][0].rearrange("(k p) -> k p", p=P), ld_first)
            load(posi[:, 0:2], a["positions"][0].rearrange("(b p) -> p b", p=P), ld_first,
                 allow_slow_non_contiguous=True)
            load(router, a["moe_w_router"][0].rearrange("(c p) e -> p c e", p=P), ld_first)

            def gain_row(src):
                pool.wait_ge(gain_free, got(gain_free))
                load(gain, src.partition_broadcast(P), ld_gain)

            def ada_bias(l, half):
                if (l, half) != (0, 0):
                    pool.wait_ge(mod_free, got(mod_free))
                load(arena[:, 0:3 * D], a["b_ada"][l, half * 3 * D:(half + 1) * 3 * D].partition_broadcast(P),
                     ld_mod)

            for l in range(2):
                ada_bias(l, 0)
                if l == 0:
                    load(gain, a["g_norm_mix"][l].partition_broadcast(P), ld_gain)
                else:
                    gain_row(a["g_norm_mix"][l])
                if l:
                    pool.wait_ge(lp_free, got(lp_free))
                load(onorm, a["hgrn_out_norm"][l].partition_broadcast(P), ld_lp)
                load(vn_g, a["gmlp_vnorm_g"][l].partition_broadcast(P), ld_lp)
                load(vn_b, a["gmlp_vnorm_b"][l].partition_broadcast(P), ld_lp)
                if l:
                    pool.wait_ge(lb_free, got(lb_free))
                    load(lb_rows, a["hgrn_lb_logits"].partition_broadcast(P), ld_lb)
                pool.wait_ge(ws_free, got(ws_free))
                load(ws, a["gmlp_w_s"][l].rearrange("g t s -> t g s"), ld_ws)
                load(bs_rows, a["gmlp_b_s"][l], ld_ws)
                ada_bias(l, 1)
                gain_row(a["g_norm_ffn"][l])
            gain_row(a["g_final"])
            pool.wait_ge(lp_free, got(lp_free))
            for dst, name in ((qg, "a_q_gain_2"), (kg, "a_k_gain_2"), (bf_b, "a_b_f_2")):
                load(dst, a[name][0].partition_broadcast(P), ld_lp)
            for dst, name in ((ksg, "ks_gain_2"), (kwg, "kw_gain_2"), (kcg, "kc_gain_2")):
                load(dst, a[name].partition_broadcast(P), ld_lp)
            load(bgate, a["b_b_gate_2"][0].partition_broadcast(P), ld_lp)
            load(nqg, a["b_q_gain_2"][0].partition_broadcast(P), ld_lp)
            load(posi[:, 0:2], a["positions_2"][0].rearrange("(b p) -> p b", p=P), ld_lp,
                 allow_slow_non_contiguous=True)
            ends = a["positions_2"][0].rearrange("(n s) -> n s", s=16)[1:1 + N_CMP, 15:16]
            load(posi[0:N_CMP, 2:3], ends, ld_lp, allow_slow_non_contiguous=True)
            gain_row(a["a_norm_2"][0])

            def conv_params(l):
                pool.wait_ge(conv_free, got(conv_free))
                load(conv_rows[0:44, 0:3, :], a["f_conv_w_2"][l].rearrange("j (t p) -> t j p", p=P), ld_conv)
                load(conv_rows[0:44, 3, :], a["f_conv_b_2"][l].rearrange("(t p) -> t p", p=P), ld_conv)
                gain_row(a["f_norm_2"][l])

            conv_params(0)
            gain_row(a["kv_norm_2"])
            for n in "kv":
                pool.wait_ge(cmp_free, got(cmp_free))
                load(pe_rows, a[f"{n}c_pe_2"].rearrange("(l s) d -> l (s d)", s=2), ld_cmp)
                load(w2c[:, 0:128].rearrange("p (c n) -> p c n", c=2),
                     a[f"{n}c_w2_2"].rearrange("(c p) n -> p c n", p=P), ld_cmp)
            gain_row(a["b_norm_2"][0])
            conv_params(1)

        @block.scalar
        def _(act):
            counts = Counts(act)
            got, sent = counts.got, counts.sent
            n = [0]
            free = [2]

            def split():
                k = n[0]
                if k < len(LEN):
                    r = k % RAW
                    act.wait_ge(raw_full[r], got(raw_full[r], 16))
                    if free[0]:
                        free[0] -= 1
                    else:
                        act.wait_ge(w_used, got(w_used))
                    act.activation(w_hi[:, k % 2, 0:LEN[k]], raw[:, r, 0:LEN[k]], ACT.Copy).then_inc(w_hi_ready, 1)
                n[0] += 1

            landed = {sem: 16 for sem in raw_full}

            def more(turns, per):
                n[0] += per * (turns - 1)

            def linear(name, ahead=True):
                for _ in SL[name][0 if ahead else 1:]:
                    split()

            def experts():
                rates = {**landed, w_hi_ready: 6, w_used: 6, e_silu_done: 1, e_act_tr: 1, e_act_hi: 1}
                whole = {k: v * E_GROUPS for k, v in rates.items()}
                whole.update({gathered: 1, xg_hi_ready: 2, back_tr: 1, back_sb: 1, e_out_sb: 1})

                def silu():
                    act.activation(e_gate, ps[:, 0, :], ACT.Silu).then_inc(e_silu_done, 1)

                def act_high():
                    act.wait_ge(e_act_tr, got(e_act_tr))
                    act.activation(aT_hi[:, :, 0:P], ps[:, 2, :].rearrange("p (j t) -> p j t", j=NT),
                                   ACT.Copy).then_inc(e_act_hi, 1)

                with counts.loop(N_EXPERTS, whole):
                    split()
                    split()
                    act.wait_ge(gathered, got(gathered))
                    for k in range(2):
                        act.activation(xT_hi[:, 4 * k:4 * k + 4, 0:P], ps[:, 6 + k, :].rearrange("p (c t) -> p c t", c=4),
                                       ACT.Copy).then_inc(xg_hi_ready, 1)
                    act.wait_ge(back_tr, got(back_tr))
                    act.activation(backT, ps[:, 3, 0:T], ACT.Copy).then_inc(back_sb, 1)
                    split()
                    split()
                    silu()
                    split()
                    with counts.loop(E_GROUPS - 1, rates):
                        split()
                        split()
                        act_high()
                        split()
                        silu()
                        split()
                        split()
                        split()
                    n[0] += 6 * (E_GROUPS - 2)
                    split()
                    act_high()
                    act.wait_ge(w_used, got(w_used, 2))
                    free[0] = 2
                    act.activation(e_out.rearrange("p (k n) -> p k n", k=2), ps[:, 4:6, :], ACT.Copy).then_inc(e_out_sb, 1)
                n[0] += 6 * E_GROUPS * (N_EXPERTS - 1)

            def to_columns():
                for k in range(4):
                    act.wait_ge(tr_psum, got(tr_psum))
                    act.activation(xT_hi[:, 2 * k:2 * k + 2, :],
                                             ps[:, k, :].rearrange("p (k t) -> p k t", k=2), ACT.Copy).then_inc(xT_hi_ready, 1)

            def square_sums(src):
                for b in range(TB):
                    act.activation(H[:, b, :], src[:, b, :], ACT.Square, accum_out=sumsq[:, b:b + 1]).then_inc(sumsq_ready, 1)

            def root(x, times=1):
                for _ in range(times):
                    act.wait_ge(root_in, got(root_in))
                    act.activation(x, x, ACT.Sqrt).then_inc(root_out, 1)

            def norm():
                act.wait_ge(x_ready, got(x_ready))
                square_sums(X)
                root(rstd)
                to_columns()

            def attend(bufs, T_, sizes):

                def exps(i):
                    nh, W = sizes[i]
                    act.wait_ge(att_centred, got(att_centred))
                    for h in range(nh):
                        s = bufs[i % 2][:, h * 256:h * 256 + W]
                        last = act.activation(s, s, ACT.Exp, bias=negmax[:, i % 2, h:h + 1],
                                              accum_out=rowsum[:, i % 2, h:h + 1])
                    last.then_inc(att_exp, 1)

                exps(0)
                for i, (nh, W) in enumerate(sizes):
                    if i + 1 < len(sizes):
                        exps(i + 1)
                    kw = min(W, P)
                    n_cols = nh * ((W + P - 1) // P) * P
                    act.wait_ge(att_tr, got(att_tr))
                    for k in range((n_cols + 511) // 512):
                        w = min(512, n_cols - 512 * k)
                        last = act.activation(T_[0:kw, 512 * k:512 * k + w], ps[0:kw, 6 + k, 0:w], ACT.Copy)
                    last.then_inc(att_trcopied, 1)

            def copy_heads(dst, banks, rows_):
                act.wait_ge(heads_tr, got(heads_tr))
                for k, (bank, w) in enumerate(banks):
                    act.activation(dst[0:rows_, 512 * k:512 * k + w], ps[0:rows_, bank, 0:w], ACT.Copy).then_inc(heads_sb, 1)

            def dense(conv):
                with counts.loop(N_GROUPS, {**landed, w_hi_ready: 6, w_used: 6, up_done: 4, silu_done: 4,
                                          act_prod: 4, act_hi: 4, conv_done: 4}):
                    group(NT, conv)
                more(N_GROUPS, 6)
                group(NT // 2, conv)

            def group(nt, conv=False):
                nsl = 2 if nt == NT else 1
                for _ in range(2 * nsl):
                    split()
                for j in range(nt):
                    if conv:
                        act.wait_ge(conv_done, got(conv_done))
                        g = cgate[:, j * T:(j + 1) * T]
                    else:
                        act.wait_ge(up_done, got(up_done))
                        g = ps[:, j, 0:T]
                    act.activation(act_g[:, j * T:(j + 1) * T], g, ACT.Silu).then_inc(silu_done, 1)
                    act.wait_ge(act_prod, got(act_prod))
                    act.activation(aT_hi[:, j, :], act_f[:, j * T:(j + 1) * T], ACT.Copy).then_inc(act_hi, 1)
                for _ in range(nsl):
                    split()

            split()
            def rotary_sines():
                act.wait_ge(angles_ready, got(angles_ready))
                act.activation(sin1[:, :, :], sin1[:, :, :], ACT.Sin).then_inc(sines, 1)
                act.activation(cos1[:, :, :], cos1[:, :, :], ACT.Sin).then_inc(sines, 1)

            act.wait_ge(ld_first, 48)
            act.activation(cond_rows, cond_rows, ACT.Silu).then_inc(cond_silu, 1)
            rotary_sines()

            def cond_columns():
                act.wait_ge(cond_ready, got(cond_ready))
                act.activation(xT_hi[:, 0:4, :].rearrange("p a (b m) -> p (a b) m", b=2),
                                         condT.unsqueeze(2).to_broadcast([P, KC, P]), ACT.Copy).then_inc(cond_hi, 1)

            for l in range(2):
                cond_columns()
                linear(f"ada{l}0")
                norm()
                linear(f"in{l}")
                copy_heads(headsT.rearrange("p n t -> p (n t)"), [(k, 512) for k in range(6)], HD)
                attend(att_bufs, attT, [(3, (b + 1) * P) for b in range(TB) for _ in range(2)])
                if l:
                    act.wait_ge(lb_diff, got(lb_diff))
                    act.activation(h_t2[:, :, :], lb_rows, ACT.Exp).then_inc(lb_exp, 1)
                    act.wait_ge(lb_sum, got(lb_sum))
                    act.activation(h_t1[:, 0, :], h_t1[:, 0, :], ACT.Ln).then_inc(lb_ln, 1)
                act.wait_ge(lf_abs, got(lf_abs))
                act.activation(h_t1, h_t1, ACT.Exp, scale=-1.0).then_inc(lf_exp, 1)
                act.wait_ge(lf_exp, sent(lf_exp))
                act.wait_ge(lf_one, got(lf_one))
                act.activation(h_t1, h_t1, ACT.Ln).then_inc(lf_ln, 1)
                if l:
                    act.wait_ge(lf_abs, got(lf_abs))
                    act.activation(h_t1, h_t1, ACT.Exp, scale=-1.0).then_inc(lf_exp, 1)
                    act.wait_ge(lf_exp, sent(lf_exp))
                    act.wait_ge(lf_one, got(lf_one))
                    act.activation(h_t1, h_t1, ACT.Ln).then_inc(lf_ln, 1)
                    act.activation(h_t3[:, 0, :], h_lb[:, 1, :], ACT.Exp).then_inc(lb_comp, 1)
                    act.wait_ge(lb_comp, sent(lb_comp))
                z = zrows(IN_DIM)
                act.activation(h_kk, z[:, :, BF:BF + BD], ACT.Sigmoid, scale=-1.0).then_inc(kk_sig, 1)
                act.wait_ge(heads_tr, got(heads_tr))
                for k in range(6):
                    dst = (h_qT if k < 3 else h_kT)[0:HD, 512 * (k % 3):512 * (k % 3) + 512]
                    act.activation(dst, ps[0:HD, k, :], ACT.Copy).then_inc(heads_sb, 1)
                for level in range(LEVELS + 1):
                    act.wait_ge(decay_sum, got(decay_sum))
                    act.activation(h_W[0:HD, :].rearrange("p (a n) -> p a n", a=3), ps[0:HD, 0:3, :],
                                             ACT.Exp).then_inc(decay, 1)
                act.wait_ge(o_out, got(o_out))
                act.activation(h_sg, z[:, :, BG:BG + BD], ACT.Silu).then_inc(gate_silu, 1)
                act.activation(z[:, :, CU:CU + 2 * C_DIM], z[:, :, CU:CU + 2 * C_DIM], ACT.Gelu).then_inc(gelu_uv, 1)
                act.wait_ge(gelu_uv, sent(gelu_uv))
                root(stat_a[:, 0:12])
                act.wait_ge(ws_tr, got(ws_tr))
                act.activation(wsT.rearrange("p g n -> p (g n)"), ps[:, 0, :], ACT.Copy).then_inc(ws_sb, 1)
                act.activation(bsT, ps[:, 1, 0:4], ACT.Copy).then_inc(ws_sb, 1)
                root(stat_b[:, 0:2])
                to_columns()
                linear(f"out{l}")
                cond_columns()
                linear(f"ada{l}1", ahead=l == 0)
                norm()
                if l == 0:
                    dense(False)
                else:
                    for b in range(TB):
                        act.wait_ge(gate_diff, got(gate_diff))
                        act.activation(ew[:, 1:2], ew[:, 0:1], ACT.Exp).then_inc(gate_exp, 1)
                    act.wait_ge(w_used, got(w_used, 2))
                    free[0] = 2
                    experts()
                    act.wait_ge(overflow_known, 1)
                    more_than_128 = act.value_load(overflow[0:1, 0:1], min_val=0, max_val=1)
                    with act.If(more_than_128 > 0):
                        experts()
                    with act.Else():
                        act.wait_ge(w_hi_ready, MOE_END)
                        act.sem_inc(w_hi_ready, MOE_SLOTS)
                        act.wait_ge(w_hi_ready, MOE_END + MOE_SLOTS)
                    split()
            act.wait_ge(x_ready, got(x_ready))
            square_sums(X)
            root(rstd)
            act.wait_ge(angles_ready, got(angles_ready))
            for s in (sin2, cos2):
                act.activation(s, s, ACT.Sin).then_inc(sines, 1)
            for s in (sinc, cosc):
                act.activation(s[0:N_CMP, :], s[0:N_CMP, :], ACT.Sin).then_inc(sines, 1)
            norm()
            linear("fa_in")
            act.wait_ge(lf_abs, got(lf_abs))
            act.activation(stat_b, stat_b, ACT.Exp, scale=-1.0).then_inc(lf_exp, 1)
            act.wait_ge(lf_exp, sent(lf_exp))
            act.wait_ge(lf_one, got(lf_one))
            act.activation(stat_b, stat_b, ACT.Ln).then_inc(lf_ln, 1)
            root(stat_a[:, 0:16], 4)
            for hb in range(4):
                act.wait_ge(heads_tr, got(heads_tr))
                for dst, bank in ((qTb, 0), (kTb, 4)):
                    for k in range(2):
                        act.activation(dst[0:66, 512 * k:512 * k + 512], ps[0:66, bank + k, :], ACT.Copy).then_inc(heads_sb, 1)
                attend(fa_bufs, attT2, [(4, (b + 1) * P) for b in range(TB)])
            to_columns()
            linear("fa_out")

            def conv_layer():
                act.wait_ge(conv_tr, got(conv_tr))
                act.activation(convT, ps[:, 7, 0:176], ACT.Copy).then_inc(conv_sb, 1)
                norm()
                dense(True)

            conv_layer()
            norm()
            linear("kv")
            root(stat_a[:, 0:2], 4)
            copy_heads(kvT.rearrange("p n t -> p (n t)"), [(0, 512), (1, 512)], HD)
            for n_ in "kv":
                act.wait_ge(raw_tr, got(raw_tr))
                act.activation(rawT, ps[:, 2, :], ACT.Copy).then_inc(raw_sb, 1)
                act.activation(peT, ps[:, 3, 0:16], ACT.Copy).then_inc(raw_sb, 1)
                act.wait_ge(blk_ready, got(blk_ready))
                act.activation(xT_hi[:, 0:2, :].rearrange("p a t -> p (a t)")[:, 0:480],
                                         blk32.rearrange("p l n -> p (l n)"), ACT.Copy).then_inc(blk_hi, 1)
                linear(f"{n_}c")
                act.wait_ge(hid_done, got(hid_done))
                for c in range(2):
                    ins = act.activation(hidT[:, c, :], ps[:, 4 + c, 0:2 * N_CMP], ACT.Gelu_apprx_tanh)
                ins.then_inc(hid_sb, 1)
                if n_ == "k":
                    root(stat_a[0:N_CMP, 0:2])
                    act.wait_ge(kc_tr, got(kc_tr))
                    act.activation(kcT[:, :, 0:N_CMP],
                                             ps[0:HD, 7, 0:32].rearrange("p (g n) -> p g n", g=2)[:, :, 0:N_CMP],
                                             ACT.Copy).then_inc(kc_sb, 1)
            norm()
            linear("nsa_in")
            act.wait_ge(bgate_added, got(bgate_added))
            z = zrows(NSA_DIM)
            act.activation(z[:, :, D:NSA_DIM], z[:, :, D:NSA_DIM], ACT.Sigmoid).then_inc(gates_sig, 1)
            root(stat_a[:, 0:16], 2)
            for hb in range(4):
                copy_heads(nqT, [(0, 512), (1, 512)], HD)
                attend(nsa_bufs, attT2, [(4, W) for b in range(TB) for W in (N_CMP, (b + 1) * P, (b + 1) * P)])
            to_columns()
            linear("nsa_out")
            conv_layer()

        @block.tensor
        def _(pe):
            counts = Counts(pe)
            got, sent = counts.got, counts.sent
            n = [0]

            def slot(nk):
                k = n[0]
                pe.wait_ge(w_lo_ready, got(w_lo_ready))
                n[0] += 1
                return [w[:, k % 2, 0:LEN[k]].rearrange("p (k f) -> p k f", k=nk) for w in (w_hi, w_lo)]

            def three(out_, lh, ll, rh, rl, start, stop):
                pe.matmul(out_, lh, rh, start=start, stop=False)
                pe.matmul(out_, lh, rl, start=False, stop=False)
                return pe.matmul(out_, ll, rh, start=False, stop=stop)

            def linear(name, blocks=TB, cond=False):
                f = gi = 0
                slots = SL[name]
                i = 0
                while i < len(slots):
                    nk, nf, _ = slots[i]
                    per = KC // nk
                    if gi >= 2:
                        pe.wait_ge(lin_evac, got(lin_evac))
                    for part in range(per):
                        hi, lo = slot(nk)
                        for k in range(nk):
                            c = part * nk + k
                            for b in range(blocks):
                                if cond:
                                    xh, xl = (x[:, c // 2, c % 2 * P:c % 2 * P + P] for x in (xT_hi, xT_lo))
                                else:
                                    xh, xl = (x[:, c, b * P:(b + 1) * P] for x in (xT_hi, xT_lo))
                                last = three(ps[:, 2 * (gi % 2) + b, 0:nf], xh, xl, hi[:, k, :], lo[:, k, :],
                                             c == 0, c == KC - 1)
                        last.then_inc(w_used, 1)
                    i += per
                    gi += 1
                got(lin_evac, min(2, gi))

            def to_columns(src):
                pe.wait_ge(rows_ready, got(rows_ready))
                for k in range(4):
                    for c in (2 * k, 2 * k + 1):
                        for b in range(TB):
                            last = pe.transpose(ps[:, k, (c % 2) * T + b * P:(c % 2) * T + (b + 1) * P],
                                                src[:, b, c * P:(c + 1) * P], ident)
                    last.then_inc(tr_psum, 1)
                pe.wait_ge(xT_ready, got(xT_ready, 4))

            def attend(bufs, T_, parts):

                def scores(i):
                    q, k, v, nh, W = parts[i]
                    for h in range(nh):
                        last = pe.matmul(ps[:, 4 * (1 - i % 2) + h // 2, (h % 2) * 256:(h % 2) * 256 + W], q(h), k(h),
                                         start=True, stop=True)
                    last.then_inc(att_scores, 1)

                scores(0)
                for i, (q, k, v, nh, W) in enumerate(parts):
                    nch = (W + P - 1) // P
                    kw = min(W, P)
                    if i + 1 < len(parts):
                        scores(i + 1)
                    if W == N_CMP:
                        got(att_exp)
                        pe.wait_ge(att_probs, got(att_probs))
                    else:
                        pe.wait_ge(att_exp, got(att_exp))
                    for h in range(nh):
                        for c in range(nch):
                            u = h * nch + c
                            at = h * 256 + c * P
                            last = pe.transpose(ps[0:kw, 6 + u // 4, (u % 4) * P:(u % 4 + 1) * P],
                                                bufs[i % 2][:, at:at + kw], ident)
                    last.then_inc(att_tr, 1)
                    pe.wait_ge(att_trcopied, got(att_trcopied))
                    if i:
                        pe.wait_ge(att_taken, got(att_taken))
                    for h in range(nh):
                        for c in range(nch):
                            u = h * nch + c
                            last = pe.matmul(ps[:, 3, h * HD:(h + 1) * HD], T_[0:kw, u * P:(u + 1) * P], v(h, c),
                                             start=c == 0, stop=c == nch - 1)
                    last.then_inc(att_out, 1)
                pe.wait_ge(att_taken, got(att_taken))

            def group(nt, first):
                nf = nt * P
                nk = 4 if nt == NT else KC
                for m in range(2):
                    for part in range(KC // nk):
                        hi, lo = slot(nk)
                        for j in range(nt):
                            for k in range(nk):
                                c = part * nk + k
                                last = three(ps[:, j, m * T:(m + 1) * T], hi[:, k, j * P:(j + 1) * P],
                                             lo[:, k, j * P:(j + 1) * P], xT_hi[:, c, :], xT_lo[:, c, :],
                                             c == 0, c == KC - 1)
                            if m == 1 and part == KC // nk - 1:
                                last.then_inc(up_done, 1)
                        if m == 0 or part < KC // nk - 1:
                            last.then_inc(w_used, 1)
                up_open = True
                pe.wait_ge(y_free, got(y_free))
                for part in range(nt // 2):
                    hi, lo = slot(2)
                    for k in range(2):
                        j = 2 * part + k
                        pe.wait_ge(act_ready, got(act_ready))
                        for b in range(TB):
                            for half in range(2):
                                last = three(ps[:, 4 + 2 * b + half, :], aT_hi[:, j, b * P:(b + 1) * P],
                                             aT_lo[:, j, b * P:(b + 1) * P], hi[:, k, half * 512:(half + 1) * 512],
                                             lo[:, k, half * 512:(half + 1) * 512], j == 0, j == nt - 1)
                                if up_open:
                                    last.then_inc(w_used, 1)
                                    up_open = False
                    last.then_inc(w_used, 1)

            FFN_RATES = {w_lo_ready: 6, w_used: 6, up_done: 4, y_free: 1, act_ready: 4}

            def dense():
                with counts.loop(N_GROUPS, FFN_RATES):
                    group(NT, False)
                n[0] += 6 * (N_GROUPS - 1)
                group(NT // 2, False)
                got(y_free)

            def experts():
                zeros = const[:, C_NEG + P:C_NEG + 2 * P]
                rates = {w_lo_ready: 6, e_silu_done: 1, e_act_rows: 1, e_act_cols: 1}
                whole = {k: v * E_GROUPS for k, v in rates.items()}
                whole.update({picked: 1, xg_ready: 2, e_out_sb: 1, back_sb: 1, e_taken: 1})

                def rows_slot(bank, part):
                    hi, lo = slot(4)
                    for k in range(4):
                        c = 4 * part + k
                        last = three(ps[:, bank, :], xT_hi[:, c, 0:P], xT_lo[:, c, 0:P], hi[:, k, :], lo[:, k, :],
                                     c == 0, c == KC - 1)
                    last.then_inc(w_used, 1)

                def hidden_columns():
                    pe.wait_ge(e_act_rows, got(e_act_rows))
                    for j in range(NT):
                        last = pe.transpose(ps[:, 2, j * P:(j + 1) * P], e_act[:, j * P:(j + 1) * P], ident)
                    last.then_inc(e_act_tr, 1)

                def down(closes):
                    pe.wait_ge(e_act_cols, got(e_act_cols))
                    for part in range(2):
                        hi, lo = slot(2)
                        for k in range(2):
                            j = 2 * part + k
                            for half in range(2):
                                last = three(ps[:, 4 + half, :], aT_hi[:, j, 0:P], aT_lo[:, j, 0:P],
                                             hi[:, k, half * 512:(half + 1) * 512],
                                             lo[:, k, half * 512:(half + 1) * 512], False, closes and j == NT - 1)
                        last.then_inc(w_used, 1)

                with counts.loop(N_EXPERTS, whole):
                    pe.wait_ge(picked, got(picked))
                    for c in range(KC):
                        for b in range(TB):
                            last = pe.matmul(ps[:, 6 + c // 4, c % 4 * P:(c % 4 + 1) * P], H[:, b, c * P:(c + 1) * P],
                                             pick[:, b, :], start=b == 0, stop=b == 1)
                    last.then_inc(gathered, 1)
                    for b in range(TB):
                        last = pe.transpose(ps[:, 3, b * P:(b + 1) * P], back[:, b, :], ident)
                    last.then_inc(back_tr, 1)
                    for half in range(2):
                        pe.matmul(ps[:, 4 + half, :], zeros, const[:, 0:512], start=True, stop=False)
                    pe.wait_ge(xg_ready, got(xg_ready, 2))
                    for bank in range(2):
                        for part in range(2):
                            rows_slot(bank, part)
                    with counts.loop(E_GROUPS - 1, rates):
                        pe.wait_ge(e_silu_done, got(e_silu_done))
                        rows_slot(0, 0)
                        hidden_columns()
                        rows_slot(0, 1)
                        down(False)
                        rows_slot(1, 0)
                        rows_slot(1, 1)
                    n[0] += 6 * (E_GROUPS - 2)
                    pe.wait_ge(e_silu_done, got(e_silu_done))
                    hidden_columns()
                    down(True)
                    pe.wait_ge(back_sb, got(back_sb))
                    pe.wait_ge(e_out_sb, got(e_out_sb))
                    for b in range(TB):
                        for half in range(2):
                            last = pe.matmul(ps[:, 6 * (1 - b) + half, :], backT[:, b * P:(b + 1) * P],
                                             e_out[:, half * 512:(half + 1) * 512], start=True, stop=True)
                    last.then_inc(e_scattered, 1)
                    pe.wait_ge(e_taken, got(e_taken))
                n[0] += 6 * E_GROUPS * (N_EXPERTS - 1)

            pe.wait_ge(ld_const, 16)
            pe.wait_ge(cond_silu, got(cond_silu))
            pe.transpose(ps[:, 7, 0:KC], cond_rows, ident[0:KC, 0:KC]).then_inc(cond_tr, 1)
            for l in range(2):
                pe.wait_ge(cond_cols, got(cond_cols))
                linear(f"ada{l}0", 1, True)
                to_columns(H)
                linear(f"in{l}")
                z = zrows(IN_DIM)
                pe.wait_ge(heads_ready, got(heads_ready))
                u = 0
                for col in [AQ + HD * h for h in range(A_HEADS)] + [AK] + [IQ + HD * h for h in range(IDX_HEADS)] + [IK]:
                    for b in range(TB):
                        last = pe.transpose(ps[0:HD, u // 4, (u % 4) * P:(u % 4 + 1) * P], z[:, b, col:col + HD], ident)
                        u += 1
                last.then_inc(heads_tr, 1)
                pe.wait_ge(heads_sb, got(heads_sb, 6))
                for b in range(TB):
                    W = (b + 1) * P
                    for h in range(IDX_HEADS):
                        last = pe.matmul(ps[:, 2 * b + h // 2, (h % 2) * 256:(h % 2) * 256 + W],
                                         headsT[0:HD, 7 + h, b * P:(b + 1) * P], headsT[0:HD, 11, 0:W],
                                         start=True, stop=True)
                    last.then_inc(idx_scores, 1)
                pe.wait_ge(idx_taken, got(idx_taken))
                attend(att_bufs, attT, [
                    (lambda h, b=b, hb=hb: headsT[0:HD, 3 * hb + h, b * P:(b + 1) * P],
                     lambda h, b=b: headsT[0:HD, 6, 0:(b + 1) * P],
                     lambda h, c: z[:, c, AV:AV + HD], 3, (b + 1) * P)
                    for b in range(TB) for hb in range(2)])
                pe.wait_ge(rec_rows, got(rec_rows))
                u = 0
                for src, c0 in ((z, BQ), (h_kk, 0)):
                    for h in range(B_HEADS):
                        for b in range(TB):
                            last = pe.transpose(ps[0:HD, u // 4, (u % 4) * P:(u % 4 + 1) * P],
                                                src[:, b, c0 + h * HD:c0 + (h + 1) * HD], ident)
                            u += 1
                last.then_inc(heads_tr, 1)
                pe.wait_ge(heads_sb, got(heads_sb, 6))

                def cut3(t, h, b):
                    return t[0:HD, (h * TB + b) * P:(h * TB + b + 1) * P]

                def products(kt, qt):
                    for h in range(B_HEADS):
                        for b in range(TB):
                            u = h * TB + b
                            last = pe.matmul(ps[:, 3 + u // 4, (u % 4) * P:(u % 4 + 1) * P], cut3(kt, h, b),
                                             cut3(qt, h, b), start=True, stop=True)
                    last.then_inc(level_prod, 1)

                products(h_kT, h_qT)
                for level in range(LEVELS + 1):
                    for h in range(B_HEADS):
                        for b in range(TB):
                            u = h * TB + b
                            e = C_E + (level + (b if level == LEVELS else 0)) * P
                            last = pe.matmul(ps[0:HD, u // 4, (u % 4) * P:(u % 4 + 1) * P],
                                             h_LF[:, b, h * HD:(h + 1) * HD], const[:, e:e + P], start=True, stop=True)
                    last.then_inc(decay_sum, 1)
                    pe.wait_ge(weighted, got(weighted))
                    if level < LEVELS:
                        products(h_W, h_QW)
                    else:
                        for h in range(B_HEADS):
                            last = pe.matmul(ps[:, 3 + h // 4, (h % 4) * P:(h % 4 + 1) * P], cut3(h_W, h, 0),
                                             cut3(h_QW, h, 1), start=True, stop=True)
                        last.then_inc(level_prod, 1)
                pe.wait_ge(rec_att, got(rec_att))
                for h in range(B_HEADS):
                    v = [z[:, b, BI + h * HD:BI + (h + 1) * HD] for b in range(TB)]
                    A = [h_A[:, (h * TB + b) * P:(h * TB + b + 1) * P] for b in range(TB)]
                    pe.matmul(ps[:, 6, h * HD:(h + 1) * HD], A[0], v[0], start=True, stop=True)
                    pe.matmul(ps[:, 7, h * HD:(h + 1) * HD], h_AX[:, h * P:(h + 1) * P], v[0], start=True, stop=False)
                    last = pe.matmul(ps[:, 7, h * HD:(h + 1) * HD], A[1], v[1], start=False, stop=True)
                last.then_inc(o_out, 1)
                pe.wait_ge(ws_masked, got(ws_masked))
                for g in range(C_GROUPS):
                    pe.transpose(ps[:, 0, g * P:(g + 1) * P], ws[:, g, :], ident)
                pe.transpose(ps[:, 1, 0:4], bs_rows, ident[0:4, 0:4]).then_inc(ws_tr, 1)
                pe.wait_ge(ws_sb, got(ws_sb, 2))
                pe.wait_ge(v_normed, got(v_normed))
                for b in range(TB):
                    for g in range(C_GROUPS):
                        c = CU + C_DIM + g * HD
                        last = pe.matmul(ps[:, 2 + b, g * HD:(g + 1) * HD], wsT[:, g, :], z[:, b, c:c + HD],
                                         start=True, stop=True)
                last.then_inc(spatial, 1)
                to_columns(mix)
                linear(f"out{l}")
                pe.wait_ge(cond_cols, got(cond_cols))
                linear(f"ada{l}1", 1, True)
                to_columns(H)
                if l == 0:
                    dense()
                else:
                    for b in range(TB):
                        for c in range(KC):
                            for x in (xT_hi, xT_lo):
                                last = pe.matmul(ps[:, 4, b * 8:b * 8 + 8], x[:, c, b * P:(b + 1) * P].bitcast(F32),
                                                 router[:, c, :], start=c == 0 and x is xT_hi,
                                                 stop=c == KC - 1 and x is xT_lo)
                    last.then_inc(router_logits, 1)
                    tri = const[:, C_E + (LEVELS + 1) * P:C_E + (LEVELS + 2) * P]
                    pe.wait_ge(chosen_places, got(chosen_places))
                    pe.matmul(ps[:, 5, 0:8], tri, chosen[:, 0, :], start=True, stop=True)
                    pe.matmul(ps[:, 5, 8:16], ones, chosen[:, 0, :], start=True, stop=False)
                    pe.matmul(ps[:, 5, 8:16], tri, chosen[:, 1, :], start=False, stop=True)
                    pe.matmul(ps[:, 5, 16:24], ones, chosen[:, 0, :], start=True, stop=False)
                    pe.matmul(ps[:, 5, 16:24], ones, chosen[:, 1, :], start=False, stop=True).then_inc(places, 1)
                    pe.wait_ge(overflow_known, 1)
                    experts()
                    more_than_128 = pe.value_load(overflow[0:1, 0:1], min_val=0, max_val=1)
                    with pe.If(more_than_128 > 0):
                        experts()
                    with pe.Else():
                        pe.wait_ge(w_used, MOE_END)
                        pe.sem_inc(w_used, MOE_SLOTS)
                        pe.wait_ge(w_used, MOE_END + MOE_SLOTS)
            to_columns(H)
            linear("fa_in")
            z = zrows(FA_DIM)
            pe.wait_ge(fa_logf_ready, got(fa_logf_ready))
            tri = const[:, C_E + (LEVELS + 1) * P:C_E + (LEVELS + 2) * P]
            pe.matmul(ps[:, 0, 0:16], tri, fa_logf[:, 0, :], start=True, stop=True)
            pe.matmul(ps[:, 0, 16:32], ones, fa_logf[:, 0, :], start=True, stop=False)
            pe.matmul(ps[:, 0, 16:32], tri, fa_logf[:, 1, :], start=False, stop=True).then_inc(fa_cumsum, 1)
            pe.wait_ge(heads_ready, got(heads_ready))
            for hb in range(4):
                for src, bank in ((qa, 0), (ka, 4)):
                    for h in range(4):
                        for b in range(TB):
                            c = (4 * hb + h) * 66
                            last = pe.transpose(ps[0:66, bank + h // 2, (h % 2) * T + b * P:(h % 2) * T + (b + 1) * P],
                                                src[:, b, c:c + 66], ident)
                last.then_inc(heads_tr, 1)
                pe.wait_ge(heads_sb, got(heads_sb, 4))
                attend(fa_bufs, attT2, [
                    (lambda h, b=b: qTb[0:66, h * T + b * P:h * T + (b + 1) * P],
                     lambda h, b=b: kTb[0:66, h * T:h * T + (b + 1) * P],
                     lambda h, c: z[:, c, 2 * D + (4 * hb + h) * HD:2 * D + (4 * hb + h + 1) * HD], 4, (b + 1) * P)
                    for b in range(TB)])
            to_columns(mix)
            linear("fa_out")

            def conv_layer(l):
                pe.wait_ge(ld_conv, 32 * (l + 1))
                for j in range(4):
                    last = pe.transpose(ps[:, 7, j * 44:(j + 1) * 44], conv_rows[0:44, j, :], ident[0:44, 0:44])
                last.then_inc(conv_tr, 1)
                pe.wait_ge(conv_sb, got(conv_sb))
                to_columns(H)
                dense()

            conv_layer(0)
            to_columns(H)
            linear("kv")
            z = zrows(KV_DIM)
            pe.wait_ge(heads_ready, got(heads_ready))
            for i, c0 in enumerate((256, 320, 512, 576)):
                for b in range(TB):
                    last = pe.transpose(ps[0:HD, i // 2, (i % 2) * T + b * P:(i % 2) * T + (b + 1) * P],
                                        z[:, b, c0:c0 + HD], ident)
            last.then_inc(heads_tr, 1)
            pe.wait_ge(heads_sb, got(heads_sb, 2))
            for i, name in enumerate("kv"):
                pe.wait_ge(dup_ready, got(dup_ready))
                for g in range(2):
                    for b in range(TB):
                        pe.transpose(ps[:, 2, g * T + b * P:g * T + (b + 1) * P], rawdup[:, b, g * P:(g + 1) * P], ident)
                pe.wait_ge(ld_cmp, 32 * (i + 1))
                pe.transpose(ps[:, 3, 0:16], pe_rows, ident[0:16, 0:16]).then_inc(raw_tr, 1)
                pe.wait_ge(blk_lo, got(blk_lo))
                bh, bl = (x[:, 0:2, :].rearrange("p a t -> p (a t)")[:, 0:480].rearrange("p (l n) -> p l n", l=16)
                          for x in (xT_hi, xT_lo))
                for part in range(2):
                    hi, lo = slot(8)
                    for c in range(2):
                        for k in range(8):
                            lpair = 8 * part + k
                            last = three(ps[:, 4 + c, 0:2 * N_CMP], hi[:, k, c * P:(c + 1) * P],
                                         lo[:, k, c * P:(c + 1) * P], bh[:, lpair, :], bl[:, lpair, :],
                                         lpair == 0, lpair == 15)
                    if part == 0:
                        last.then_inc(w_used, 1)
                last.then_inc(hid_done, 1)
                pe.wait_ge(hid_sb, got(hid_sb))
                for g in range(2):
                    for c in range(2):
                        last = pe.matmul(ps[0:N_CMP, 6, g * HD:(g + 1) * HD], hidT[:, c, g * N_CMP:(g + 1) * N_CMP],
                                         w2c[:, c * HD:(c + 1) * HD], start=c == 0, stop=c == 1)
                        if g == c == 0:
                            last.then_inc(w_used, 1)
                last.then_inc(cmp_out, 1)
                if name == "k":
                    pe.wait_ge(kc_normed, got(kc_normed))
                    for g in range(2):
                        last = pe.transpose(ps[0:HD, 7, g * 16:g * 16 + N_CMP], kc_n[:, g, :],
                                            ident[0:N_CMP, 0:N_CMP])
                    last.then_inc(kc_tr, 1)
                    pe.wait_ge(kc_sb, got(kc_sb))
            to_columns(H)
            linear("nsa_in")
            z = zrows(NSA_DIM)
            pe.wait_ge(heads_ready, got(heads_ready))
            for hb in range(4):
                for h in range(4):
                    for b in range(TB):
                        c = (4 * hb + h) * HD
                        last = pe.transpose(ps[0:HD, h // 2, (h % 2) * T + b * P:(h % 2) * T + (b + 1) * P],
                                            z[:, b, c:c + HD], ident)
                last.then_inc(heads_tr, 1)
                pe.wait_ge(heads_sb, got(heads_sb, 2))
                g = hb // 2
                parts = []
                for b in range(TB):
                    def q(h, b=b):
                        return nqT[0:HD, h * T + b * P:h * T + (b + 1) * P]
                    parts.append((q, lambda h: kcT[:, g, 0:N_CMP], lambda h, c: vcr[:, g, :], 4, N_CMP))
                    for kind in range(2):
                        parts.append((q, lambda h, b=b, kind=kind: kvT[:, 2 * kind + g, 0:(b + 1) * P],
                                      lambda h, c, kind=kind: kv_v[:, c, kind * P + g * HD:kind * P + (g + 1) * HD],
                                      4, (b + 1) * P))
                attend(nsa_bufs, attT2, parts)
            to_columns(mix)
            linear("nsa_out")
            conv_layer(1)

        @block.vector
        def _(dve):
            counts = Counts(dve)
            got, sent = counts.got, counts.sent
            n = [0]

            def split():
                k = n[0]
                if k < len(LEN):
                    dve.wait_ge(w_hi_ready, got(w_hi_ready))
                    dve.tensor_tensor(w_lo[:, k % 2, 0:LEN[k]], raw[:, k % RAW, 0:LEN[k]],
                                                w_hi[:, k % 2, 0:LEN[k]].bitcast(F32), ALU.subtract).then_inc(w_lo_ready, 1)
                n[0] += 1

            def step(ins):
                ins.then_inc(dve_step, 1)
                dve.wait_ge(dve_step, sent(dve_step))

            def tt(o, x, y, op):
                step(dve.tensor_tensor(o, x, y, op))

            def ts(o, x, s1, op0, s2=None, op1=None):
                if op1 is None:
                    step(dve.tensor_scalar(o, x, s1, None, op0))
                else:
                    step(dve.tensor_scalar(o, x, s1, s2, op0, op1))

            def stt(o, x, s, y, op0, op1):
                step(dve.scalar_tensor_tensor(o, x, s, y, op0, op1))

            def linear(name, evac, ahead=True):
                f = gi = done_slots = 0
                slots = SL[name]
                i = 0
                while i < len(slots):
                    nk, nf, _ = slots[i]
                    per = KC // nk
                    for _ in range(per):
                        if ahead or i + _ + 1 < len(slots):
                            split()
                    used(per)
                    evac(gi, 2 * (gi % 2), f, nf)
                    f += nf
                    i += per
                    gi += 1

            def used(k):
                dve.wait_ge(w_used, got(w_used, k))

            def to_columns():
                for k in range(4):
                    dve.wait_ge(xT_hi_ready, got(xT_hi_ready))
                    dve.tensor_tensor(xT_lo[:, 2 * k:2 * k + 2, :],
                                                ps[:, k, :].rearrange("p (k t) -> p k t", k=2),
                                                xT_hi[:, 2 * k:2 * k + 2, :].bitcast(F32), ALU.subtract).then_inc(xT_ready, 1)

            def inv_root(o, x, width):
                ts(o, x, 1.0 / width, ALU.mult, EPS, ALU.add)
                dve.reciprocal(o, o).then_inc(root_in, 1)
                dve.wait_ge(root_in, sent(root_in))
                dve.wait_ge(root_out, got(root_out))

            gains = [0]

            def norm(adaptive):
                dve.wait_ge(sumsq_ready, got(sumsq_ready, 2))
                gains[0] += 16
                dve.wait_ge(ld_gain, gains[0])
                inv_root(rstd, sumsq, D)
                scale = gain
                if adaptive:
                    stt(mod[:, 1, :], mod[:, 1, :], 1.0, gain, ALU.add, ALU.mult)
                    scale = mod[:, 1, :]
                for b in range(TB):
                    stt(H[:, b, :], X[:, b, :], rstd[:, b:b + 1], scale, ALU.mult, ALU.mult)
                    if adaptive:
                        tt(H[:, b, :], H[:, b, :], mod[:, 0, :], ALU.add)
                beat().then_inc(rows_ready, 1)
                dve.wait_ge(rows_ready, sent(rows_ready))
                to_columns()

            def into_rows(width):
                z = zrows(width)

                def evac(gi, bank, f, nf):
                    step(dve.tensor_copy(z[:, 0, f:f + nf], ps[:, bank, 0:nf]))
                    dve.tensor_copy(z[:, 1, f:f + nf], ps[:, bank + 1, 0:nf]).then_inc(lin_evac, 1)
                    dve.wait_ge(lin_evac, sent(lin_evac))
                return evac

            def into_residual(gate):
                def evac(gi, bank, f, nf):
                    for b in range(TB):
                        if gate:
                            tt(mix[:, b, f:f + nf], ps[:, bank + b, 0:nf], mod[:, 2, f:f + nf], ALU.mult)
                            tt(X[:, b, f:f + nf], X[:, b, f:f + nf], mix[:, b, f:f + nf], ALU.add)
                        else:
                            tt(X[:, b, f:f + nf], X[:, b, f:f + nf], ps[:, bank + b, 0:nf], ALU.add)
                    beat().then_inc(lin_evac, 1)
                    dve.wait_ge(lin_evac, sent(lin_evac))
                return evac

            mods = [0]

            def ada(name, ahead=True):
                beat().then_inc(cond_ready, 1)
                dve.wait_ge(cond_ready, sent(cond_ready))
                dve.wait_ge(cond_hi, got(cond_hi))
                cb = condT.unsqueeze(2).to_broadcast([P, KC, P])
                dve.tensor_tensor(xT_lo[:, 0:4, :].rearrange("p a (b m) -> p (a b) m", b=2), cb, xT_hi[:, 0:4, :].rearrange("p a (b m) -> p (a b) m", b=2).bitcast(F32), ALU.subtract).then_inc(cond_cols, 1)
                dve.wait_ge(cond_cols, sent(cond_cols))
                mods[0] += 16
                dve.wait_ge(ld_mod, mods[0])
                flat = arena[:, 0:3 * D]

                def evac(gi, bank, f, nf):
                    dve.tensor_tensor(flat[:, f:f + nf], flat[:, f:f + nf], ps[:, bank, 0:nf], ALU.add).then_inc(lin_evac, 1)
                    dve.wait_ge(lin_evac, sent(lin_evac))
                linear(name, evac, ahead)

            def beat():
                return dve.tensor_copy(tick[:, 1:2], tick[:, 0:1])

            def angles(pos, inv, width, s, c, rows_=P):
                c1 = 6.28125
                c2 = float(np.float32(np.round((2 * np.pi - c1) * 2 ** 20) / 2 ** 20))
                c3 = float(2 * np.pi - c1 - c2)
                magic = 1.5 * 2 ** 23
                ts(s, inv, pos, ALU.mult)
                ts(c, s, float(1 / (2 * np.pi)), ALU.mult, magic, ALU.add)
                ts(c, c, magic, ALU.subtract)
                for k in (c1, c2, c3):
                    stt(s, c, -k, s, ALU.mult, ALU.add)
                ts(s, s, 3.1415925, ALU.min, -3.1415925, ALU.max)
                stt(c, s, -1.0, s, ALU.mult, ALU.max)
                ts(c, c, -1.0, ALU.mult, float(np.pi / 2), ALU.add)

            def rope(x, nh, half, cos, sin, tmp, rows_=P):
                x1, x2 = x[:, :, 0:half], x[:, :, half:2 * half]
                cb = cos.unsqueeze(1).to_broadcast([rows_, nh, half])
                sb_ = sin.unsqueeze(1).to_broadcast([rows_, nh, half])
                t = [m[:, 0:nh * half].rearrange("p (h d) -> p h d", h=nh) for m in tmp]
                for o, x_, y in ((t[0], x1, cb), (t[1], x2, sb_), (t[2], x2, cb), (t[3], x1, sb_)):
                    dve.tensor_tensor(o, x_, y, ALU.mult).then_inc(dve_step, 1)
                dve.wait_ge(dve_step, sent(dve_step, 4))
                tt(x1, t[0], t[1], ALU.subtract)
                tt(x2, t[2], t[3], ALU.add)

            def attend(bufs, parts):

                def maxima(i):
                    nh, W, mask, _, _ = parts[i]
                    dve.wait_ge(att_scores, got(att_scores))
                    for h in range(nh):
                        dve.tensor_tensor_reduce(
                            out=bufs[i % 2][:, h * 256:h * 256 + W],
                            in0=ps[:, 4 * (1 - i % 2) + h // 2, (h % 2) * 256:(h % 2) * 256 + W], in1=mask,
                            scale=HD ** -0.5, scalar=GONE, op0=ALU.add, op1=ALU.max,
                            accum_out=rowmax[:, i % 2, h:h + 1]).then_inc(dve_step, 1)
                    dve.wait_ge(dve_step, sent(dve_step, nh))
                    dve.tensor_scalar(negmax[:, i % 2, 0:nh], rowmax[:, i % 2, 0:nh], -1.0, None,
                                      ALU.mult).then_inc(att_centred, 1)

                maxima(0)
                for i, (nh, W, _, take, m01) in enumerate(parts):
                    if i + 1 < len(parts):
                        maxima(i + 1)
                    total, inverse = rowsum[:, i % 2, 0:nh], rinv[:, i % 2, 0:nh]
                    dve.wait_ge(att_exp, got(att_exp))
                    if m01 is not None:
                        s = bufs[i % 2][:, 0:nh * 256].rearrange("p (h w) -> p h w", h=nh)[:, :, 0:W]
                        tt(s, s, m01.unsqueeze(1).to_broadcast([P, nh, W]), ALU.mult)
                        dve.tensor_reduce(total, s, AX.X, ALU.add).then_inc(att_probs, 1)
                        dve.wait_ge(att_probs, sent(att_probs))
                    ts(total, total, 1.0, ALU.max)
                    step(dve.reciprocal(inverse, total))
                    dve.wait_ge(att_out, got(att_out))
                    take(ps[:, 3, 0:nh * HD].rearrange("p (h d) -> p h d", h=nh), inverse)

            def take_into(dst):
                def take(o, r):
                    nh = r.shape[1]
                    dve.tensor_tensor(dst.rearrange("p (h d) -> p h d", h=nh), o, r.unsqueeze(2).to_broadcast([P, nh, HD]), ALU.mult).then_inc(att_taken, 1)
                    dve.wait_ge(att_taken, sent(att_taken))
                return take

            def log_sigmoid(o, x, t, second=None):
                dve.scalar_tensor_tensor(t, x, -1.0, x, ALU.mult, ALU.max).then_inc(lf_abs, 1)
                dve.wait_ge(lf_abs, sent(lf_abs))
                dve.wait_ge(lf_exp, got(lf_exp))
                dve.tensor_scalar(t, t, 1.0, None, ALU.add).then_inc(lf_one, 1)
                dve.wait_ge(lf_one, sent(lf_one))
                dve.wait_ge(lf_ln, got(lf_ln))
                stt(o, x, 0.0, t, ALU.min, ALU.subtract)

            def group(nt, weight, conv=None):
                nsl = 2 if nt == NT else 1
                for _ in range(2 * nsl - 1):
                    split()
                split()
                for j in range(nt):
                    cols = slice(j * T, (j + 1) * T)
                    dve.wait_ge(up_done, got(up_done))
                    up = ps[:, j, T:2 * T]
                    if conv is not None:
                        for m, dst in ((0, cgate), (1, cval)):
                            w = [conv(m, k, j) for k in range(4)]
                            u = ps[:, j, m * T:(m + 1) * T]
                            d = dst[:, cols]
                            ts(d, u, w[2], ALU.mult, w[3], ALU.add)
                            stt(d[:, 1:T], u[:, 0:T - 1], w[1], d[:, 1:T], ALU.mult, ALU.add)
                            stt(d[:, 2:T], u[:, 0:T - 2], w[0], d[:, 2:T], ALU.mult, ALU.add)
                        beat().then_inc(conv_done, 1)
                        dve.wait_ge(conv_done, sent(conv_done))
                        up = cval[:, cols]
                    dve.wait_ge(silu_done, got(silu_done))
                    dve.tensor_tensor(act_f[:, cols], act_g[:, cols], up, ALU.mult).then_inc(act_prod, 1)
                    dve.wait_ge(act_hi, got(act_hi))
                    dve.tensor_tensor(aT_lo[:, j, :], act_f[:, cols], aT_hi[:, j, :].bitcast(F32),
                                                ALU.subtract).then_inc(act_ready, 1)
                for _ in range(nsl - 1):
                    split()
                split()
                used(3 * nsl)
                for b in range(TB):
                    for half in range(2):
                        y = ps[:, 4 + 2 * b + half, :]
                        o = acc[:, b, half * 512:(half + 1) * 512]
                        if weight is None:
                            tt(o, o, y, ALU.add)
                        else:
                            stt(o, y, weight(b), o, ALU.mult, ALU.add)
                beat().then_inc(y_free, 1)
                dve.wait_ge(y_free, sent(y_free))

            def dve_rates(conv):
                r = {w_hi_ready: 6, w_lo_ready: 6, w_used: 6, up_done: 4, silu_done: 4, act_prod: 4,
                     act_hi: 4, act_ready: 4, y_free: 1, dve_step: 4}
                if conv:
                    r[conv_done] = 4
                    r[dve_step] += 4 * 6
                return r

            def experts():
                rates = {w_hi_ready: 6, w_used: 6, e_silu_done: 1, e_act_hi: 1}
                whole = {k: v * E_GROUPS for k, v in rates.items()}
                whole.update({xg_hi_ready: 2, e_scattered: 1, dve_step: 6})
                iota = const[:, C_IOTA:C_IOTA + P]

                def product():
                    dve.wait_ge(e_silu_done, got(e_silu_done))
                    dve.tensor_tensor(e_act, e_gate, ps[:, 1, :], ALU.mult).then_inc(e_act_rows, 1)

                def act_low():
                    dve.wait_ge(e_act_hi, got(e_act_hi))
                    dve.tensor_tensor(aT_lo[:, :, 0:P], ps[:, 2, :].rearrange("p (j t) -> p j t", j=NT),
                                      aT_hi[:, :, 0:P].bitcast(F32), ALU.subtract).then_inc(e_act_cols, 1)

                with counts.loop(N_EXPERTS, whole) as e:
                    for b in range(TB):
                        at = place[:, b, bass.ds(e, 1)]
                        ts(pick[:, b, :], iota, at, ALU.is_equal, chosen[:, b, bass.ds(e, 1)], ALU.mult)
                        ts(back[:, b, :], iota, at, ALU.is_equal, gates[:, b, bass.ds(e, 1)], ALU.mult)
                    beat().then_inc(picked, 1)
                    split()
                    for k in range(2):
                        dve.wait_ge(xg_hi_ready, got(xg_hi_ready))
                        dve.tensor_tensor(xT_lo[:, 4 * k:4 * k + 4, 0:P],
                                          ps[:, 6 + k, :].rearrange("p (c t) -> p c t", c=4),
                                          xT_hi[:, 4 * k:4 * k + 4, 0:P].bitcast(F32), ALU.subtract).then_inc(xg_ready, 1)
                    for _ in range(4):
                        split()
                    used(4)
                    product()
                    with counts.loop(E_GROUPS - 1, rates):
                        split()
                        split()
                        act_low()
                        for _ in range(4):
                            split()
                        used(6)
                        product()
                    n[0] += 6 * (E_GROUPS - 2)
                    split()
                    act_low()
                    used(2)
                    dve.wait_ge(e_scattered, got(e_scattered))
                    for b in range(TB):
                        o = acc[:, b, :].rearrange("p (k n) -> p k n", k=2)
                        y = ps[:, 6 * (1 - b):6 * (1 - b) + 2, :]
                        tt(o, o, y, ALU.add)
                    beat().then_inc(e_taken, 1)
                n[0] += 6 * E_GROUPS * (N_EXPERTS - 1)

            def clear_acc():
                dve.memset(acc, 0.0).then_inc(y_free, 1)
                dve.wait_ge(y_free, sent(y_free))

            def dense(conv):
                clear_acc()
                with counts.loop(N_GROUPS, dve_rates(conv)) as g:
                    if conv:
                        def w(m, k, j):
                            return convT[:, bass.ds(g * NT + (k * 44 + m * 22 + j), 1)]
                        group(NT, None, w)
                    else:
                        group(NT, None)
                n[0] += 6 * (N_GROUPS - 1)
                if conv:
                    def w(m, k, j):
                        c = k * 44 + m * 22 + N_GROUPS * NT + j
                        return convT[:, c:c + 1]
                    group(NT // 2, None, w)
                else:
                    group(NT // 2, None)

            def add_gated():
                for b in range(TB):
                    tt(acc[:, b, :], acc[:, b, :], mod[:, 2, :], ALU.mult)
                for b in range(TB):
                    tt(X[:, b, :], X[:, b, :], acc[:, b, :], ALU.add)

            def head_norm(dst, src, nh, g, rows_=P, sq=None):
                x = src
                t = sq[0:rows_, 0:nh * HD].rearrange("p (h d) -> p h d", h=nh)
                tt(t, x, x, ALU.mult)
                step(dve.tensor_reduce(stat_a[0:rows_, 0:nh], t, AX.X, ALU.add))
                inv_root(stat_a[0:rows_, 0:nh], stat_a[0:rows_, 0:nh], HD)
                tt(dst, x, stat_a[0:rows_, 0:nh].unsqueeze(2).to_broadcast([rows_, nh, HD]), ALU.mult)
                tt(dst, dst, g[0:rows_, :].unsqueeze(1).to_broadcast([rows_, nh, HD]), ALU.mult)

            split()
            step(dve.memset(tick, 0.0))
            dve.wait_ge(ld_const, 16)
            dve.wait_ge(ld_first, 48)
            step(dve.tensor_copy(posf[:, 0:2], posi[:, 0:2]))
            for b in range(TB):
                angles(posf[:, b:b + 1], const[:, C_INV1:C_INV1 + 32], 32, sin1[:, b, :], cos1[:, b, :])
            beat().then_inc(angles_ready, 1)
            dve.wait_ge(angles_ready, sent(angles_ready))
            dve.wait_ge(sines, got(sines, 2))
            dve.wait_ge(cond_tr, got(cond_tr))
            step(dve.tensor_copy(condT, ps[:, 7, 0:KC]))
            dve.wait_ge(ld_x, 16)
            lp_loads = 0
            for l in range(2):
                ada(f"ada{l}0")
                beat().then_inc(x_ready, 1)
                dve.wait_ge(x_ready, sent(x_ready))
                norm(True)
                z = zrows(IN_DIM)
                linear(f"in{l}", into_rows(IN_DIM))
                for b in range(TB):
                    for c0, nh in ((AQ, 7), (IQ, 5)):
                        rope(z[:, b, c0:c0 + nh * HD].rearrange("p (h d) -> p h d", h=nh), nh, 32,
                             cos1[:, b, :], sin1[:, b, :], rope_t)
                dve.tensor_scalar(iw_half, z[:, :, IW:IW + IDX_HEADS], IDX_HEADS ** -0.5, None, ALU.mult).then_inc(heads_ready, 1)
                dve.wait_ge(heads_ready, sent(heads_ready))
                for b in range(TB):
                    W = (b + 1) * P
                    dve.wait_ge(idx_scores, got(idx_scores))
                    rel = idx_rel.rearrange("p (h w) -> p h w", h=4)
                    for k in range(2):
                        ts(rel[:, 2 * k:2 * k + 2, 0:W],
                           ps[:, 2 * b + k, :].rearrange("p (h w) -> p h w", h=2)[:, :, 0:W],
                           HD ** -0.5, ALU.mult, 0.0, ALU.max)
                    if b == 0:
                        beat().then_inc(idx_taken, 1)
                        dve.wait_ge(idx_taken, sent(idx_taken))
                    s = idx_acc[:, 0:W]
                    ts(s, rel[:, 0, 0:W], iw_half[:, b, 0:1], ALU.mult)
                    for h in range(1, IDX_HEADS):
                        stt(s, rel[:, h, 0:W], iw_half[:, b, h:h + 1], s, ALU.mult, ALU.add)
                    tt(s, s, const[:, C_M01 + AT[b]:C_M01 + AT[b] + W], ALU.mult)
                    tt(s, s, const[:, C_NEG + AT[b]:C_NEG + AT[b] + W], ALU.add)
                    for _ in range(TOPK // 8):
                        step(dve.max(top8, s))
                        step(dve.match_replace(s, top8, s, GONE))
                    ts(topw[:, 0:W], s, GONE / 2, ALU.is_gt, NEG, ALU.mult)
                    tt(dsa_mask[:, b, 0:W], topw[:, 0:W], const[:, C_NEG + AT[b]:C_NEG + AT[b] + W], ALU.add)
                attend(att_bufs, [(3, (b + 1) * P, dsa_mask[:, b, 0:(b + 1) * P],
                                   take_into(mix[:, b, 192 * hb:192 * hb + 192]), None)
                                  for b in range(TB) for hb in range(2)])
                F = z[:, :, BF:BF + BD]
                if l:
                    beat().then_inc(lb_free, 1)
                    dve.wait_ge(lb_free, sent(lb_free))
                    dve.wait_ge(ld_lb, 16)
                    tt(h_t3[:, 0, :], lb_rows[:, 0, :], lb_rows[:, 1, :], ALU.max)
                    for k in range(2):
                        tt(lb_rows[:, k, :], lb_rows[:, k, :], h_t3[:, 0, :], ALU.subtract)
                    beat().then_inc(lb_diff, 1)
                    dve.wait_ge(lb_diff, sent(lb_diff))
                    dve.wait_ge(lb_exp, got(lb_exp))
                    dve.tensor_tensor(h_t1[:, 0, :], h_t2[:, 0, :], h_t2[:, 1, :], ALU.add).then_inc(lb_sum, 1)
                    dve.wait_ge(lb_sum, sent(lb_sum))
                    dve.wait_ge(lb_ln, got(lb_ln))
                    tt(h_lb[:, 0, :], lb_rows[:, 1, :], h_t1[:, 0, :], ALU.subtract)
                    tt(h_lb[:, 1, :], lb_rows[:, 0, :], h_t1[:, 0, :], ALU.subtract)
                log_sigmoid(h_LF, F, h_t1)
                if l:
                    lb = h_lb[:, 0:1, :].to_broadcast([P, TB, BD])
                    lcomp = h_lb[:, 1:2, :].to_broadcast([P, TB, BD])
                    tt(h_LF, h_LF, lcomp, ALU.add)
                    tt(h_t2, h_LF, lb, ALU.subtract)
                    tt(h_LF, h_LF, lb, ALU.max)
                    dve.scalar_tensor_tensor(h_t1, h_t2, -1.0, h_t2, ALU.mult, ALU.max).then_inc(lf_abs, 1)
                    dve.wait_ge(lf_abs, sent(lf_abs))
                    dve.wait_ge(lf_exp, got(lf_exp))
                    dve.tensor_scalar(h_t1, h_t1, 1.0, None, ALU.add).then_inc(lf_one, 1)
                    dve.wait_ge(lf_one, sent(lf_one))
                    dve.wait_ge(lf_ln, got(lf_ln))
                    tt(h_LF, h_LF, h_t1, ALU.add)
                    dve.wait_ge(lb_comp, got(lb_comp))
                dve.wait_ge(kk_sig, got(kk_sig))
                if l:
                    tt(h_kk, h_kk, h_t3[:, 0:1, :].to_broadcast([P, TB, BD]), ALU.mult)
                beat().then_inc(rec_rows, 1)
                dve.wait_ge(rec_rows, sent(rec_rows))
                got(heads_sb, 6)
                dve.wait_ge(heads_sb, got(heads_sb, 6))

                hs = mix[:, 0, BD:BD + 512]
                dve.wait_ge(level_prod, got(level_prod))
                for k in range(3):
                    tt(h_A[:, 512 * k:512 * k + 512].rearrange("p (n t) -> p n t", n=4),
                       ps[:, 3 + k, :].rearrange("p (n t) -> p n t", n=4),
                       ident.unsqueeze(1).to_broadcast([P, 4, P]), ALU.mult)
                for level in range(LEVELS + 1):
                    dve.wait_ge(decay, got(decay))
                    w = h_W[0:HD, :]
                    tt(h_QW[0:HD, :], h_qT[0:HD, :], w, ALU.mult)
                    dve.tensor_tensor(w, h_kT[0:HD, :], w, ALU.mult).then_inc(weighted, 1)
                    dve.wait_ge(weighted, sent(weighted))
                    dve.wait_ge(level_prod, got(level_prod))
                    if level < LEVELS:
                        m = const[:, C_LM + level * P:C_LM + (level + 1) * P]
                        for k in range(3):
                            t = hs.rearrange("p (n t) -> p n t", n=4)
                            tt(t, ps[:, 3 + k, :].rearrange("p (n t) -> p n t", n=4),
                               m.unsqueeze(1).to_broadcast([P, 4, P]), ALU.mult)
                            tt(h_A[:, 512 * k:512 * k + 512], h_A[:, 512 * k:512 * k + 512], hs, ALU.add)
                    else:
                        step(dve.tensor_copy(h_AX[:, 0:512], ps[:, 3, :]))
                        dve.tensor_copy(h_AX[:, 512:768], ps[:, 4, 0:256]).then_inc(rec_att, 1)
                        dve.wait_ge(rec_att, sent(rec_att))
                dve.wait_ge(o_out, got(o_out))
                for b in range(TB):
                    step(dve.tensor_copy(h_O[:, b, :], ps[:, 6 + b, 0:BD]))
                beat().then_inc(ws_free, 1)
                dve.wait_ge(ws_free, sent(ws_free))
                tt(h_sq, h_O, h_O, ALU.mult)
                step(dve.tensor_reduce(stat_a[:, 0:12], h_sq.rearrange("p b (h d) -> p (b h) d", d=HD), AX.X, ALU.add))
                inv_root(stat_a[:, 0:12], stat_a[:, 0:12], HD)
                o4 = h_O.rearrange("p b (h d) -> p (b h) d", d=HD)
                tt(o4, o4, stat_a[:, 0:12].unsqueeze(2).to_broadcast([P, 12, HD]), ALU.mult)
                lp_loads += 48
                dve.wait_ge(ld_lp, lp_loads)
                tt(o4, o4, onorm.unsqueeze(1).to_broadcast([P, 12, HD]), ALU.mult)
                dve.wait_ge(gate_silu, got(gate_silu))
                tt(mix[:, :, BD:2 * BD], h_O, h_sg, ALU.mult)
                dve.wait_ge(ld_ws, 32 * (l + 1))
                dve.tensor_tensor(ws, ws, const[:, C_M01:C_M01 + P].unsqueeze(1).to_broadcast([P, 4, P]), ALU.mult).then_inc(ws_masked, 1)
                dve.wait_ge(ws_masked, sent(ws_masked))
                dve.wait_ge(gelu_uv, got(gelu_uv))
                V = z[:, :, CU + C_DIM:CU + 2 * C_DIM]
                step(dve.tensor_reduce(stat_a[:, 0:2], V, AX.X, ALU.add))
                ts(stat_a[:, 0:2], stat_a[:, 0:2], 1.0 / C_DIM, ALU.mult)
                for b in range(TB):
                    ts(V[:, b, :], V[:, b, :], stat_a[:, b:b + 1], ALU.subtract)
                tt(g_t, V, V, ALU.mult)
                step(dve.tensor_reduce(stat_b[:, 0:2], g_t, AX.X, ALU.add))
                inv_root(stat_b[:, 0:2], stat_b[:, 0:2], C_DIM)
                for b in range(TB):
                    stt(V[:, b, :], V[:, b, :], stat_b[:, b:b + 1], vn_g, ALU.mult, ALU.mult)
                dve.tensor_tensor(V, V, vn_b.unsqueeze(1).to_broadcast([P, TB, C_DIM]), ALU.add).then_inc(v_normed, 1)
                dve.wait_ge(v_normed, sent(v_normed))
                dve.wait_ge(spatial, got(spatial))
                for b in range(TB):
                    tt(g_t[:, b, :].rearrange("p (g d) -> p g d", g=4),
                       ps[:, 2 + b, 0:C_DIM].rearrange("p (g d) -> p g d", g=4),
                       bsT.unsqueeze(2).to_broadcast([P, 4, HD]), ALU.add)
                dve.tensor_tensor(mix[:, :, 2 * BD:D], g_t, z[:, :, CU:CU + C_DIM], ALU.mult).then_inc(rows_ready, 1)
                dve.wait_ge(rows_ready, sent(rows_ready))
                beat().then_inc(lp_free, 1)
                dve.wait_ge(lp_free, sent(lp_free))
                beat().then_inc(gain_free, 1)
                dve.wait_ge(gain_free, sent(gain_free))
                to_columns()
                linear(f"out{l}", into_residual(True))
                beat().then_inc(mod_free, 1)
                dve.wait_ge(mod_free, sent(mod_free))
                ada(f"ada{l}1", ahead=l == 0)
                beat().then_inc(x_ready, 1)
                dve.wait_ge(x_ready, sent(x_ready))
                norm(True)
                if l == 0:
                    dense(False)
                else:
                    dve.wait_ge(router_logits, got(router_logits))
                    step(dve.tensor_copy(logits.rearrange("p b e -> p (b e)"), ps[:, 4, 0:16]))
                    iota = const[:, C_IOTA:C_IOTA + 8]
                    for b in range(TB):
                        step(dve.max(top8, logits[:, b, :]))
                        step(dve.max_index(top_i, top8, logits[:, b, :]))
                        step(dve.tensor_copy(top_f, top_i))
                        dve.tensor_tensor(ew[:, 0:1], top8[:, 1:2], top8[:, 0:1], ALU.subtract).then_inc(gate_diff, 1)
                        dve.wait_ge(gate_diff, sent(gate_diff))
                        dve.wait_ge(gate_exp, got(gate_exp))
                        ts(ew[:, 2:3], ew[:, 1:2], 1.0, ALU.add)
                        step(dve.reciprocal(ew[:, 2:3], ew[:, 2:3]))
                        tt(ew[:, 3:4], ew[:, 1:2], ew[:, 2:3], ALU.mult)
                        ts(chosen[:, b, :], iota, top_f[:, 0:1], ALU.is_equal)
                        stt(chosen[:, b, :], iota, top_f[:, 1:2], chosen[:, b, :], ALU.is_equal, ALU.add)
                        ts(top8, iota, top_f[:, 0:1], ALU.is_equal, ew[:, 2:3], ALU.mult)
                        ts(gates[:, b, :], iota, top_f[:, 1:2], ALU.is_equal, ew[:, 3:4], ALU.mult)
                        tt(gates[:, b, :], gates[:, b, :], top8, ALU.add)
                    beat().then_inc(chosen_places, 1)
                    dve.wait_ge(places, got(places))
                    ts(place.rearrange("p b e -> p (b e)"), ps[:, 5, 0:16], 1.0, ALU.subtract)
                    step(dve.tensor_reduce(most, ps[:, 5, 16:24], AX.X, ALU.max))
                    ts(most, most, float(P), ALU.is_gt)
                    dve.tensor_copy(overflow, most).then_inc(overflow_known, 1)
                    step(dve.memset(acc, 0.0))
                    experts()
                    dve.wait_ge(overflow_known, 1)
                    more_than_128 = dve.value_load(overflow[0:1, 0:1], min_val=0, max_val=1)
                    made = counts.signalled[dve_step]
                    with dve.If(more_than_128 > 0):
                        ts(place, place, float(P), ALU.subtract)
                        experts()
                    added = counts.signalled[dve_step] - made
                    with dve.Else():
                        for sem, total, more in ((w_lo_ready, MOE_END, MOE_SLOTS), (dve_step, made, added)):
                            dve.wait_ge(sem, total)
                            dve.sem_inc(sem, more)
                            dve.wait_ge(sem, total + more)
                    split()
                add_gated()
                if l == 0:
                    beat().then_inc(mod_free, 1)
                    dve.wait_ge(mod_free, sent(mod_free))
                beat().then_inc(gain_free, 1)
                dve.wait_ge(gain_free, sent(gain_free))
            beat().then_inc(x_ready, 1)
            dve.wait_ge(x_ready, sent(x_ready))
            dve.wait_ge(sumsq_ready, got(sumsq_ready, 2))
            gains[0] += 16
            dve.wait_ge(ld_gain, gains[0])
            inv_root(rstd, sumsq, D)
            for b in range(TB):
                stt(X[:, b, :], X[:, b, :], rstd[:, b:b + 1], gain, ALU.mult, ALU.mult)
            beat().then_inc(gain_free, 1)
            dve.wait_ge(gain_free, sent(gain_free))
            lp_loads += 160
            dve.wait_ge(ld_lp, lp_loads)
            step(dve.tensor_copy(posf[:, 0:2], posi[:, 0:2]))
            step(dve.tensor_copy(posf[0:N_CMP, 2:3], posi[0:N_CMP, 2:3]))
            inv2 = const[:, C_INV2:C_INV2 + 8]
            for b in range(TB):
                angles(posf[:, b:b + 1], inv2, 8, sin2[:, b, :], cos2[:, b, :])
            angles(posf[0:N_CMP, 2:3], inv2[0:N_CMP, :], 8, sinc[0:N_CMP, :], cosc[0:N_CMP, :])
            beat().then_inc(angles_ready, 1)
            dve.wait_ge(angles_ready, sent(angles_ready))
            beat().then_inc(x_ready, 1)
            dve.wait_ge(x_ready, sent(x_ready))
            dve.wait_ge(sines, got(sines, 4))
            norm(False)
            linear("fa_in", into_rows(FA_DIM))
            z = zrows(FA_DIM)
            tt(fa_logf, z[:, :, 3 * D:FA_DIM], bf_b.unsqueeze(1).to_broadcast([P, TB, HEADS2]), ALU.add)
            lf_t = stat_b.rearrange("p (b h) -> p b h", b=2)
            log_sigmoid(fa_logf, fa_logf, lf_t)
            beat().then_inc(fa_logf_ready, 1)
            dve.wait_ge(fa_logf_ready, sent(fa_logf_ready))
            for src0, dst, g in ((0, qa, qg), (D, ka, kg)):
                for b in range(TB):
                    x = z[:, b, src0:src0 + D].rearrange("p (h d) -> p h d", h=HEADS2)
                    o = dst[:, b, :].rearrange("p (h d) -> p h d", h=HEADS2)[:, :, 0:HD]
                    head_norm(o, x, HEADS2, g, sq=fa_sq)
            dve.wait_ge(fa_cumsum, got(fa_cumsum))
            step(dve.tensor_copy(fa_c.rearrange("p b h -> p (b h)"), ps[:, 0, 0:32]))
            up8 = float(HD) ** 0.5
            for b in range(TB):
                q4 = qa[:, b, :].rearrange("p (h d) -> p h d", h=HEADS2)
                k4 = ka[:, b, :].rearrange("p (h d) -> p h d", h=HEADS2)
                c = fa_c[:, b, :].unsqueeze(2)
                step(dve.memset(q4[:, :, 64:65], up8))
                ts(q4[:, :, 65:66], c, up8, ALU.mult)
                ts(k4[:, :, 64:65], c, -1.0, ALU.mult)
                step(dve.memset(k4[:, :, 65:66], 1.0))
            beat().then_inc(heads_ready, 1)
            dve.wait_ge(heads_ready, sent(heads_ready))
            for hb in range(4):
                attend(fa_bufs, [(4, (b + 1) * P, const[:, C_NEG + AT[b]:C_NEG + AT[b] + (b + 1) * P],
                                  take_into(mix[:, b, 256 * hb:256 * hb + 256]), None) for b in range(TB)])
            beat().then_inc(rows_ready, 1)
            dve.wait_ge(rows_ready, sent(rows_ready))
            beat().then_inc(conv_free, 1)
            dve.wait_ge(conv_free, sent(conv_free))
            beat().then_inc(gain_free, 1)
            dve.wait_ge(gain_free, sent(gain_free))
            to_columns()
            linear("fa_out", into_residual(False))

            def conv_layer():
                beat().then_inc(x_ready, 1)
                dve.wait_ge(x_ready, sent(x_ready))
                norm(False)
                dense(True)
                for b in range(TB):
                    tt(X[:, b, :], X[:, b, :], acc[:, b, :], ALU.add)
                beat().then_inc(gain_free, 1)
                dve.wait_ge(gain_free, sent(gain_free))

            conv_layer()
            beat().then_inc(cmp_free, 1)
            dve.wait_ge(cmp_free, sent(cmp_free))
            beat().then_inc(x_ready, 1)
            dve.wait_ge(x_ready, sent(x_ready))
            norm(False)
            linear("kv", into_rows(KV_DIM))
            z = zrows(KV_DIM)
            for c0, g in ((256, ksg), (512, kwg)):
                for b in range(TB):
                    x = z[:, b, c0:c0 + P].rearrange("p (h d) -> p h d", h=2)
                    head_norm(x, x, 2, g, sq=kv_sq)
                    rope(x, 2, 8, cos2[:, b, :], sin2[:, b, :], krope)
            beat().then_inc(heads_ready, 1)
            dve.wait_ge(heads_ready, sent(heads_ready))
            for kind, c0 in enumerate((384, 640)):
                step(dve.tensor_copy(kv_v[:, :, kind * P:(kind + 1) * P], z[:, :, c0:c0 + P]))
            for i, name in enumerate("kv"):
                for g in range(2):
                    for s in range(2):
                        step(dve.tensor_copy(rawdup[:, :, g * P + s * HD:g * P + (s + 1) * HD],
                                           z[:, :, i * P + g * HD:i * P + (g + 1) * HD]))
                beat().then_inc(dup_ready, 1)
                dve.wait_ge(dup_ready, sent(dup_ready))
                dve.wait_ge(raw_sb, got(raw_sb, 2))
                for s in range(2):
                    part = slice(s * HD, (s + 1) * HD)
                    for g in range(2):
                        src = rawT[part, g * T:(g + 1) * T].rearrange("p (n l s) -> p s l n", l=8, s=2)[:, s, :, :]
                        for half in range(2):
                            o = blk32[part, 8 * half:8 * half + 8, g * N_CMP:(g + 1) * N_CMP]
                            tt(o, src[:, :, half:half + N_CMP],
                               peT[part, 8 * half:8 * half + 8].unsqueeze(2).to_broadcast([HD, 8, N_CMP]), ALU.add)
                beat().then_inc(blk_ready, 1)
                dve.wait_ge(blk_ready, sent(blk_ready))
                dve.wait_ge(blk_hi, got(blk_hi))
                bh, bl = (x[:, 0:2, :].rearrange("p a t -> p (a t)")[:, 0:480] for x in (xT_hi, xT_lo))
                dve.tensor_tensor(bl, blk32.rearrange("p l n -> p (l n)"), bh.bitcast(F32), ALU.subtract).then_inc(blk_lo, 1)
                dve.wait_ge(blk_lo, sent(blk_lo))
                split()
                split()
                used(2)
                dve.wait_ge(cmp_out, got(cmp_out))
                o6 = ps[0:N_CMP, 6, 0:P].rearrange("p (g d) -> p g d", g=2)
                if name == "k":
                    step(dve.tensor_copy(kc_n, o6))
                    head_norm(kc_n, kc_n, 2, kcg, N_CMP, kc_t.rearrange("p g d -> p (g d)"))
                    rope(kc_n, 2, 8, cosc[0:N_CMP, :], sinc[0:N_CMP, :], crope, N_CMP)
                    beat().then_inc(kc_normed, 1)
                    dve.wait_ge(kc_normed, sent(kc_normed))
                    dve.wait_ge(kc_sb, got(kc_sb))
                    beat().then_inc(cmp_free, 1)
                    dve.wait_ge(cmp_free, sent(cmp_free))
                else:
                    step(dve.tensor_copy(vcr, o6))
            beat().then_inc(gain_free, 1)
            dve.wait_ge(gain_free, sent(gain_free))
            beat().then_inc(x_ready, 1)
            dve.wait_ge(x_ready, sent(x_ready))
            norm(False)
            linear("nsa_in", into_rows(NSA_DIM))
            z = zrows(NSA_DIM)
            dve.tensor_tensor(z[:, :, D:NSA_DIM], z[:, :, D:NSA_DIM], bgate.unsqueeze(1).to_broadcast([P, TB, 3 * HEADS2]), ALU.add).then_inc(bgate_added, 1)
            dve.wait_ge(bgate_added, sent(bgate_added))
            for b in range(TB):
                x = z[:, b, 0:D].rearrange("p (h d) -> p h d", h=HEADS2)
                head_norm(x, x, HEADS2, nqg, sq=nq_sq)
                rope(x, HEADS2, 8, cos2[:, b, :], sin2[:, b, :], nrope)
            beat().then_inc(heads_ready, 1)
            dve.wait_ge(heads_ready, sent(heads_ready))
            dve.wait_ge(gates_sig, got(gates_sig))

            def take_gated(b, hb, kind):
                def take(o, r):
                    g0 = D + kind * HEADS2 + 4 * hb
                    tt(r, r, z[:, b, g0:g0 + 4], ALU.mult)
                    dst = mix[:, b, 256 * hb:256 * hb + 256].rearrange("p (h d) -> p h d", h=4)
                    rb = r.unsqueeze(2).to_broadcast([P, 4, HD])
                    if kind == 0:
                        dve.tensor_tensor(dst, o, rb, ALU.mult).then_inc(att_taken, 1)
                        dve.wait_ge(att_taken, sent(att_taken))
                    else:
                        t = nsa_tmp.rearrange("p (h d) -> p h d", h=4)
                        dve.tensor_tensor(t, o, rb, ALU.mult).then_inc(att_taken, 1)
                        dve.wait_ge(att_taken, sent(att_taken))
                        tt(dst, dst, t, ALU.add)
                return take

            for hb in range(4):
                parts = []
                for b in range(TB):
                    parts.append((4, N_CMP, const[:, C_CNEG + 16 * b:C_CNEG + 16 * b + N_CMP], take_gated(b, hb, 0),
                                  const[:, C_CM01 + 16 * b:C_CM01 + 16 * b + N_CMP]))
                    for kind in (1, 2):
                        parts.append((4, (b + 1) * P, const[:, C_NEG + AT[b]:C_NEG + AT[b] + (b + 1) * P],
                                      take_gated(b, hb, kind), None))
                attend(nsa_bufs, parts)
            beat().then_inc(rows_ready, 1)
            dve.wait_ge(rows_ready, sent(rows_ready))
            beat().then_inc(conv_free, 1)
            dve.wait_ge(conv_free, sent(conv_free))
            beat().then_inc(gain_free, 1)
            dve.wait_ge(gain_free, sent(gain_free))
            to_columns()
            linear("nsa_out", into_residual(False))
            conv_layer()
            beat().then_inc(result, 1)
            dve.wait_ge(result, sent(result))


_INS = ["x", "c", "positions", "w_ada", "b_ada", "g_norm_mix", "g_norm_ffn", "w_in", "w_out", "hgrn_lb_logits",
        "hgrn_out_norm", "gmlp_vnorm_g", "gmlp_vnorm_b", "gmlp_w_s", "gmlp_b_s", "ffn_w_gate", "ffn_w_up",
        "ffn_w_down", "moe_w_router", "moe_w_gate", "moe_w_up", "moe_w_down", "g_final", "positions_2", "a_norm_2",
        "a_w_in_2", "a_b_f_2", "a_q_gain_2", "a_k_gain_2", "a_w_out_2", "kv_norm_2", "kv_w_2", "kc_pe_2", "vc_pe_2",
        "kc_w1_2", "kc_w2_2", "vc_w1_2", "vc_w2_2", "kc_gain_2", "ks_gain_2", "kw_gain_2", "b_norm_2", "b_w_in_2",
        "b_b_gate_2", "b_q_gain_2", "b_w_out_2", "f_norm_2", "f_w_up_2", "f_conv_w_2", "f_conv_b_2", "f_w_down_2"]


def kernel(**inputs):
    import concourse.bacc as _bacc
    from concourse.bass_utils import run_bass_kernel_spmd as _run

    nc = _bacc.Bacc("TRN2", target_bir_lowering=False, num_devices=1)
    arrays, args = {}, {}
    for name in _INS:
        v = np.ascontiguousarray(inputs[name])
        arrays[f"in_{name}"] = v
        args[name] = nc.dram_tensor(f"in_{name}", v.shape, mybir.dt.from_np(v.dtype), kind="ExternalInput").ap()
    arrays["shape_constants"] = constants()
    consts = nc.dram_tensor("shape_constants", (P, C_END), F32, kind="ExternalInput").ap()
    out = nc.dram_tensor("out", (1, T, D), F32, kind="ExternalOutput").ap()
    build(nc, args, consts, out)
    r = _run(nc, [arrays], core_ids=[0])
    return r.results[0]["out"]
```
